# Optimizing a Trainium2 kernel written in Bass

```python
import math
import jax, jax.numpy as jnp
from jax import lax
import numpy as np

D_MODEL = 1024
BATCH = 1
SEQ = 256
DEPTH = 1
DEC_BATCH = 8
DEC_SEQ = 1
PAST_LEN = 2048
PAGE_SIZE = 128

N_Q_HEADS = 8
N_KV_HEADS = 2
HEAD_DIM = 64
GQA_GROUP = N_Q_HEADS // N_KV_HEADS
WINDOW = 128
ATTN_BLOCK = 128
ATTN_SCALE = HEAD_DIM ** -0.5
NUM_BUCKETS = 32
MAX_DISTANCE = 128
Q_WIDTH = N_Q_HEADS * HEAD_DIM
KV_WIDTH = N_KV_HEADS * HEAD_DIM
RW_HEADS = 8
RW_HEAD = 64
RW_WIDTH = RW_HEADS * RW_HEAD
DECAY_LORA = 64
AAA_LORA = 64
GATE_LORA = 128
RW_COLS = 3 * RW_WIDTH + DECAY_LORA + AAA_LORA + GATE_LORA
RW_SPLITS = (RW_WIDTH, 2 * RW_WIDTH, 3 * RW_WIDTH, 3 * RW_WIDTH + DECAY_LORA,
             3 * RW_WIDTH + DECAY_LORA + AAA_LORA)
IN_COLS = Q_WIDTH + 2 * KV_WIDTH + RW_COLS + 2 * D_MODEL
IN_SPLITS = (Q_WIDTH, Q_WIDTH + KV_WIDTH, Q_WIDTH + 2 * KV_WIDTH,
             Q_WIDTH + 2 * KV_WIDTH + RW_COLS, Q_WIDTH + 2 * KV_WIDTH + RW_COLS + D_MODEL)
N_EXPERTS = 32
TOP_K = 4
D_EXPERT = 1024
SWIGLU_LIMIT = 7.0
SWIGLU_ALPHA = 1.702
MOE_BLOCK = 128
NORM_EPS = 1e-5
QK_EPS = 1e-6
GN_EPS = 64e-5

kernel_name = 'hybrid_swa_rwkv7_moe_step'

def rms_norm(x, g, eps):
    xf = x.astype(jnp.float32)
    y = xf * lax.rsqrt(jnp.mean(xf * xf, axis=-1, keepdims=True) + eps)
    return (y * g.astype(jnp.float32)).astype(x.dtype)

def t5_bucket(dist):
    max_exact = NUM_BUCKETS // 2
    d = jnp.maximum(dist, 0)
    large = max_exact + (jnp.log(jnp.maximum(d, 1).astype(jnp.float32) / max_exact)
                         / math.log(MAX_DISTANCE / max_exact)
                         * (NUM_BUCKETS - max_exact)).astype(jnp.int32)
    large = jnp.minimum(large, NUM_BUCKETS - 1)
    return jnp.where(d < max_exact, d, large)

def rel_bias(dist, t5_table):
    b = t5_table.astype(jnp.float32)[t5_bucket(dist)]
    return jnp.transpose(b, (2, 0, 1)).reshape(N_KV_HEADS, GQA_GROUP, *dist.shape)

def sink_softmax(s, valid, sinks):
    s = jnp.where(valid, s, -jnp.inf)
    sink = jnp.broadcast_to(sinks.astype(jnp.float32).reshape(N_KV_HEADS, GQA_GROUP, 1, 1),
                            s.shape[:-1] + (1,))
    p = jax.nn.softmax(jnp.concatenate([s, sink], axis=-1), axis=-1)
    return p[..., :-1]

def swa_prompt(q, k, v, sinks, t5_table):
    B, T = q.shape[:2]
    nb = T // ATTN_BLOCK
    qb = q.reshape(B, nb, ATTN_BLOCK, N_KV_HEADS, GQA_GROUP, HEAD_DIM)

    def band(t):
        tp = jnp.pad(t, ((0, 0), (ATTN_BLOCK, 0), (0, 0), (0, 0)))
        tp = tp.reshape(B, nb + 1, ATTN_BLOCK, N_KV_HEADS, HEAD_DIM)
        return jnp.concatenate([tp[:, :-1], tp[:, 1:]], axis=2)

    kb, vb = band(k), band(v)
    s = jnp.einsum('bnqkgd,bnjkd->bnkgqj', qb, kb).astype(jnp.float32) * ATTN_SCALE
    qi = jnp.arange(ATTN_BLOCK)[:, None]
    kj = jnp.arange(2 * ATTN_BLOCK)[None, :]
    dist = qi + ATTN_BLOCK - kj
    s = s + rel_bias(dist, t5_table)
    key_pos = (jnp.arange(nb) * ATTN_BLOCK - ATTN_BLOCK)[:, None, None] + kj[None]
    valid = ((dist >= 0) & (dist <= WINDOW))[None] & (key_pos >= 0)
    p = sink_softmax(s, valid[None, :, None, None], sinks).astype(v.dtype)
    o = jnp.einsum('bnkgqj,bnjkd->bnqkgd', p, vb)
    return o.reshape(B, T, Q_WIDTH)

def swa_sample(q, k, v, cache_k, cache_v, sinks, t5_table):
    B, S = q.shape[:2]
    kf = jnp.concatenate([cache_k.astype(k.dtype), k], axis=1)
    vf = jnp.concatenate([cache_v.astype(v.dtype), v], axis=1)
    s = jnp.einsum('bqkgd,bjkd->bkgqj', q, kf).astype(jnp.float32) * ATTN_SCALE
    dist = (WINDOW + jnp.arange(S))[:, None] - jnp.arange(WINDOW + S)[None, :]
    s = s + rel_bias(dist, t5_table)
    valid = (dist >= 0) & (dist <= WINDOW)
    p = sink_softmax(s, valid, sinks).astype(v.dtype)
    o = jnp.einsum('bkgqj,bjkd->bqkgd', p, vf)
    return o.reshape(B, S, Q_WIDTH), kf[:, -WINDOW:], vf[:, -WINDOW:]

def rwkv7_step(S, inp):
    r_t, w_t, k_t, v_t, kk_t, a_t = inp
    sa = jnp.einsum('bhvk,bhk->bhv', S, -kk_t)
    S = (S * w_t[:, :, None, :] + sa[..., None] * (kk_t * a_t)[:, :, None, :]
         + v_t[..., None] * k_t[:, :, None, :])
    return S, jnp.einsum('bhvk,bhk->bhv', S, r_t)

def rwkv7_mix(p_rw, prev_row, wkv0, mu, w0, w_w2, a0, w_a2, w_g2, k_k, k_a, r_k, gn_w, gn_b):
    B, T, _ = p_rw.shape
    prev = jnp.concatenate([prev_row[:, None, :].astype(p_rw.dtype), p_rw[:, :-1]], axis=1)
    xm = p_rw + (prev - p_rw) * mu
    r, k, v, wl, al, gl = jnp.split(xm, RW_SPLITS, axis=-1)
    w_log = -jax.nn.softplus(-(w0 + jnp.tanh(wl) @ w_w2).astype(jnp.float32)) - 0.5
    decay = jnp.exp(-jnp.exp(w_log))
    a = jax.nn.sigmoid((a0 + al @ w_a2).astype(jnp.float32))
    g = (jax.nn.sigmoid(gl) @ w_g2).astype(jnp.float32)

    def heads(t):
        return t.astype(jnp.float32).reshape(B, T, RW_HEADS, RW_HEAD)

    kk = heads(k * k_k)
    kk = kk / jnp.maximum(jnp.sqrt(jnp.sum(kk * kk, axis=-1, keepdims=True)), 1e-12)
    k_mod = k.astype(jnp.float32) * (1.0 + (a - 1.0) * k_a.astype(jnp.float32))
    r_h, w_h, k_h, v_h, a_h = heads(r), heads(decay), heads(k_mod), heads(v), heads(a)
    xs = tuple(jnp.swapaxes(t, 0, 1) for t in (r_h, w_h, k_h, v_h, kk, a_h))
    S_T, o = lax.scan(rwkv7_step, wkv0.astype(jnp.float32), xs)
    o = jnp.swapaxes(o, 0, 1)
    mean = jnp.mean(o, axis=-1, keepdims=True)
    var = jnp.mean(jnp.square(o - mean), axis=-1, keepdims=True)
    o = ((o - mean) * lax.rsqrt(var + GN_EPS)).reshape(B, T, RW_WIDTH)
    o = o * gn_w.astype(jnp.float32) + gn_b.astype(jnp.float32)
    bonus = jnp.sum(r_h * k_h * r_k.astype(jnp.float32), axis=-1, keepdims=True) * v_h
    o = (o + bonus.reshape(B, T, RW_WIDTH)) * g
    return o.astype(p_rw.dtype), S_T

def moe_ffn(h, w_router, b_router, w1, b1, w2, b2):
    T, D = h.shape
    logits = (h @ w_router + b_router).astype(jnp.float32)
    top_v, top_i = lax.top_k(logits, TOP_K)
    gates = jax.nn.softmax(top_v, axis=-1)
    n_assign = T * TOP_K
    flat_e = top_i.reshape(-1)
    flat_tok = jnp.arange(n_assign, dtype=jnp.int32) // TOP_K
    flat_g = gates.reshape(-1)
    order = jnp.argsort(flat_e)
    se = flat_e[order]
    counts = jnp.bincount(flat_e, length=N_EXPERTS)
    padded = (counts + MOE_BLOCK - 1) // MOE_BLOCK * MOE_BLOCK
    end_pad = jnp.cumsum(padded)
    start_pad = end_pad - padded
    start = jnp.cumsum(counts) - counts
    dest = start_pad[se] + jnp.arange(n_assign) - start[se]
    n_blocks = -(-n_assign // MOE_BLOCK) + N_EXPERTS
    n_rows = n_blocks * MOE_BLOCK
    row_tok = jnp.zeros((n_rows,), jnp.int32).at[dest].set(flat_tok[order])
    row_gate = jnp.zeros((n_rows,), jnp.float32).at[dest].set(flat_g[order])
    blk_e = jnp.minimum(jnp.searchsorted(end_pad, jnp.arange(n_blocks) * MOE_BLOCK, side='right'),
                        N_EXPERTS - 1)
    xb = h[row_tok].reshape(n_blocks, MOE_BLOCK, D)

    def expert_block(args):
        xe, e = args
        u = xe @ w1[e] + b1[e]
        u_glu = jnp.minimum(u[:, :D_EXPERT], SWIGLU_LIMIT)
        u_lin = jnp.clip(u[:, D_EXPERT:], -SWIGLU_LIMIT, SWIGLU_LIMIT)
        act = u_glu * jax.nn.sigmoid(SWIGLU_ALPHA * u_glu) * (u_lin + 1.0)
        return act @ w2[e] + b2[e]

    yb = lax.map(expert_block, (xb, blk_e))
    y = yb.reshape(n_rows, D) * row_gate[:, None].astype(h.dtype)
    return jax.ops.segment_sum(y, row_tok, num_segments=T)

def layer_forward(x, c, attn_cache, rw_prev, rw_wkv, t5_table, lw):
    B, T, D = x.shape
    mod = (jax.nn.silu(c) @ lw['w_mod'] + lw['b_mod'])[:, None, :]
    sh1, sc1, gt1, sh2, sc2, gt2 = jnp.split(mod, 6, axis=-1)
    h = rms_norm(x, lw['norm1'], NORM_EPS) * (1.0 + sc1) + sh1
    p = h @ lw['w_in']
    q, k, v, p_rw, g_a, g_b = jnp.split(p, IN_SPLITS, axis=-1)
    q = rms_norm(q.reshape(B, T, N_KV_HEADS, GQA_GROUP, HEAD_DIM), lw['q_norm'], QK_EPS)
    k = rms_norm(k.reshape(B, T, N_KV_HEADS, HEAD_DIM), lw['k_norm'], QK_EPS)
    v = v.reshape(B, T, N_KV_HEADS, HEAD_DIM)
    if attn_cache is None:
        o_a = swa_prompt(q, k, v, lw['sinks'], t5_table)
        new_k, new_v = k[:, -WINDOW:], v[:, -WINDOW:]
    else:
        o_a, new_k, new_v = swa_sample(q, k, v, attn_cache[0], attn_cache[1], lw['sinks'], t5_table)
    o_b, new_wkv = rwkv7_mix(p_rw, rw_prev, rw_wkv, *lw['rw'])
    new_shift = p_rw[:, -1]
    m = jax.nn.sigmoid(g_a) * (o_a @ lw['w_pa']) + jax.nn.sigmoid(g_b) * (o_b @ lw['w_pb'])
    x = x + gt1 * (m @ lw['w_o'])
    h2 = rms_norm(x, lw['norm2'], NORM_EPS) * (1.0 + sc2) + sh2
    y = moe_ffn(h2.reshape(B * T, D), *lw['moe']).reshape(B, T, D)
    x = x + gt2 * y
    return x, new_k, new_v, new_shift, new_wkv

def setup_inputs(seed: int = 0) -> dict:
    key = jax.random.key(seed)
    ks = iter(jax.random.split(key, 48))
    f = jnp.float32
    L, D, E, F = DEPTH, D_MODEL, N_EXPERTS, D_EXPERT

    def nrm(shape, scale):
        return jax.random.normal(next(ks), shape, f) * scale

    def gain(shape):
        return 1.0 + nrm(shape, 0.02)

    return {
        'x_prompt': nrm((BATCH, SEQ, D), 1.0),
        'x_sample': nrm((DEC_BATCH, DEC_SEQ, D), 1.0),
        'cache_k': nrm((L, DEC_BATCH, WINDOW, N_KV_HEADS, HEAD_DIM), 1.0),
        'cache_v': nrm((L, DEC_BATCH, WINDOW, N_KV_HEADS, HEAD_DIM), 1.0),
        'state_shift': nrm((L, DEC_BATCH, RW_COLS), 1.0),
        'state_wkv': nrm((L, DEC_BATCH, RW_HEADS, RW_HEAD, RW_HEAD), 0.5),
        'c_prompt': nrm((BATCH, D), 1.0),
        'c_sample': nrm((DEC_BATCH, D), 1.0),
        't5_table': nrm((NUM_BUCKETS, N_Q_HEADS), 0.5),
        'w_mod': nrm((L, D, 6 * D), 0.5 * D ** -0.5),
        'b_mod': nrm((L, 6 * D), 0.02),
        'norm1': gain((L, D)),
        'w_in': nrm((L, D, IN_COLS), D ** -0.5),
        'q_norm': gain((L, HEAD_DIM)),
        'k_norm': gain((L, HEAD_DIM)),
        'sinks': nrm((L, N_Q_HEADS), 0.5),
        'rw_mu': jax.random.uniform(next(ks), (L, RW_COLS), f),
        'rw_w0': nrm((L, RW_WIDTH), 0.5) - 0.5,
        'rw_w_w2': nrm((L, DECAY_LORA, RW_WIDTH), 0.1),
        'rw_a0': nrm((L, RW_WIDTH), 0.1),
        'rw_w_a2': nrm((L, AAA_LORA, RW_WIDTH), AAA_LORA ** -0.5),
        'rw_w_g2': nrm((L, GATE_LORA, RW_WIDTH), GATE_LORA ** -0.5),
        'rw_k_k': 0.85 + nrm((L, RW_WIDTH), 0.05),
        'rw_k_a': gain((L, RW_WIDTH)),
        'rw_r_k': nrm((L, RW_HEADS, RW_HEAD), 0.1),
        'rw_gn_w': gain((L, RW_WIDTH)),
        'rw_gn_b': nrm((L, RW_WIDTH), 0.02),
        'w_pa': nrm((L, Q_WIDTH, D), Q_WIDTH ** -0.5),
        'w_pb': nrm((L, RW_WIDTH, D), RW_WIDTH ** -0.5),
        'w_o': nrm((L, D, D), D ** -0.5),
        'norm2': gain((L, D)),
        'w_router': nrm((L, D, E), D ** -0.5),
        'b_router': nrm((L, E), 0.01),
        'w1': nrm((L, E, D, 2 * F), D ** -0.5),
        'b1': nrm((L, E, 2 * F), 0.01),
        'w2': nrm((L, E, F, D), F ** -0.5),
        'b2': nrm((L, E, D), 0.01),
    }

def reference(x_prompt, x_sample, cache_k, cache_v, state_shift, state_wkv, c_prompt, c_sample,
              t5_table, w_mod, b_mod, norm1, w_in, q_norm, k_norm, sinks,
              rw_mu, rw_w0, rw_w_w2, rw_a0, rw_w_a2, rw_w_g2, rw_k_k, rw_k_a, rw_r_k,
              rw_gn_w, rw_gn_b, w_pa, w_pb, w_o, norm2,
              w_router, b_router, w1, b1, w2, b2):
    xp, xs = x_prompt, x_sample
    bp = x_prompt.shape[0]
    zero_shift = jnp.zeros((bp, RW_COLS), x_prompt.dtype)
    zero_wkv = jnp.zeros((bp, RW_HEADS, RW_HEAD, RW_HEAD), jnp.float32)
    kp_l, vp_l, sp_l, wp_l, ks_l, vs_l, ss_l, ws_l = ([] for _ in range(8))
    for l in range(DEPTH):
        lw = dict(
            w_mod=w_mod[l], b_mod=b_mod[l], norm1=norm1[l], w_in=w_in[l],
            q_norm=q_norm[l], k_norm=k_norm[l], sinks=sinks[l],
            rw=(rw_mu[l], rw_w0[l], rw_w_w2[l], rw_a0[l], rw_w_a2[l], rw_w_g2[l],
                rw_k_k[l], rw_k_a[l], rw_r_k[l], rw_gn_w[l], rw_gn_b[l]),
            w_pa=w_pa[l], w_pb=w_pb[l], w_o=w_o[l], norm2=norm2[l],
            moe=(w_router[l], b_router[l], w1[l], b1[l], w2[l], b2[l]),
        )
        xp, kp, vp, sp, wp = layer_forward(xp, c_prompt, None, zero_shift, zero_wkv, t5_table, lw)
        xs, ks_, vs_, ss, ws = layer_forward(xs, c_sample, (cache_k[l], cache_v[l]),
                                             state_shift[l], state_wkv[l], t5_table, lw)
        kp_l.append(kp); vp_l.append(vp); sp_l.append(sp); wp_l.append(wp)
        ks_l.append(ks_); vs_l.append(vs_); ss_l.append(ss); ws_l.append(ws)
    k_prompt = jnp.stack(kp_l)
    v_prompt = jnp.stack(vp_l)
    shift_prompt = jnp.stack(sp_l)
    wkv_prompt = jnp.stack(wp_l)
    k_sample = jnp.stack(ks_l)
    v_sample = jnp.stack(vs_l)
    shift_sample = jnp.stack(ss_l)
    wkv_sample = jnp.stack(ws_l)
    return (xp, xs, k_prompt, v_prompt, shift_prompt, wkv_prompt,
            k_sample, v_sample, shift_sample, wkv_sample)


_drawn_inputs = setup_inputs


def setup_inputs(seed=0):
    import zlib

    import numpy as np

    out = dict(_drawn_inputs(seed))
    spreads = {}
    factors = {'q_norm': 8.0,
     'k_norm': 2.946,
     'sinks': 64.0,
     'rw_k_k': 3.217,
     'rw_gn_w': 8.0,
     'rw_gn_b': 8.0,
     'norm2': 3.856,
     'b_router': 10.31,
     'b1': 8.0,
     'b2': 64.0}
    for name, (base, spread) in spreads.items():
        noise = np.random.default_rng([zlib.crc32(name.encode()), seed]).standard_normal(out[name].shape)
        drawn = base * np.exp(spread * noise) if base else spread * noise
        out[name] = __import__('jax').numpy.asarray(drawn.astype(out[name].dtype))
    for name, factor in factors.items():
        out[name] = (out[name] * factor).astype(out[name].dtype)
    return out
```

```python
from contextlib import ExitStack

import numpy as np
import concourse.bass as bass
from concourse import mybir
from concourse.alu_op_type import AluOpType as ALU

F32 = mybir.dt.float32
I32 = mybir.dt.int32
U32 = mybir.dt.uint32
ACT = mybir.ActivationFunctionType
AX = mybir.AxisListType

P = 128
D = 1024
KD = D // P
NP, NS = 256, 8
T = NP + NS
TILES = [(0, 128), (128, 128), (256, NS)]
HQ, HKV, HD, GQA = 8, 2, 64, 4
WINDOW = 128
KEYS = WINDOW + 1
RW = 1792
NCH = 20
CQ, CK, CV, CR = 0, 4, 5, 6
NE, FE, C = 32, 1024, 64
NF = FE // P
MAXR = -(-T // C)
CH = 64
NCHUNK = NP // CH
RING_PRE = 2
SCALE = HD ** -0.5
E_HALF = float(np.exp(-0.5))
NEG = -1e30
LEVELS = [1, 2, 4, 8, 16, 32]

K_ID, K_II, K_BO, K_ONE, K_US, K_REV, K_M2, K_LV, K_IO, K_IE, K_OB = (
    0, 128, 256, 384, 512, 640, 768, 896, 1280, 1408, 1440)
K_COLS = K_OB + KEYS + 1

PARAMS = [("b_mod", 48), ("norm1", 8), ("norm2", 8), ("rw_mu", 14), ("rw_w0", 4), ("rw_a0", 4),
          ("rw_k_k", 4), ("rw_k_a", 4), ("rw_r_k", 4), ("rw_gn_w", 4), ("rw_gn_b", 4),
          ("q_norm", 1), ("k_norm", 1)]
PCOL, _n = {}, 0
for _name, _rows in PARAMS:
    PCOL[_name] = _n
    _n += _rows
NPAR = _n


def constants():
    c = np.zeros((P, K_COLS), np.float32)
    p = np.arange(P)[:, None]
    m = np.arange(P)[None, :]
    c[:, K_ID:K_ID + P] = p == m
    c[:, K_II:K_II + P] = p % 64 == m % 64
    c[:, K_BO:K_BO + P] = p // 64 == m // 64
    c[:, K_ONE:K_ONE + P] = 1.0
    c[:, K_US:K_US + P] = p < m
    c[:, K_REV:K_REV + P] = p + m == P - 1
    s, t = p % 64, np.arange(64)[None, :]
    c[:, K_M2:K_M2 + 64] = t > s
    c[:, K_M2 + 64:K_M2 + 128] = t >= s
    for i, b in enumerate(LEVELS):
        c[:, K_LV + 64 * i:K_LV + 64 * i + 64] = (t // b % 2 == 1) & (s // b == t // b - 1)
    c[:, K_IO:K_IO + 2 * C] = np.arange(2 * C) % C
    c[:, K_IE:K_IE + NE] = np.arange(NE)
    dist = WINDOW - np.arange(KEYS)
    half = NE // 2
    far = half + (np.log(np.maximum(dist, 1).astype(np.float32) / half) / np.log(128 / half) * half).astype(np.int32)
    bucket = np.where(dist < half, dist, np.minimum(far, NE - 1))
    c[:NE, K_OB:K_OB + KEYS] = np.arange(NE)[:, None] == bucket[None, :]
    return c


class Sems(dict):

    def __init__(self, nc, ctx):
        super().__init__()
        self.nc, self.ctx = nc, ctx

    def __missing__(self, name):
        self[name] = self.ctx.enter_context(self.nc.semaphore(name))
        return self[name]


class Chain:

    def __init__(self, engine, sem):
        self.engine, self.sem, self.count, self.base = engine, sem, 0, 0

    def __call__(self, instruction):
        self.count += 1
        instruction.then_inc(self.sem, 1)
        self.engine.wait_ge(self.sem, self.base + self.count)


def build(nc, io):
    with ExitStack() as ctx:
        sem = Sems(nc, ctx)

        def sb(name, shape, dt=F32):
            return ctx.enter_context(nc.sbuf_tensor(name, shape, dt))

        ring = sb("ring", [P, 6, 8, 512])
        RZ = ring[:, RING_PRE:6, :, :].rearrange("p a b c -> p (a b c)")
        cst = sb("cst", [P, K_COLS])
        PT = sb("PT", [P, NCH * T])
        XM = sb("XM", [P, 14 * T])
        SG = sb("SG", [P, 16 * T])
        XT = sb("XT", [P, KD, T])
        HT = sb("HT", [P, KD, T])
        SQ = sb("SQ", [P, KD, T])
        XR = sb("XR", [P, 3, D])
        BM = sb("BM", [P, HQ * 2 * P])
        modT = sb("modT", [P, 48, 9])
        PC = sb("PC", [P, NPAR])
        b1T = sb("b1T", [P, NE * 16])
        cT = sb("cT", [P, KD, 9])
        A1 = sb("A1", [P, KD, 9])
        RS = sb("RS", [P, T])
        SS = sb("SS", [P, 14, NS])
        SMP = sb("SMP", [P, 6, 4, NS])
        brow = sb("brow", [HQ, KEYS + 1])
        sinkb = sb("sinkb", [P, HQ])
        sinkc = sb("sinkc", [HQ, 1])
        tab = sb("tab", [NE, HQ])
        st = sb("st", [P, 96])
        pcol = sb("pcol", [P, 4, NCHUNK])

        def view(t, off, *shape):
            n = int(np.prod(shape))
            v = t[:, off:off + n]
            if len(shape) == 2:
                return v.rearrange("p (a b) -> p a b", b=shape[1])
            if len(shape) == 3:
                return v.rearrange("p (a b c) -> p a b c", b=shape[1], c=shape[2])
            if len(shape) == 4:
                return v.rearrange("p (a b c d) -> p a b c d", b=shape[1], c=shape[2], d=shape[3])
            return v

        SQf = SQ[:, :, :].rearrange("p a b -> p (a b)")
        XRf = XR[:, :, :].rearrange("p a b -> p (a b)")
        PTv = PT[:, :].rearrange("p (a b) -> p a b", b=T)
        XMv = XM[:, :].rearrange("p (a b) -> p a b", b=T)
        SGv = SG[:, :].rearrange("p (a b) -> p a b", b=T)
        LD, CS, eP, eN, eM = (view(RZ, 0, 4, T), view(RZ, 1056, 4, NP), view(RZ, 2080, 4, NP),
                              view(RZ, 3104, 4, NP), view(RZ, 4128, 4, NP))
        NK, Aa, TM = view(RZ, 5152, 4, T), view(RZ, 6208, 4, T), view(RZ, 7264, 4, T)
        Bh, Kh = view(RZ, 8320, 4, NP), view(RZ, 9344, 4, NP)
        vcr, SsT, kd, vr = (view(RZ, 10368, NS, P), view(RZ, 11392, NS, KEYS), view(RZ, 12424, 2, T),
                            view(RZ, 12952, 3, P))
        LWw, LWg = view(RZ, 13336, 512), view(RZ, 13848, 512)
        ssr = view(RZ, 14360, RW)
        GG, ZR = view(PT, 6 * T, 4, T), view(PT, 10 * T, 4, NCHUNK, 2, CH)
        BON = SQ[:, 0:4, :]
        NR, KR = view(RZ, 0, 16, P), view(RZ, 2048, 16, P)
        ZU, Br, Kr = view(RZ, 4096, 16, P), view(RZ, 6144, 16, CH), view(RZ, 7168, 16, CH)
        Vr = view(SQf, 1056, 16, CH)
        X, XX = view(XM, 0, 16, CH), view(XM, 1024, 16, CH)
        Y = view(RZ, 8320, 16, CH)
        NM = [view(RZ, 9344, 16, CH), view(RZ, 13336, 16, CH)]
        XZW = view(RZ, 8320, 16, P)
        MC, G4 = view(RZ, 4096, 4, NCHUNK, CH), view(RZ, 5120, NCHUNK, 4, CH)
        N0 = view(XM, 0, 4, NCHUNK, CH)
        OT = view(XM, 1024, 4, T)
        TMn, OSQ = SQ[:, 4:8, :], view(XM, 2112, 4, T)
        Pm, pT = view(SG, 0, 4, 2 * P), view(SG, 1024, 4, 2, P)
        kcT, kcr = view(SG, 2048, NS, KEYS), view(SG, 3080, NS, P)
        OA = view(PT, 0, 4, T)
        HK = view(SG, 0, HQ, 2 * P)
        prow, b1r, ext = view(SG, 2048, P), view(SG, 2176, 4, P), view(SG, 2688, 384)
        crow, csig = view(BM, 0, D), view(BM, 1024, D)
        S0, T1, EX = view(XRf, 0, 32, CH), view(RZ, 0, 32, CH), view(RZ, 2048, 32, CH)
        OH, OG = view(PT, 0, 3, C), view(PT, 192, 3, 2 * C)
        POSM, GATE = view(PT, 576, 3, NE * MAXR + 1), view(PT, 1059, 3, NE * MAXR + 1)
        XG, GT = view(PT, 1542, 4, 2, C), view(PT, 2054, 2, T)
        UG, UL, US_, AC = (view(PT, 2582, 4, C), view(PT, 2838, 4, C), view(PT, 3094, 4, C),
                           view(PT, 3350, NF, C))
        YS, XGR, UR = view(PT, 3862, 512), view(PT, 4374, 512), view(SG, 0, 2, 512)
        XGf = view(PT, 1542, 512)
        YA = SQ
        LG, MSK, GTE, TMP32 = (view(XM, 0, 3, NE), view(XM, 96, 3, NE), view(XM, 192, 3, NE), view(XM, 288, NE))
        gT, b2r = view(XM, 1408, T), view(XM, 2112, D)
        wr, brt = view(XM, 3168, KD, NE), view(XM, 3424, NE)
        fin = view(RZ, 0, 3, D)
        mx8, ix8, ixf = sb("mx8", [P, 3, 8]), sb("ix8", [P, 3, 8], U32), sb("ixf", [P, 3, 8])
        rounds_i = sb("rounds_i", [P, 1], I32)
        Qs = sb("Qs", [P, HQ, NS])
        pTs, PSf, OS = sb("pTs", [P, NS, HQ]), sb("PSf", [NS, NS, HQ]), sb("OS", [P, NS, HQ])
        epsc = sb("epsc", [P, 3])
        qk_eps, gn_eps = epsc[:, 0:1], epsc[:, 1:2]
        kvr = view(XRf, 10 * T, 2, P)
        wps = view(XM, 0, 4, CH)

        ps = ctx.enter_context(nc.psum_tensor("ps", [P, 8, 512], F32))
        ID = cst[:, K_ID:K_ID + P]
        II = cst[:, K_II:K_II + P]
        BO = cst[:, K_BO:K_BO + P]
        ONE = cst[:, K_ONE:K_ONE + P]
        ext_d = nc.dram_tensor("bias_by_distance", [HQ, 384], F32, kind="Internal")

        def par(name, i=0):
            return PC[:, PCOL[name] + i:PCOL[name] + i + 1]

        win = io["w_in"].rearrange("(k p) n -> p k n", p=P)
        wmod = io["w_mod"].rearrange("(k p) n -> p k n", p=P)
        wo = io["w_o"].rearrange("(k p) n -> p k n", p=P)
        WIN1, WIN2 = [1, 2, 3, 4, 0], [5, 6, 7, 8]
        stream = [("mod", wmod, j) for j in range(4)] + [("win", win, j) for j in WIN1]
        stream += [("mod", wmod, j) for j in range(4, 12)] + [("win", win, j) for j in WIN2]
        stream += [("pa", None, 0), ("pb", None, 0), ("wo", wo, 0), ("wo", wo, 1)]
        NSTREAM = len(stream)
        STREAM_AT = {(kind, j): g for g, (kind, _, j) in enumerate(stream)}

        def uses_before(slot):
            return len([g for g in range(NSTREAM) if g % RING_PRE == slot]) if slot < RING_PRE else 0

        w1v = io["w1"].rearrange("e (k p) n -> e p k n", p=P)
        w2v = io["w2"].rearrange("e (k p) n -> e p k n", p=P)

        def expert_chunk(e, c):
            if c < 4:
                col = (c // 2) * 512 + (c % 2) * FE
                return w1v[e, :, :, col:col + 512]
            return w2v[e, :, :, (c - 4) * 512:(c - 4) * 512 + 512]

        def slot_used(c, i):
            return (sem["u_done"], 2 * i + 1 + c // 2) if c < 4 else (sem["y2_done"], i + 1)

        A_X, A_WIN1, A_LORA, A_NORM, A_WIN2 = 0, 8, 28, 40, 49
        A_TOTAL = A_WIN2 + 16

        def chunk_used(g):
            kind, _, j = stream[g]
            if kind == "mod":
                return sem["mod_done"], j + 1
            if kind == "win" and j in WIN1:
                return sem["a_done"], A_WIN1 + 4 * (WIN1.index(j) + 1)
            if kind == "win":
                return sem["a_done"], A_WIN2 + 4 * (WIN2.index(j) + 1)
            return sem["pab_done"], 2 * KD

        block = ctx.enter_context(nc.Block())

        @block.sync
        def _(sp):
            sp.dma_start(cst[:, :], io["cst"]).then_inc(sem["ld_cst"], 16)
            sp.dma_start(crow[0:1, :], io["c_prompt"]).then_inc(sem["ld_c"], 16)
            sp.dma_start(crow[1:9, :], io["c_sample"]).then_inc(sem["ld_c"], 16)
            for n, (t0, nt) in enumerate(TILES):
                src = io["x_prompt"][t0:t0 + nt, :] if n < 2 else io["x_sample"]
                sp.dma_start(XR[0:nt, n, :], src).then_inc(sem["ld_x"], 16)
            for name, rows in PARAMS[:-2]:
                at = PCOL[name]
                sp.dma_start(prow[at:at + rows, :], io[name]).then_inc(sem["ld_par"], 16)
            for name in ("q_norm", "k_norm"):
                at = PCOL[name]
                for s in range(2):
                    sp.dma_start(prow[at:at + 1, 64 * s:64 * s + 64], io[name]).then_inc(sem["ld_par"], 16)
            for g, (kind, src, j) in enumerate(stream):
                slot = g % RING_PRE
                if g >= RING_PRE:
                    sp.wait_ge(*chunk_used(g - RING_PRE))
                if kind in ("pa", "pb"):
                    dst = ring[:, slot, :, :].rearrange("p k n -> p (k n)").rearrange("p (k n) -> p k n", n=D)
                    sp.dma_start(dst, io["w_" + kind].rearrange("(k p) n -> p k n", p=P)).then_inc(sem[f"ring{slot}"], 16)
                else:
                    sp.dma_start(ring[:, slot, :, :], src[:, :, j * 512:j * 512 + 512]).then_inc(sem[f"ring{slot}"], 16)
            sp.wait_ge(sem["smp_step"], 5)
            sp.wait_ge(sem["sh_out"], 32)
            sp.wait_ge(sem["st_kv"], 64)
            for c in (2, 3, 4, 5, 0, 1):
                if c < RING_PRE:
                    sp.wait_ge(sem["wo_done"], 8)
                sp.dma_start(ring[:, c, :, :], expert_chunk(0, c)).then_inc(sem[f"ring{c}"], 16)
            with sp.Fori(1, NE) as e:
                for c in range(6):
                    sp.wait_ge(*slot_used(c, e - 1))
                    sp.dma_start(ring[:, c, :, :], expert_chunk(e, c)).then_inc(sem[f"ring{c}"], 16)
            sp.wait_ge(sem["rounds_ready"], 1)
            rounds = sp.value_load(rounds_i[0:1, 0:1], min_val=1, max_val=MAXR)
            with sp.If(rounds > 1):
                with sp.Fori(1, rounds) as r:
                    with sp.Fori(0, NE) as e:
                        for c in range(6):
                            sp.wait_ge(*slot_used(c, r * NE + e - 1))
                            sp.dma_start(ring[:, c, :, :], expert_chunk(e, c)).then_inc(sem[f"ring{c}"], 16)
            for n, (t0, nt) in enumerate(TILES):
                sp.wait_ge(sem["fin_evac"], 2 * n + 2)
                dst = io["y_prompt"][t0:t0 + nt, :] if n < 2 else io["y_sample"]
                sp.dma_start(dst, fin[0:nt, n, :]).then_inc(sem["y_out"], 16)
            sp.wait_ge(sem["y_out"], 48)

        def state_rows(h):
            return S0[64 * (h % 2):64 * (h % 2) + 64, (h // 2) * NS:(h // 2) * NS + NS, :]

        @block.gpsimd
        def _(pool):
            chain = Chain(pool, sem["pool_chain"])
            pool.wait_ge(sem["brow_ready"], 1)
            chain(pool.memset(ext[0:HQ, :], NEG))
            chain(pool.tensor_copy(ext[0:HQ, 127:127 + KEYS], brow[:, 0:KEYS]))
            pool.dma_start(ext_d.ap(), ext[0:HQ, :]).then_inc(sem["ext_out"], 16)
            pool.wait_ge(sem["ext_out"], 16)
            band = bass.AP(ext_d, 0, [[1, P], [384, HQ], [1, 2 * P]])
            pool.dma_start(HK, band).then_inc(sem["ld_hk"], 16)
            pool.wait_ge(sem["sh_evac"], 4)
            pool.dma_start(io["shift_prompt"], ssr[0:1, :]).then_inc(sem["sh_out"], 16)
            pool.dma_start(io["shift_sample"], ssr[1:9, :]).then_inc(sem["sh_out"], 16)
            pool.wait_ge(sem["a_done"], A_NORM)
            pool.dma_start(wr, io["w_router"].rearrange("(k p) e -> p k e", p=P)).then_inc(sem["ld_r"], 16)
            pool.dma_start(brt, io["b_router"].partition_broadcast(P).rearrange("p a b -> p (a b)")).then_inc(sem["ld_r"], 16)
            pool.wait_ge(sem["qk_ready"], 1)
            for h in range(HQ):
                pool.dma_start(state_rows(h), io["state_wkv"][:, h // 2, h % 2].rearrange("b v k -> v b k")).then_inc(sem["ld_s0"], 16)
            pool.wait_ge(sem["kvrow_evac"], 1)
            pool.dma_start(io["k_prompt"], kvr[:, 0, :]).then_inc(sem["st_kv"], 16)
            pool.dma_start(io["v_prompt"], vr[:, 1, :]).then_inc(sem["st_kv"], 16)
            pool.dma_start(io["k_sample"][:, WINDOW - 1, :], kvr[0:NS, 1, :]).then_inc(sem["st_kv"], 16)
            pool.dma_start(io["v_sample"][:, WINDOW - 1, :], vr[0:NS, 2, :]).then_inc(sem["st_kv"], 16)
            for i in range(len(LEVELS)):
                pool.wait_ge(sem["nr_ready"], 2)
                pool.wait_ge(sem["kr_ready"], 2)
                if i >= 2:
                    pool.wait_ge(sem["y_done"], 2 * i - 2)
                    pool.wait_ge(sem["x_ready"], 2)
                mask = cst[:, K_LV + 64 * i:K_LV + 64 * i + 64].unsqueeze(1).broadcast_to([P, 16, CH])
                pool.tensor_tensor(NM[i % 2], NR[:, :, 0:CH], mask, ALU.mult).then_inc(sem["nm_ready"], 1)
            for q in range(5):
                pool.wait_ge(sem["smp_ready"], 1)
                pool.wait_ge(sem["o_done"], 4)
                if q:
                    pool.wait_ge(sem["ex_used"], q)
                pool.tensor_tensor(
                    EX, SMP[:, q, :, :].rearrange("p a b -> p (a b)").unsqueeze(2).broadcast_to([P, 32, CH]),
                    II[:, 0:CH].unsqueeze(1).broadcast_to([P, 32, CH]), ALU.mult).then_inc(sem["ex_ready"], 1)
            pool.wait_ge(sem["smp_step"], 5)
            for h in range(HQ):
                pool.dma_start(io["wkv_sample"][:, h // 2, h % 2].rearrange("b v k -> v b k"), state_rows(h)).then_inc(sem["st_s"], 16)
            pool.wait_ge(sem["gn_done"], 8)
            pool.dma_start(b2r[0:NE, :], io["b2"]).then_inc(sem["ld_r"], 16)
            pool.wait_ge(sem["sh_out"], 32)
            pool.wait_ge(sem["st_s"], 16 * HQ)
            pool.wait_ge(sem["st_kv"], 64)
            pool.memset(XR[:, 2, :], 0.0).then_inc(sem["xr_zero"], 1)

        @block.scalar
        def _(act):
            chain = Chain(act, sem["act_chain"])
            dma = act.dma_start
            dma(tab[:, :], io["t5_table"]).then_inc(sem["ld_tab"], 16)
            dma(b1r, io["b1"].rearrange("(a p) f -> p a f", p=P)).then_inc(sem["ld_b1"], 16)
            dma(ssr[0:NS, :], io["state_shift"]).then_inc(sem["ld_ss"], 16)
            dma(LWw[0:64, :], io["rw_w_w2"]).then_inc(sem["ld_lw"], 16)
            dma(LWw[64:128, :], io["rw_w_a2"]).then_inc(sem["ld_lw"], 16)
            dma(LWg, io["rw_w_g2"]).then_inc(sem["ld_lw"], 16)
            dma(sinkb[:, :], io["sinks"].partition_broadcast(P).rearrange("p a b -> p (a b)")).then_inc(sem["ld_sink"], 16)
            dma(sinkc[:, :], io["sinks"].rearrange("a b -> b a")).then_inc(sem["ld_sink"], 16)
            dma(kcr, io["cache_k"].rearrange("b j n -> j b n")).then_inc(sem["ld_kc"], 16)
            dma(vcr, io["cache_v"].rearrange("b j n -> j b n")).then_inc(sem["ld_vc"], 16)
            dma(io["k_sample"][:, 0:WINDOW - 1, :], io["cache_k"][:, 1:WINDOW, :]).then_inc(sem["st_k"], 16)
            dma(io["v_sample"][:, 0:WINDOW - 1, :], io["cache_v"][:, 1:WINDOW, :]).then_inc(sem["st_k"], 16)

            act.wait_ge(sem["ld_c"], 32)
            act.activation(csig[0:9, :], crow[0:9, :], ACT.Sigmoid).then_inc(sem["csig_ready"], 1)

            a = [0]

            def group():
                g = a[0]
                a[0] += 1
                act.wait_ge(sem["a_done"], g + 1)
                return ps[:, g % 4, 0:T]

            for k in range(KD):
                chain(act.copy(XT[:, k, :], group()))
                act.activation(SQ[:, k, :], XT[:, k, :], ACT.Square).then_inc(sem["a_evac"], 1)
            act.wait_ge(sem["ms_ready"], 1)
            act.activation(RS[:, :], RS[:, :], ACT.Sqrt).then_inc(sem["sqrt_done"], 1)

            def project(chunks):
                for j in chunks:
                    for s in range(4):
                        cc = 4 * j + s
                        if cc < NCH:
                            act.copy(PTv[:, cc, :], group()).then_inc(sem["a_evac"], 1)
                        else:
                            act.activation(SGv[:, cc - NCH, :], group(), ACT.Sigmoid).then_inc(sem["a_evac"], 1)

            project(WIN1)
            act.wait_ge(sem["mixed"], 1)
            act.activation(XMv[0:64, 12, :], XMv[0:64, 12, :], ACT.Tanh).then_inc(sem["lora_in"], 1)
            act.activation(XMv[:, 13, :], XMv[:, 13, :], ACT.Sigmoid).then_inc(sem["lora_in"], 1)
            for hp in range(4):
                act.activation(LD[:, hp, :], group(), ACT.Sigmoid, bias=par("rw_w0", hp)).then_inc(sem["a_evac"], 1)
            for hp in range(4):
                act.activation(Aa[:, hp, :], group(), ACT.Sigmoid, bias=par("rw_a0", hp)).then_inc(sem["a_evac"], 1)
            act.wait_ge(sem["sh_t"], 4)
            for hp in range(4):
                act.copy(GG[:, hp, :], group()).then_inc(sem["a_evac"], 1)
            for hp in range(4):
                act.activation(SQ[:, 4 + hp, :], group(), ACT.Sqrt).then_inc(sem["a_evac"], 1)
            for i in range(5):
                act.activation(XRf[:, (5 + i) * T:(6 + i) * T], group(), ACT.Sqrt,
                               bias=qk_eps, scale=1.0 / HD).then_inc(sem["a_evac"], 1)
            act.wait_ge(sem["cs_ready"], 1)
            act.activation(eP, CS, ACT.Exp).then_inc(sem["decays"], 1)
            act.activation(eN, CS, ACT.Exp, scale=-1.0).then_inc(sem["decays"], 1)
            act.wait_ge(sem["cs_ready"], 2)
            act.activation(eM, eM, ACT.Exp).then_inc(sem["decays"], 1)
            act.activation(SMP[:, 1, :, :], LD[:, :, NP:T], ACT.Exp).then_inc(sem["decays"], 1)

            for m in range(4, 12):
                act.wait_ge(sem["mod_done"], m + 1)
                act.copy(modT[:, 4 * m:4 * m + 4, :],
                         ps[:, 4 + m % 4, 0:36].rearrange("p (a b) -> p a b", b=9)).then_inc(sem["mod_evac"], 1)

            for g4 in range(4):
                J = P if g4 < 2 else 2 * P
                act.wait_ge(sem["att_max"], g4 + 1)
                for g in range(4):
                    act.activation(Pm[:, g, 0:J], Pm[:, g, 0:J], ACT.Exp, bias=st[:, 4 + g:5 + g],
                                   accum_out=st[:, 8 + g:9 + g]).then_inc(sem["att_exp"], 1)
                act.activation(st[:, 12:16], st[:, 12:16], ACT.Exp).then_inc(sem["att_exp"], 1)
                for g in range(4 * J // P // 4):
                    act.wait_ge(sem["att_pt"], (g4 if g4 < 2 else 2 * g4 - 2) + g + 1)
                    act.copy(pT[:, :, g, :], ps[:, 4 + g, :].rearrange("p (a b) -> p a b", b=P)).then_inc(sem["att_pte"], 1)
            act.wait_ge(sem["smp_max"], 1)
            act.activation(SsT[0:HQ, :, :], SsT[0:HQ, :, :], ACT.Exp).then_inc(sem["smp_exp"], 1)
            act.activation(st[0:HQ, 48:56], st[0:HQ, 48:56], ACT.Exp).then_inc(sem["smp_exp"], 1)

            for hp in range(4):
                act.wait_ge(sem["bon_done"], hp + 1)
                act.copy(BON[:, hp, :], ps[:, hp, 0:T]).then_inc(sem["bon_evac"], 1)
            for i in range(8):
                mat, n = i // 2, i % 2
                dst = [ZU[:, 8 * n:8 * n + 8, 0:CH], Br[:, 8 * n:8 * n + 8, :], Kr[:, 8 * n:8 * n + 8, :],
                       Vr[:, 8 * n:8 * n + 8, :]][mat]
                act.wait_ge(sem["row_done"], i + 1)
                act.copy(dst, ps[:, i % 4, :].rearrange("p (a b) -> p a b", b=CH)).then_inc(sem["row_evac"], 1)
            for i in range(1, len(LEVELS)):
                for n in range(2):
                    act.wait_ge(sem["y_done"], 2 * i + n + 1)
                    act.copy(Y[:, 8 * n:8 * n + 8, :], ps[:, 4 * n, :].rearrange("p (a b) -> p a b", b=CH)).then_inc(sem["y_evac"], 1)
            for n in range(2):
                act.wait_ge(sem["u0_done"], n + 1)
                act.copy(ZU[:, 8 * n:8 * n + 8, CH:P], ps[:, 3 + 4 * n, :].rearrange("p (a b) -> p a b", b=CH)).then_inc(sem["u0_evac"], 1)
            for n in range(2):
                act.wait_ge(sem["xzw_done"], n + 1)
                act.copy(XZW[:, 8 * n:8 * n + 8, :],
                         ps[:, 4 * n:4 * n + 2, :].rearrange("p a b -> p (a b)").rearrange("p (a b) -> p a b", b=P)).then_inc(sem["xzw_evac"], 1)
            act.wait_ge(sem["carry_done"], 3)
            for q in range(2):
                act.copy(N0[:, :, q::2, :], ps[:, 2 + q, :].rearrange("p (h c k) -> p h c k", c=2, k=CH)).then_inc(sem["n0_evac"], 1)
            act.wait_ge(sem["wps_done"], 1)
            act.wait_ge(sem["g_ready"], NCHUNK)
            act.copy(wps, ps[:, 2, 0:4 * CH].rearrange("p (a b) -> p a b", b=CH)).then_inc(sem["wps_evac"], 1)
            act.wait_ge(sem["wps_evac"], 1)
            for s in range(2):
                dma(io["wkv_prompt"].rearrange("(hp s) v k -> s v hp k", s=2)[s],
                    wps[64 * s:64 * s + 64, :, :]).then_inc(sem["st_w"], 16)

            project(WIN2)
            for hp in range(4):
                act.wait_ge(sem["gn_done"], hp + 1)
                act.mul(TMn[:, hp, :], ps[:, 4 + hp, 0:T], 1.0 / CH).then_inc(sem["gn_evac"], 1)
            for hp in range(4):
                act.wait_ge(sem["gn_done"], hp + 5)
                act.activation(TMn[:, hp, :], ps[:, 4 + hp, 0:T], ACT.Sqrt, bias=gn_eps, scale=1.0 / CH).then_inc(sem["gn_evac"], 1)
            for k in range(KD):
                act.wait_ge(sem["x1_ready"], 2 * k + 2)
                act.activation(SQ[:, k, :], XT[:, k, :], ACT.Square).then_inc(sem["sq2_ready"], 1)
            act.wait_ge(sem["ms_ready"], 2)
            act.activation(RS[:, :], RS[:, :], ACT.Sqrt).then_inc(sem["sqrt_done"], 1)
            for i in range(6):
                n = i // 2
                nt = TILES[n][1]
                act.wait_ge(sem["h2r_done"], i + 1)
                if i == 0:
                    act.wait_ge(sem["xr_zero"], 1)
                act.copy(XR[0:nt, n, (i % 2) * 512:(i % 2) * 512 + 512], ps[0:nt, i % 4, :]).then_inc(sem["h2r_evac"], 1)
            for n, (_, nt) in enumerate(TILES):
                act.wait_ge(sem["top_ready"], n + 1)
                act.activation(st[0:nt, 56 + 4 * n:60 + 4 * n], mx8[0:nt, n, 0:4], ACT.Exp, bias=st[0:nt, 70 + n:71 + n],
                               accum_out=st[0:nt, 76 + n:77 + n]).then_inc(sem["top_exp"], 1)

            act.wait_ge(sem["rounds_ready"], 1)
            rounds = act.value_load(rounds_i[0:1, 0:1], min_val=1, max_val=MAXR)

            def scatter_matrix():
                act.copy(GT[0:C, 0, :], ps[0:C, 1, 0:T]).then_inc(sem["gt_evac"], 1)
                act.copy(GT[C:P, 1, :], ps[C:P, 1, 0:T]).then_inc(sem["gt_evac"], 1)

            act.wait_ge(sem["xr_done"], 1)
            act.copy(XGR, ps[:, 0, :]).then_inc(sem["xr_evac"], 1)
            act.wait_ge(sem["xg_done"], 1)
            act.copy(XGf, ps[:, 5, :]).then_inc(sem["xg_evac"], 1)
            act.wait_ge(sem["gt_zero"], 1)
            act.wait_ge(sem["gt_done"], 1)
            scatter_matrix()
            with act.Fori(0, rounds * NE) as i:
                for h in range(2):
                    act.wait_ge(sem["u_done"], 2 * i + h + 1)
                    act.copy(UR[:, h, :], ps[:, 2 + h, :]).then_inc(sem["ur_evac"], 1)
                act.wait_ge(sem["ug_ready"], 2 * i + 1)
                act.activation(US_, UG, ACT.Sigmoid, scale=1.702).then_inc(sem["us_ready"], 1)
                act.wait_ge(sem["xr_done"], i + 2)
                act.copy(XGR, ps[:, 0, :]).then_inc(sem["xr_evac"], 1)
                act.wait_ge(sem["ug_ready"], 2 * i + 2)
                act.activation(US_, UG, ACT.Sigmoid, scale=1.702).then_inc(sem["us_ready"], 1)
                act.wait_ge(sem["y2_done"], i + 1)
                act.copy(YS, ps[:, 4, :]).then_inc(sem["ys_evac"], 1)
                act.wait_ge(sem["xg_done"], i + 2)
                act.copy(XGf, ps[:, 5, :]).then_inc(sem["xg_evac"], 1)
                act.wait_ge(sem["comb_done"], 8 * i + 16)
                scatter_matrix()
            for i in range(6):
                n = i // 2
                nt = TILES[n][1]
                act.wait_ge(sem["fin_done"], i + 1)
                act.copy(fin[0:nt, n, (i % 2) * 512:(i % 2) * 512 + 512], ps[0:nt, i % 4, :]).then_inc(sem["fin_evac"], 1)
            for name, total in (("st_k", 32), ("st_kv", 64), ("st_w", 32)):
                act.wait_ge(sem[name], total)

        @block.tensor
        def _(pe):
            mm, tr = nc.tensor.matmul, nc.tensor.transpose
            a = [0]

            def group():
                g = a[0]
                a[0] += 1
                if g >= 4:
                    pe.wait_ge(sem["a_evac"], g - 3)
                return ps[:, g % 4, :]

            def weights(kind, j):
                g = STREAM_AT[kind, j]
                pe.wait_ge(sem[f"ring{g % RING_PRE}"], 16 * (g // RING_PRE + 1))
                return ring[:, g % RING_PRE, :, :]

            pe.wait_ge(sem["ld_cst"], 16)
            pe.wait_ge(sem["ld_par"], 16 * (len(PARAMS) + 2))
            tr(ps[:, 6, 0:NPAR], prow[0:NPAR, :], ID[0:NPAR, 0:NPAR]).then_inc(sem["setup_t"], 1)
            pe.wait_ge(sem["ld_b1"], 16)
            for i in range(4):
                last = tr(ps[:, 7, i * P:i * P + P], b1r[:, i, :], ID)
            last.then_inc(sem["setup_t"], 1)
            pe.wait_ge(sem["silu_ready"], 1)
            for k in range(KD):
                last = tr(ps[:, 4, 9 * k:9 * k + 9], crow[0:9, k * P:k * P + P], ID[0:9, 0:9])
            last.then_inc(sem["setup_t"], 1)
            pe.wait_ge(sem["ld_ss"], 16)
            for i in range(14):
                tr(ps[:, 5, NS * i:NS * i + NS], ssr[0:NS, i * P:i * P + P], ID[0:NS, 0:NS])
            pe.wait_ge(sem["ld_tab"], 16)
            mm(ps[0:HQ, 5, 256:256 + KEYS], tab[:, :], cst[0:NE, K_OB:K_OB + KEYS], start=True, stop=True).then_inc(sem["setup_t"], 1)
            pe.wait_ge(sem["ld_x"], 48)
            for k in range(KD):
                bank = group()
                for n, (t0, nt) in enumerate(TILES):
                    last = tr(bank[:, t0:t0 + nt], XR[0:nt, n, k * P:k * P + P], ID[0:nt, 0:nt])
                last.then_inc(sem["a_done"], 1)
            pe.wait_ge(sem["setup_ready"], 1)
            for k in range(KD):
                pe.wait_ge(sem["a_evac"], k + 1)
                last = mm(ps[:, 6, 0:T], ONE, SQ[:, k, :], start=(k == 0), stop=(k == KD - 1))
            last.then_inc(sem["ss_done"], 1)

            def modulation(js, banks):
                for j in js:
                    w = weights("mod", j)
                    bank = banks[j % len(banks)]
                    if j >= len(banks):
                        pe.wait_ge(sem["mod_evac"], j - len(banks) + 1)
                    for s in range(4):
                        for k in range(KD):
                            last = mm(ps[:, bank, 9 * s:9 * s + 9], w[:, k, s * P:s * P + P], cT[:, k, :],
                                      start=(k == 0), stop=(k == KD - 1))
                    last.then_inc(sem["mod_done"], 1)

            def project(js):
                for j in js:
                    w = weights("win", j)
                    for s in range(4):
                        bank = group()
                        for k in range(KD):
                            last = mm(bank[:, 0:T], w[:, k, s * P:s * P + P], HT[:, k, :], start=(k == 0), stop=(k == KD - 1))
                        last.then_inc(sem["a_done"], 1)

            pe.wait_ge(sem["setup_ready"], 3)
            pe.wait_ge(sem["setup_ready"], 4)
            modulation(range(4), [4, 5])
            pe.wait_ge(sem["h1_ready"], 1)
            project(WIN1)
            pe.wait_ge(sem["ms_ready"], 1)
            pe.wait_ge(sem["setup_ready"], 2)
            for i in range(4):
                if i >= 2:
                    pe.wait_ge(sem["sh_evac"], i - 1)
                for c in range(4 * i, min(4 * i + 4, 14)):
                    last = tr(ps[0:9, 6 + i % 2, (c % 4) * P:(c % 4) * P + P], PTv[:, CR + c, NP - 1:T], ID)
                last.then_inc(sem["sh_t"], 1)
            pe.wait_ge(sem["ld_lw"], 48)
            pe.wait_ge(sem["lora_in"], 1)
            for hp in range(4):
                mm(group()[:, 0:T], LWw[0:64, hp * P:hp * P + P], XMv[0:64, 12, :], start=True, stop=True).then_inc(sem["a_done"], 1)
            for hp in range(4):
                mm(group()[:, 0:T], LWw[64:128, hp * P:hp * P + P], XMv[64:128, 12, :], start=True, stop=True).then_inc(sem["a_done"], 1)
            pe.wait_ge(sem["lora_in"], 2)
            for hp in range(4):
                mm(group()[:, 0:T], LWg[:, hp * P:hp * P + P], XMv[:, 13, :], start=True, stop=True).then_inc(sem["a_done"], 1)
            pe.wait_ge(sem["kksq_ready"], 1)
            for hp in range(4):
                mm(group()[:, 0:T], BO, SQ[:, hp, :], start=True, stop=True).then_inc(sem["a_done"], 1)
            pe.wait_ge(sem["qksq_ready"], 1)
            for i in range(5):
                mm(group()[:, 0:T], BO, XRf[:, i * T:i * T + T], start=True, stop=True).then_inc(sem["a_done"], 1)
            pe.wait_ge(sem["sh_evac"], 4)
            modulation(range(4, 12), [4, 5, 6, 7])

            pe.wait_ge(sem["a_evac"], A_WIN2)
            pe.wait_ge(sem["qk_ready"], 1)
            for kv in range(HKV):
                mm(ps[:, kv, 0:T], II[64 * kv:64 * kv + 64, :], PTv[64 * kv:64 * kv + 64, CK, :],
                   start=True, stop=True).then_inc(sem["kvrow_done"], 1)
            for n, (t0, nt) in enumerate(TILES):
                tr(ps[0:nt, 2, n * P:n * P + P], PTv[:, CV, t0:t0 + nt], ID)
            for n, (t0, nt) in enumerate(TILES[1:]):
                last = tr(ps[0:nt, 3, n * P:n * P + P], PTv[:, CK, t0:t0 + nt], ID)
            last.then_inc(sem["kvrow_done"], 1)
            pe.wait_ge(sem["ld_kc"], 16)
            pe.wait_ge(sem["mod_evac"], 12)
            for b in range(NS):
                last = tr(ps[:, 4 + b // 4, (b % 4) * P:(b % 4) * P + P], kcr[:, b, :], ID)
            last.then_inc(sem["kc_done"], 1)
            pe.wait_ge(sem["ld_hk"], 16)
            HKf = HK.rearrange("p a b -> p (a b)")
            for i in range(4):
                if i == 2:
                    pe.wait_ge(sem["kc_evac"], 1)
                mm(ps[:, [6, 7, 4, 5][i], :], cst[:, K_REV:K_REV + P], HKf[:, i * 512:i * 512 + 512],
                   start=True, stop=True).then_inc(sem["bm_done"], 1)
            pe.wait_ge(sem["kvrow_evac"], 1)
            for h in range(HQ):
                s = h % 2
                last = mm(ps[:, 2 + s, NS * (h // 2):NS * (h // 2) + NS], II[64 * s:64 * s + 64, :], PTv[64 * s:64 * s + 64, h // 2, NP:T],
                          start=True, stop=True)
            last.then_inc(sem["qs_done"], 1)
            pe.wait_ge(sem["qs_evac"], 1)
            pe.wait_ge(sem["bm_evac"], 4)

            def scores(g4):
                n, kv = g4 // 2, g4 % 2
                J = P if n == 0 else 2 * P
                for g in range(GQA):
                    h = GQA * kv + g
                    s = h % 2
                    last = mm(ps[:, 2 * (g4 % 2) + s, (g // 2) * J:(g // 2) * J + J],
                              PTv[64 * s:64 * s + 64, h // 2, n * P:n * P + P], kd[64 * s:64 * s + 64, kv, 0:J],
                              start=True, stop=True)
                last.then_inc(sem["att_s"], 1)

            scores(0)
            scores(1)
            for g4 in range(4):
                n, kv = g4 // 2, g4 % 2
                pe.wait_ge(sem["att_p"], g4 + 1)
                for jt in range(n + 1):
                    if g4:
                        pe.wait_ge(sem["att_pte"], g4 if n == 0 else 2 * g4 - 2)
                    for g in range(GQA):
                        last = tr(ps[:, 4 + jt, g * P:g * P + P], Pm[:, g, jt * P:jt * P + P], ID)
                    last.then_inc(sem["att_pt"], 1)
                if g4 < 2:
                    scores(g4 + 2)
                pe.wait_ge(sem["att_pte"], g4 + 1 if n == 0 else 2 * g4)
                if g4:
                    pe.wait_ge(sem["att_oe"], g4)
                for g in range(GQA):
                    s = g % 2
                    for jt in range(n + 1):
                        last = mm(ps[64 * s:64 * s + 64, 6, (g // 2) * P:(g // 2) * P + P], vr[:, jt, 64 * kv:64 * kv + 64],
                                  pT[:, g, jt, :], start=(jt == 0), stop=(jt == n))
                last.then_inc(sem["att_o"], 1)
            for b in range(NS):
                last = mm(ps[0:HQ, b // 3, (b % 3) * KEYS:(b % 3) * KEYS + KEYS], Qs[:, :, b], kcT[:, b, :], start=True, stop=True)
            last.then_inc(sem["smp_done"], 1)
            pe.wait_ge(sem["smp_p"], 1)
            for b in range(NS):
                tr(ps[:, 3, b * NS:b * NS + NS], SsT[0:HQ, b, 0:P], ID[0:HQ, 0:HQ])
            tr(ps[0:NS, 3, 64:72], SsT[0:HQ, :, P], ID[0:HQ, 0:HQ]).then_inc(sem["smp_done"], 1)
            pe.wait_ge(sem["smp_pte"], 1)
            pe.wait_ge(sem["ld_vc"], 16)
            for b in range(NS):
                mm(ps[:, 7, b * HQ:b * HQ + HQ], vcr[:, b, :], pTs[:, b, :], start=True, stop=False)
                last = mm(ps[:, 7, b * HQ:b * HQ + HQ], vr[0:NS, 2, :], PSf[:, b, :], start=False, stop=True)
            last.then_inc(sem["smp_done"], 1)
            pe.wait_ge(sem["os_ready"], 1)
            for kv in range(HKV):
                last = mm(ps[:, 2 + kv, 0:32].rearrange("p (a b) -> p a b", b=4), II[64 * kv:64 * kv + 64, :],
                          OS[64 * kv:64 * kv + 64, :, 4 * kv:4 * kv + 4], start=True, stop=True)
            last.then_inc(sem["smp_done"], 1)

            pe.wait_ge(sem["zr_ready"], 1)
            pe.wait_ge(sem["smp_oe"], 1)
            for hp in range(4):
                mm(ps[:, hp, 0:T], BO, TM[:, hp, :], start=True, stop=True).then_inc(sem["bon_done"], 1)
            for i in range(8):
                mat, n = i // 2, i % 2
                if i < 4:
                    pe.wait_ge(sem["bon_evac"], i + 1)
                if i >= 4:
                    pe.wait_ge(sem["row_evac"], i - 3)
                for hp in range(4):
                    if mat == 0:
                        for par in range(2):
                            last = mm(ps[64 * par:64 * par + 64, i % 4, hp * P:hp * P + P], ZR[:, hp, 2 * n + par, 0, :], ID,
                                      start=True, stop=True)
                        continue
                    src = [Bh[:, hp, n * P:n * P + P], Kh[:, hp, n * P:n * P + P], XMv[:, 8 + hp, n * P:n * P + P]][mat - 1]
                    last = tr(ps[:, i % 4, hp * P:hp * P + P], src, ID)
                last.then_inc(sem["row_done"], 1)
            units = [(n, h, par) for n in range(2) for h in range(HQ) for par in range(2)]

            def half(x, par):
                return x[64 * par:64 * par + 64]

            for n in range(2):
                if n:
                    pe.wait_ge(sem["nr_ready"], 1)
                    pe.wait_ge(sem["kr_ready"], 1)
                for q, M in enumerate((Bh, Kh)):
                    for _, h, par in units[:16]:
                        s, hp, c = h % 2, h // 2, 2 * n + par
                        last = mm(ps[64 * par:64 * par + 64, 4 + 2 * q + s, hp * P:hp * P + P],
                                  M[64 * s:64 * s + 64, hp, c * CH:c * CH + CH],
                                  ZR[64 * s:64 * s + 64, hp, c, :, :].rearrange("p a b -> p (a b)"), start=True, stop=True)
                    last.then_inc(sem["ab_done"], 1)
            for i in range(len(LEVELS)):
                pe.wait_ge(sem["nm_ready"], i + 1)
                for n in range(2):
                    if i == 0:
                        pe.wait_ge(sem["row_evac"], 8)
                        pe.wait_ge(sem["nr_ready"], 2)
                        pe.wait_ge(sem["kr_ready"], 2)
                    else:
                        pe.wait_ge(sem["x_ready"], 2 * (i - 1) + n + 1)
                    for _, h, par in units[:16]:
                        u = 8 * n + h
                        rhs = II[64 * par:64 * par + 64, 0:CH] if i == 0 else half(X, par)[:, u, :]
                        last = mm(ps[64 * par:64 * par + 64, 4 * n, h * CH:h * CH + CH], half(NM[i % 2], par)[:, u, :], rhs,
                                  start=True, stop=True)
                    last.then_inc(sem["y_done"], 1)
                if i == 0:
                    continue
                for n in range(2):
                    pe.wait_ge(sem["y_evac"], 2 * (i - 1) + n + 1)
                    if i < len(LEVELS) - 1:
                        for _, h, par in units[:16]:
                            u = 8 * n + h
                            last = mm(ps[64 * par:64 * par + 64, 4 * n + 1, h * CH:h * CH + CH], half(XX, par)[:, u, :],
                                      half(Y, par)[:, u, :], start=True, stop=True)
                    for _, h, par in units[:16]:
                        u = 8 * n + h
                        last = mm(ps[64 * par:64 * par + 64, 4 * n + 2, h * CH:h * CH + CH], half(Y, par)[:, u, :],
                                  half(XX, par)[:, u, :], start=True, stop=True)
                    last.then_inc(sem["dx_done"], 1)
            for n in range(2):
                for _, h, par in units[:16]:
                    u = 8 * n + h
                    last = mm(ps[64 * par:64 * par + 64, 3 + 4 * n, h * CH:h * CH + CH], half(KR, par)[:, u, 0:CH],
                              half(Vr, par)[:, u, :], start=True, stop=True)
                last.then_inc(sem["u0_done"], 1)
            for n in range(2):
                pe.wait_ge(sem["x_ready"], 2 * (len(LEVELS) - 1) + n + 1)
                pe.wait_ge(sem["u0_evac"], n + 1)
                for _, h, par in units[:16]:
                    u = 8 * n + h
                    last = mm(ps[64 * par:64 * par + 64, 4 * n + h // 4, (h % 4) * P:(h % 4) * P + P], half(XX, par)[:, u, :],
                              half(ZU, par)[:, u, :], start=True, stop=True)
                last.then_inc(sem["xzw_done"], 1)
            pe.wait_ge(sem["xzw_evac"], 2)
            allu = [(h, c) for h in range(HQ) for c in range(NCHUNK)]

            def head_chunk(bank, h, c):
                col = (h // 2) * 2 * CH + (c // 2) * CH
                s = h % 2
                return ps[64 * s:64 * s + 64, bank + c % 2, col:col + CH]

            def rows_of(M, h, c, lo, hi):
                return M[64 * (c % 2):64 * (c % 2) + 64, 8 * (c // 2) + h, lo:hi]

            for h, c in allu:
                last = mm(head_chunk(0, h, c), rows_of(XZW, h, c, 0, CH), rows_of(NR, h, c, CH, P), start=True, stop=True)
            last.then_inc(sem["carry_done"], 1)
            for h, c in allu:
                last = mm(head_chunk(4, h, c), rows_of(XZW, h, c, 0, CH), rows_of(Br, h, c, 0, CH), start=True, stop=True)
            last.then_inc(sem["carry_done"], 1)
            for h, c in allu:
                mm(head_chunk(2, h, c), rows_of(Br, h, c, 0, CH), rows_of(XZW, h, c, CH, P), start=True, stop=False)
                last = mm(head_chunk(2, h, c), rows_of(Kr, h, c, 0, CH), rows_of(Vr, h, c, 0, CH), start=False, stop=True)
            last.then_inc(sem["carry_done"], 1)
            pe.wait_ge(sem["dr_ready"], 2)
            pe.wait_ge(sem["mc_ready"], 2)
            for c in range(NCHUNK):
                if c:
                    pe.wait_ge(sem["g_ready"], c)
                    for h in range(HQ):
                        s, hp = h % 2, h // 2
                        last = mm(ps[64 * s:64 * s + 64, 7, hp * CH:hp * CH + CH], MC[64 * s:64 * s + 64, hp, c, :],
                                  G4[64 * s:64 * s + 64, c - 1, hp, :], start=True, stop=True)
                    last.then_inc(sem["gm_done"], 1)
                for h in range(HQ):
                    s, hp = h % 2, h // 2
                    out = head_chunk(4, h, c)
                    mm(out, rows_of(XZW, h, c, CH, P), rows_of(NR, h, c, CH, P), start=True, stop=False)
                    last = mm(out, rows_of(Vr, h, c, 0, CH), rows_of(KR, h, c, CH, P), start=False, stop=True)
                for h in range(HQ if c else 0):
                    s, hp = h % 2, h // 2
                    last = mm(ps[64 * s:64 * s + 64, 6 if c < 3 else 3, (c - 1) % 2 * 256 + hp * CH:(c - 1) % 2 * 256 + hp * CH + CH],
                              G4[64 * s:64 * s + 64, c - 1, hp, :], ZR[64 * s:64 * s + 64, hp, c, 1, :], start=True, stop=True)
                last.then_inc(sem["o_done"], 1)
            pe.wait_ge(sem["g_ready"], NCHUNK)
            pe.wait_ge(sem["dr_ready"], 2)
            for h in range(HQ):
                s, hp = h % 2, h // 2
                last = mm(ps[64 * s:64 * s + 64, 2, hp * CH:hp * CH + CH], G4[64 * s:64 * s + 64, NCHUNK - 1, hp, :],
                          II[64 * s:64 * s + 64, 0:CH], start=True, stop=True)
            last.then_inc(sem["wps_done"], 1)
            pe.wait_ge(sem["wps_evac"], 1)
            pe.wait_ge(sem["ot_ready"], 1)

            def spread(q):
                pe.wait_ge(sem["ex_ready"], q + 1)
                if q:
                    pe.wait_ge(sem["smp_step"], q)
                EXf = EX.rearrange("p a b -> p (a b)")
                for i in range(4):
                    last = mm(ps[:, 4 + i, :], BO, EXf[:, i * 512:i * 512 + 512], start=True, stop=True)
                last.then_inc(sem["ex_used"], 1)

            spread(0)
            for q, j in enumerate(WIN2):
                project([j])
                spread(q + 1)
            pe.wait_ge(sem["smp_step"], 5)
            for hp in range(4):
                mm(ps[:, 4 + hp, 0:T], BO, OT[:, hp, :], start=True, stop=True).then_inc(sem["gn_done"], 1)
            pe.wait_ge(sem["gnsq_ready"], 1)
            for hp in range(4):
                mm(ps[:, 4 + hp, 0:T], BO, OSQ[:, hp, :], start=True, stop=True).then_inc(sem["gn_done"], 1)
            pe.wait_ge(sem["a_evac"], A_TOTAL)
            wpa = weights("pa", 0).rearrange("p k n -> p (k n)").rearrange("p (k n) -> p k n", n=D)
            for q, src in enumerate(("pa", "pb")):
                weights(src, 0)
            wpb = ring[:, STREAM_AT["pb", 0] % RING_PRE, :, :].rearrange("p k n -> p (k n)").rearrange("p (k n) -> p k n", n=D)
            for k in range(KD):
                for q, (w, src) in enumerate(((wpa, OA), (wpb, OT))):
                    if q and k == 0:
                        pe.wait_ge(sem["ob_ready"], 1)
                    if k >= 2:
                        pe.wait_ge(sem["pab_evac"], 2 * k - 3 + q)
                    for i in range(4):
                        last = mm(ps[:, 2 * (k % 2) + q, 0:T], w[:, i, k * P:k * P + P], src[:, i, :], start=(i == 0), stop=(i == 3))
                    last.then_inc(sem["pab_done"], 1)
            pe.wait_ge(sem["m_ready"], KD)
            pe.wait_ge(sem["ob_ready"], 1)
            for k in range(KD):
                w = weights("wo", k // 4)
                if k >= 4:
                    pe.wait_ge(sem["x1_ready"], 2 * (k - 3))
                for i in range(KD):
                    last = mm(ps[:, 4 + k % 4, 0:T], w[:, i, (k % 4) * P:(k % 4) * P + P], HT[:, i, :], start=(i == 0), stop=(i == KD - 1))
                last.then_inc(sem["wo_done"], 1)
            for k in range(KD):
                pe.wait_ge(sem["sq2_ready"], k + 1)
                last = mm(ps[:, 0, 0:T], ONE, SQ[:, k, :], start=(k == 0), stop=(k == KD - 1))
            last.then_inc(sem["ss_done"], 1)
            pe.wait_ge(sem["h2_ready"], 1)
            pe.wait_ge(sem["ld_r"], 48)
            for n, (t0, nt) in enumerate(TILES):
                for k in range(KD):
                    last = mm(ps[0:nt, 4, n * NE:n * NE + NE], HT[:, k, t0:t0 + nt], wr[:, k, :], start=(k == 0), stop=(k == KD - 1))
                last.then_inc(sem["lg_done"], 1)
            for i in range(6):
                n = i // 2
                t0, nt = TILES[n]
                if i >= 4:
                    pe.wait_ge(sem["h2r_evac"], i - 3)
                for k in range(4 * (i % 2), 4 * (i % 2) + 4):
                    last = tr(ps[0:nt, i % 4, (k % 4) * P:(k % 4) * P + P], HT[:, k, t0:t0 + nt], ID)
                last.then_inc(sem["h2r_done"], 1)
            pe.wait_ge(sem["msk_ready"], 3)
            for n, (t0, nt) in enumerate(TILES):
                for i in range(n + 1):
                    mi = TILES[i][1]
                    mm(ps[0:nt, 5, n * NE:n * NE + NE], (cst[0:mi, K_US:K_US + nt] if i == n else ONE[0:mi, 0:nt]),
                       MSK[0:mi, i, :], start=(i == 0), stop=(i == n))
            for i in range(3):
                mi = TILES[i][1]
                last = mm(ps[:, 5, 96:96 + NE], ONE[0:mi, :], MSK[0:mi, i, :], start=(i == 0), stop=(i == 2))
            last.then_inc(sem["pos_done"], 1)
            pe.wait_ge(sem["pos_evac"], 1)
            for n, (t0, nt) in enumerate(TILES):
                last = tr(ps[0:NE, 4, t0:t0 + nt], GTE[0:nt, n, :], ID[0:nt, 0:nt])
            last.then_inc(sem["gT_done"], 1)
            pe.wait_ge(sem["gT_ready"], 1)
            for k in range(KD):
                if k >= 2:
                    pe.wait_ge(sem["comb_used"], k - 1)
                mm(ps[:, 6 + k % 2, 0:T], b2r[0:NE, k * P:k * P + P], gT[0:NE, :], start=True, stop=True).then_inc(sem["comb_done"], 1)

            def gather():
                for n in range(3):
                    for s in range(2):
                        last = mm(ps[64 * s:64 * s + 64, 0, :], OH[:, n, :], XR[:, n, s * 512:s * 512 + 512], start=(n == 0), stop=(n == 2))
                last.then_inc(sem["xr_done"], 1)

            def gather_transposed():
                for k in range(4):
                    last = tr(ps[:, 5, k * P:k * P + P], XGR[:, k * P:k * P + P], ID)
                last.then_inc(sem["xg_done"], 1)
                for n, (t0, nt) in enumerate(TILES):
                    last = tr(ps[:, 1, t0:t0 + nt], OG[0:nt, n, :], ID[0:nt, 0:nt])
                last.then_inc(sem["gt_done"], 1)

            pe.wait_ge(sem["rounds_ready"], 1)
            rounds = pe.value_load(rounds_i[0:1, 0:1], min_val=1, max_val=MAXR)
            pe.wait_ge(sem["h2r_evac"], 6)
            pe.wait_ge(sem["oh_ready"], 1)
            gather()
            pe.wait_ge(sem["xr_evac"], 1)
            gather_transposed()
            before = [uses_before(c) for c in range(6)]
            with pe.Fori(0, rounds * NE) as i:
                pe.wait_ge(sem["xg_evac"], i + 1)
                for hh in range(2):
                    for lin in range(2):
                        c = 2 * hh + lin
                        pe.wait_ge(sem[f"ring{c}"], i * 16 + 16 * (before[c] + 1))
                    for k in range(KD):
                        for lin in range(2):
                            last = mm(ps[64 * lin:64 * lin + 64, 2 + hh, :], XG[:, k % 4, k // 4, :], ring[:, 2 * hh + lin, k, :],
                                      start=(k == 0), stop=(k == KD - 1))
                    last.then_inc(sem["u_done"], 1)

                def hidden_transposed(hh):
                    pe.wait_ge(sem["ur_evac"], 2 * i + hh + 1)
                    for f in range(4):
                        last = tr(ps[:, 2 + hh, f * P:f * P + P], UR[:, hh, f * P:f * P + P], ID)
                    last.then_inc(sem["ut_done"], 1)

                hidden_transposed(0)
                pe.wait_ge(sem["oh_ready"], i + 2)
                gather()
                hidden_transposed(1)
                for c in (4, 5):
                    pe.wait_ge(sem[f"ring{c}"], i * 16 + 16 * (before[c] + 1))
                for f in range(NF):
                    if f % 4 == 0:
                        pe.wait_ge(sem["ac_ready"], 2 * i + f // 4 + 1)
                    for hh in range(2):
                        last = mm(ps[64 * hh:64 * hh + 64, 4, :], AC[:, f, :], ring[:, 4 + hh, f, :], start=(f == 0), stop=(f == NF - 1))
                last.then_inc(sem["y2_done"], 1)
                pe.wait_ge(sem["xr_evac"], i + 2)
                pe.wait_ge(sem["gt_evac"], 2 * i + 2)
                gather_transposed()
                pe.wait_ge(sem["ys_evac"], i + 1)
                for k in range(KD):
                    pe.wait_ge(sem["comb_used"], 8 * i + 7 + k)
                    mm(ps[:, 6 + k % 2, 0:T], YS[:, (k % 4) * P:(k % 4) * P + P], GT[:, k // 4, :], start=True, stop=True).then_inc(sem["comb_done"], 1)
            pe.wait_ge(sem["gt_evac"], rounds * (2 * NE) + 2)
            pe.wait_ge(sem["x2_ready"], KD)
            for i in range(6):
                n = i // 2
                t0, nt = TILES[n]
                if i >= 4:
                    pe.wait_ge(sem["fin_evac"], i - 3)
                for k in range(4 * (i % 2), 4 * (i % 2) + 4):
                    last = tr(ps[0:nt, i % 4, (k % 4) * P:(k % 4) * P + P], XT[:, k, t0:t0 + nt], ID)
                last.then_inc(sem["fin_done"], 1)

        @block.vector
        def _(dve):
            v = nc.vector
            chain = Chain(dve, sem["dve_chain"])

            def done(instruction, name, value):
                instruction.then_inc(sem[name], 1)
                dve.wait_ge(sem[name], value)

            v.memset(epsc[:, 0:1], 1e-6)
            v.memset(epsc[:, 1:2], 64e-5)
            v.memset(Qs[:, :, :], 0.0).then_inc(sem["qs_zero"], 1)
            dve.wait_ge(sem["ld_c"], 32)
            dve.wait_ge(sem["csig_ready"], 1)
            v.tensor_tensor(crow[0:9, :], crow[0:9, :], csig[0:9, :], ALU.mult).then_inc(sem["silu_ready"], 1)
            dve.wait_ge(sem["setup_t"], 1)
            done(v.tensor_copy(PC[:, :], ps[:, 6, 0:NPAR]), "setup_ready", 1)
            dve.wait_ge(sem["setup_t"], 2)
            v.tensor_copy(b1T[:, :], ps[:, 7, :]).then_inc(sem["setup_ready"], 1)
            dve.wait_ge(sem["setup_t"], 3)
            v.tensor_copy(cT[:, :, :], ps[:, 4, 0:72].rearrange("p (a b) -> p a b", b=9)).then_inc(sem["setup_ready"], 1)
            dve.wait_ge(sem["setup_t"], 4)
            chain(v.tensor_copy(SS[:, :, :], ps[:, 5, 0:112].rearrange("p (a b) -> p a b", b=NS)))
            v.tensor_copy(brow[:, 0:KEYS], ps[0:HQ, 5, 256:256 + KEYS]).then_inc(sem["brow_ready"], 1)
            dve.wait_ge(sem["brow_ready"], 1)
            dve.sem_inc(sem["setup_ready"], 1)

            def rms(i):
                dve.wait_ge(sem["ss_done"], i)
                v.tensor_scalar(RS[:, :], ps[:, 6 if i == 1 else 0, 0:T], 1.0 / D, 1e-5, ALU.mult, ALU.add).then_inc(sem["ms_ready"], 1)
                dve.wait_ge(sem["sqrt_done"], i)
                chain(v.reciprocal(RS[:, :], RS[:, :]))
                chain(v.tensor_tensor(HT[:, :, :], XT[:, :, :], RS[:, :].unsqueeze(1).broadcast_to([P, KD, T]), ALU.mult))

            def modulate(shift, scale, name):
                chain(v.scalar_tensor_tensor(out=A1[:, :, :], in0=modT[:, scale:scale + KD, :], scalar=1.0,
                                             in1=PC[:, PCOL[name]:PCOL[name] + KD].unsqueeze(2).broadcast_to([P, KD, 9]),
                                             op0=ALU.add, op1=ALU.mult))
                for k in range(KD):
                    chain(v.tensor_scalar(HT[:, k, 0:NP], HT[:, k, 0:NP], A1[:, k, 0:1], modT[:, shift + k, 0:1], ALU.mult, ALU.add))
                chain(v.tensor_tensor(HT[:, :, NP:T], HT[:, :, NP:T], A1[:, :, 1:9], ALU.mult))
                return v.tensor_tensor(HT[:, :, NP:T], HT[:, :, NP:T], modT[:, shift:shift + KD, 1:9], ALU.add)

            def add_bias(lo, hi):
                return modT[:, lo:hi, :], PC[:, PCOL["b_mod"] + lo:PCOL["b_mod"] + hi].unsqueeze(2).broadcast_to([P, hi - lo, 9])

            rms(1)
            for m in range(4):
                dve.wait_ge(sem["mod_done"], m + 1)
                out, bias = add_bias(4 * m, 4 * m + 4)
                done(v.tensor_tensor(out, ps[:, 4 + m % 2, 0:36].rearrange("p (a b) -> p a b", b=9), bias, ALU.add), "mod_evac", m + 1)
            done(modulate(0, 8, "norm1"), "h1_ready", 1)

            dve.wait_ge(sem["a_evac"], A_WIN1 + 16)
            R0 = CR
            chain(v.tensor_tensor(XMv[:, :, 1:NP], PTv[:, R0:NCH, 0:NP - 1], PTv[:, R0:NCH, 1:NP], ALU.subtract))
            chain(v.tensor_scalar(XMv[:, :, 0:1], PTv[:, R0:NCH, 0:1], -1.0, None, ALU.mult))
            chain(v.tensor_tensor(XMv[:, :, NP:T], SS[:, :, :], PTv[:, R0:NCH, NP:T], ALU.subtract))
            for i in [12, 13] + list(range(12)):
                ins = v.scalar_tensor_tensor(out=XMv[:, i, :], in0=XMv[:, i, :], scalar=par("rw_mu", i), in1=PTv[:, R0 + i, :],
                                             op0=ALU.mult, op1=ALU.add)
                if i == 11:
                    done(ins, "mixed", 1)
                else:
                    chain(ins)
            for i in range(4):
                dve.wait_ge(sem["sh_t"], i + 1)
                w = min(512, RW - 512 * i)
                done(v.tensor_copy(ssr[0:9, 512 * i:512 * i + w], ps[0:9, 6 + i % 2, 0:w]), "sh_evac", i + 1)
            for hp in range(4):
                chain(v.tensor_scalar(NK[:, hp, :], XMv[:, 4 + hp, :], par("rw_k_k", hp), None, ALU.mult))
            done(v.tensor_tensor(SQ[:, 0:4, :], NK, NK, ALU.mult), "kksq_ready", 1)
            dve.wait_ge(sem["a_evac"], A_LORA)
            qk = PT[:, 0:5 * T]
            done(v.tensor_tensor(XRf[:, 0:5 * T], qk, qk, ALU.mult), "qksq_ready", 1)
            dve.wait_ge(sem["a_evac"], A_LORA + 4)
            LDf, CSf = RZ[:, 0:4 * T], RZ[:, 1056:1056 + 4 * NP]
            chain(v.tensor_scalar(LDf, LDf, -E_HALF, None, ALU.mult))
            for hp in range(4):
                for c in range(NCHUNK):
                    ins = v.tensor_tensor_scan(out=CS[:, hp, c * CH:c * CH + CH], data0=ONE[:, 0:CH], data1=LD[:, hp, c * CH:c * CH + CH],
                                               initial=0.0, op0=ALU.mult, op1=ALU.add)
                    if hp == 3 and c == NCHUNK - 1:
                        done(ins, "cs_ready", 1)
                    else:
                        chain(ins)
            done(v.tensor_tensor(eM, CS, LD[:, :, 0:NP], ALU.subtract), "cs_ready", 2)
            dve.wait_ge(sem["a_evac"], A_LORA + 16)
            Rn = SQ[:, 4:8, :]
            chain(v.tensor_scalar(Rn, Rn, 1e-12, None, ALU.max))
            chain(v.reciprocal(Rn, Rn))
            chain(v.scalar_tensor_tensor(out=NK, in0=NK, scalar=-1.0, in1=Rn, op0=ALU.mult, op1=ALU.mult))
            for hp in range(4):
                chain(v.tensor_scalar(TM[:, hp, :], Aa[:, hp, :], 1.0, par("rw_k_a", hp), ALU.subtract, ALU.mult))
            k_mod, r, vv = XMv[:, 4:8, :], XMv[:, 0:4, :], XMv[:, 8:12, :]
            chain(v.scalar_tensor_tensor(out=k_mod, in0=TM, scalar=1.0, in1=k_mod, op0=ALU.add, op1=ALU.mult))
            chain(v.scalar_tensor_tensor(out=Aa, in0=NK, scalar=-1.0, in1=Aa, op0=ALU.mult, op1=ALU.mult))
            for hp in range(4):
                chain(v.scalar_tensor_tensor(out=TM[:, hp, :], in0=r[:, hp, :], scalar=par("rw_r_k", hp), in1=k_mod[:, hp, :],
                                             op0=ALU.mult, op1=ALU.mult))
            dve.wait_ge(sem["decays"], 4)

            def by_chunk(x):
                return x[:, :, 0:NP].rearrange("p h (c t) -> p h c t", t=CH)

            chain(v.tensor_tensor(ZR[:, :, :, 0, :], by_chunk(NK), by_chunk(eM), ALU.mult))
            chain(v.tensor_tensor(ZR[:, :, :, 1, :], by_chunk(r), by_chunk(eP), ALU.mult))
            chain(v.tensor_tensor(Bh, Aa[:, :, 0:NP], eN, ALU.mult))
            chain(v.tensor_tensor(Kh, k_mod[:, :, 0:NP], eN, ALU.mult))
            chain(v.tensor_copy(pcol[:, :, :], by_chunk(eP)[:, :, :, CH - 1]))
            for q, src in ((0, NK), (2, Aa), (3, k_mod), (4, r), (5, vv)):
                chain(v.tensor_copy(SMP[:, q, :, :], src[:, :, NP:T]))
            dve.sem_inc(sem["zr_ready"], 1)
            dve.sem_inc(sem["smp_ready"], 1)

            dve.wait_ge(sem["a_evac"], A_WIN2)
            chain(v.reciprocal(XRf[:, 5 * T:10 * T], XRf[:, 5 * T:10 * T]))
            chain(v.tensor_tensor(qk, qk, XRf[:, 5 * T:10 * T], ALU.mult))
            chain(v.tensor_scalar(PT[:, 0:4 * T], PT[:, 0:4 * T], par("q_norm"), SCALE, ALU.mult, ALU.mult))
            done(v.tensor_scalar(PTv[:, CK, :], PTv[:, CK, :], par("k_norm"), None, ALU.mult), "qk_ready", 1)
            dve.wait_ge(sem["kvrow_done"], 2)
            chain(v.tensor_copy(kd, ps[:, 0:2, 0:T]))
            dve.wait_ge(sem["kvrow_done"], 3)
            chain(v.tensor_copy(vr[:, 0:2, :], ps[:, 2, 0:2 * P].rearrange("p (a b) -> p a b", b=P)))
            chain(v.tensor_copy(vr[0:NS, 2, :], ps[0:NS, 2, 2 * P:3 * P]))
            chain(v.tensor_copy(kvr[:, 0, :], ps[:, 3, 0:P]))
            done(v.tensor_copy(kvr[0:NS, 1, :], ps[0:NS, 3, P:2 * P]), "kvrow_evac", 1)
            dve.wait_ge(sem["kc_done"], 1)
            dve.wait_ge(sem["ext_out"], 16)
            chain(v.tensor_copy(kcT[:, :, 0:P], ps[:, 4:6, :].rearrange("p a (b c) -> p (a b) c", c=P)))
            done(v.tensor_copy(kcT[:, :, P], PTv[:, CK, NP:T]), "kc_evac", 1)
            for i in range(4):
                dve.wait_ge(sem["bm_done"], i + 1)
                done(v.tensor_copy(BM[:, i * 512:i * 512 + 512], ps[:, [6, 7, 4, 5][i], :]), "bm_evac", i + 1)
            dve.wait_ge(sem["qs_done"], 1)
            dve.wait_ge(sem["qs_zero"], 1)
            for kv in range(HKV):
                rows = slice(64 * kv, 64 * kv + 64)
                ins = v.tensor_copy(Qs[rows, 4 * kv:4 * kv + 4, :].rearrange("p (j s) b -> p s j b", s=2),
                                    ps[rows, 2:4, 16 * kv:16 * kv + 16].rearrange("p s (j b) -> p s j b", b=NS))
                if kv:
                    done(ins, "qs_evac", 1)
                else:
                    chain(ins)
            BMv = BM[:, :].rearrange("p (a b) -> p a b", b=2 * P)
            dve.wait_ge(sem["ld_sink"], 32)

            def att_out(g4):
                n, kv = g4 // 2, g4 % 2
                dve.wait_ge(sem["att_o"], g4 + 1)
                done(v.tensor_copy(OA[:, 2 * kv:2 * kv + 2, n * P:n * P + P],
                                   ps[:, 6, 0:2 * P].rearrange("p (a b) -> p a b", b=P)), "att_oe", g4 + 1)

            for g4 in range(4):
                n, kv = g4 // 2, g4 % 2
                J = P if n == 0 else 2 * P
                b0 = 2 * (g4 % 2)
                dve.wait_ge(sem["att_s"], g4 + 1)
                S = ps[:, b0:b0 + 2, 0:2 * J].rearrange("p s (j q) -> p s j q", q=J)
                heads = slice(4 * kv, 4 * kv + 4)
                if g4:
                    dve.wait_ge(sem["att_pt"], g4 if n == 0 else 2 * g4 - 2)
                chain(v.tensor_tensor(Pm[:, :, 0:J].rearrange("p (j s) q -> p s j q", s=2), S,
                                      BMv[:, heads, 2 * P - J:2 * P].rearrange("p (j s) q -> p s j q", s=2), ALU.add))
                chain(v.tensor_reduce(st[:, 0:4], Pm[:, :, 0:J], AX.X, ALU.max))
                chain(v.tensor_tensor(st[:, 0:4], st[:, 0:4], sinkb[:, heads], ALU.max))
                chain(v.tensor_scalar(st[:, 4:8], st[:, 0:4], -1.0, None, ALU.mult))
                done(v.tensor_tensor(st[:, 12:16], sinkb[:, heads], st[:, 4:8], ALU.add), "att_max", g4 + 1)
                if g4:
                    att_out(g4 - 1)
                dve.wait_ge(sem["att_exp"], 5 * g4 + 5)
                chain(v.tensor_tensor(st[:, 8:12], st[:, 8:12], st[:, 12:16], ALU.add))
                chain(v.reciprocal(st[:, 8:12], st[:, 8:12]))
                done(v.tensor_tensor(Pm[:, :, 0:J], Pm[:, :, 0:J], st[:, 8:12].unsqueeze(2).broadcast_to([P, 4, J]), ALU.mult),
                     "att_p", g4 + 1)
            att_out(3)
            dve.wait_ge(sem["smp_done"], 1)
            for b0 in range(0, NS, 3):
                nb = min(3, NS - b0)
                chain(v.tensor_tensor(SsT[0:HQ, b0:b0 + nb, :], ps[0:HQ, b0 // 3, 0:nb * KEYS].rearrange("p (a b) -> p a b", b=KEYS),
                                      brow[:, 0:KEYS].unsqueeze(1).broadcast_to([HQ, nb, KEYS]), ALU.add))
            mx, es, sm = st[0:HQ, 40:48], st[0:HQ, 48:56], st[0:HQ, 32:40]
            chain(v.tensor_reduce(mx, SsT[0:HQ, :, :], AX.X, ALU.max))
            chain(v.tensor_scalar(mx, mx, sinkc[:, 0:1], None, ALU.max))
            chain(v.tensor_scalar(es, mx, -1.0, sinkc[:, 0:1], ALU.mult, ALU.add))
            done(v.tensor_tensor(SsT[0:HQ, :, :], SsT[0:HQ, :, :], mx.unsqueeze(2).broadcast_to([HQ, NS, KEYS]), ALU.subtract), "smp_max", 1)
            dve.wait_ge(sem["smp_exp"], 2)
            chain(v.tensor_reduce(sm, SsT[0:HQ, :, :], AX.X, ALU.add))
            chain(v.tensor_tensor(sm, sm, es, ALU.add))
            chain(v.reciprocal(sm, sm))
            done(v.tensor_tensor(SsT[0:HQ, :, :], SsT[0:HQ, :, :], sm.unsqueeze(2).broadcast_to([HQ, NS, KEYS]), ALU.mult), "smp_p", 1)
            dve.wait_ge(sem["smp_done"], 2)
            chain(v.tensor_copy(pTs[:, :, :], ps[:, 3, 0:64].rearrange("p (a b) -> p a b", b=HQ)))
            done(v.tensor_tensor(PSf[:, :, :], ps[0:NS, 3, 64:72].unsqueeze(1).broadcast_to([NS, NS, HQ]),
                                 ID[0:NS, 0:NS].unsqueeze(2).broadcast_to([NS, NS, HQ]), ALU.mult), "smp_pte", 1)
            dve.wait_ge(sem["smp_done"], 3)
            done(v.tensor_copy(OS[:, :, :], ps[:, 7, 0:64].rearrange("p (a b) -> p a b", b=HQ)), "os_ready", 1)
            dve.wait_ge(sem["smp_done"], 4)
            for kv in range(HKV):
                for s in range(2):
                    src = ps[64 * s:64 * s + 64, 2 + kv, 0:32].rearrange("p (b j s) -> p s j b", j=2, s=2)[:, s]
                    ins = v.tensor_copy(OA[64 * s:64 * s + 64, 2 * kv:2 * kv + 2, NP:T], src)
                    if kv and s:
                        done(ins, "smp_oe", 1)
                    else:
                        chain(ins)

            for hp in range(4):
                pass
            dve.wait_ge(sem["bon_evac"], 4)
            chain(v.tensor_tensor(BON, BON, vv, ALU.mult))
            M2 = cst[:, K_M2:K_M2 + P].unsqueeze(1).broadcast_to([P, 8, P])
            for n in range(2):
                for q, (M, name) in enumerate(((NR, "nr_ready"), (KR, "kr_ready"))):
                    dve.wait_ge(sem["ab_done"], 2 * n + q + 1)
                    src = ps[:, 4 + 2 * q:6 + 2 * q, :].rearrange("p s (h c) -> p s h c", c=P)
                    done(v.tensor_tensor(M[:, 8 * n:8 * n + 8, :].rearrange("p (h s) c -> p s h c", s=2), src,
                                         M2.rearrange("p (h s) c -> p s h c", s=2), ALU.mult), name, n + 1)
            Ib = II[:, 0:CH].unsqueeze(1).broadcast_to([P, 8, CH])

            def bank(i):
                return ps[:, i, :].rearrange("p (a b) -> p a b", b=CH)

            dve.wait_ge(sem["row_evac"], 8)
            for n in range(2):
                hs = slice(8 * n, 8 * n + 8)
                dve.wait_ge(sem["nm_ready"], 1)
                chain(v.tensor_tensor(XX[:, hs, :], NM[0][:, hs, :], Ib, ALU.add))
                dve.wait_ge(sem["y_done"], n + 1)
                done(v.tensor_tensor(X[:, hs, :], bank(4 * n), Ib, ALU.add), "x_ready", n + 1)
            for i in range(1, len(LEVELS)):
                for n in range(2):
                    hs = slice(8 * n, 8 * n + 8)
                    dve.wait_ge(sem["dx_done"], 2 * (i - 1) + n + 1)
                    if i < len(LEVELS) - 1:
                        chain(v.tensor_tensor(X[:, hs, :], bank(4 * n + 1), X[:, hs, :], ALU.add))
                    done(v.tensor_tensor(XX[:, hs, :], bank(4 * n + 2), XX[:, hs, :], ALU.add), "x_ready", 2 * i + n + 1)

            def chunks(b):
                return ps[:, b, :].rearrange("p (h c k) -> p h c k", c=2, k=CH)

            dve.wait_ge(sem["carry_done"], 1)
            for q in range(2):
                R_ = ZR[:, :, q::2, 1, :]
                done(v.tensor_tensor(R_, chunks(q), R_, ALU.add), "dr_ready", q + 1)
            dve.wait_ge(sem["carry_done"], 2)
            for q in range(2):
                done(v.tensor_tensor(MC[:, :, q::2, :], chunks(4 + q), II[:, 0:CH].unsqueeze(1).broadcast_to([P, 8, CH]).rearrange(
                    "p (a b) c -> p a b c", b=2), ALU.add), "mc_ready", q + 1)
            dve.wait_ge(sem["n0_evac"], 2)
            for c in range(NCHUNK):
                G = G4[:, c, :, :]
                if c:
                    dve.wait_ge(sem["gm_done"], c)
                    chain(v.tensor_tensor(G, ps[:, 7, 0:4 * CH].rearrange("p (a b) -> p a b", b=CH), N0[:, :, c, :], ALU.add))
                src = G if c else N0[:, :, 0, :]
                done(v.tensor_tensor(G, src, pcol[:, :, c:c + 1].broadcast_to([P, 4, CH]), ALU.mult), "g_ready", c + 1)
            dve.wait_ge(sem["o_done"], NCHUNK)
            OTc = OT[:, :, 0:NP].rearrange("p h (c t) -> p h c t", t=CH)
            for q in range(2):
                chain(v.tensor_copy(OTc[:, :, q::2, :], chunks(4 + q)))
            for c in range(1, NCHUNK):
                src = ps[:, 6 if c < 3 else 3, (c - 1) % 2 * 256:(c - 1) % 2 * 256 + 256].rearrange("p (h k) -> p h k", k=CH)
                ins = v.tensor_tensor(OTc[:, :, c, :], src, OTc[:, :, c, :], ALU.add)
                if c == NCHUNK - 1:
                    done(ins, "ot_ready", 1)
                else:
                    chain(ins)
            dve.wait_ge(sem["ld_s0"], 16 * HQ)
            sa, so = st[:, 0:32], st[:, 32:64]
            for q in range(5):
                dve.wait_ge(sem["ex_used"], q + 1)
                B = ps[:, 4:8, :].rearrange("p a b -> p (a b)").rearrange("p (a b) -> p a b", b=CH)
                if q == 0:
                    chain(v.tensor_tensor(T1, B, S0, ALU.mult))
                    done(v.tensor_reduce(sa, T1, AX.X, ALU.add), "smp_step", 1)
                elif q == 1:
                    done(v.tensor_tensor(S0, B, S0, ALU.mult), "smp_step", 2)
                elif q in (2, 3):
                    w = sa if q == 2 else SMP[:, 5, :, :].rearrange("p a b -> p (a b)")
                    chain(v.tensor_tensor(T1, B, w.unsqueeze(2).broadcast_to([P, 32, CH]), ALU.mult))
                    done(v.tensor_tensor(S0, S0, T1, ALU.add), "smp_step", q + 1)
                else:
                    chain(v.tensor_tensor(T1, B, S0, ALU.mult))
                    chain(v.tensor_reduce(so, T1, AX.X, ALU.add))
                    done(v.tensor_copy(OT[:, :, NP:T], so.rearrange("p (a b) -> p a b", b=NS)), "smp_step", 5)
            dve.wait_ge(sem["gn_evac"], 4)
            chain(v.tensor_tensor(OT, OT, TMn, ALU.subtract))
            done(v.tensor_tensor(OSQ, OT, OT, ALU.mult), "gnsq_ready", 1)
            dve.wait_ge(sem["gn_evac"], 8)
            chain(v.reciprocal(TMn, TMn))
            chain(v.tensor_tensor(OT, OT, TMn, ALU.mult))
            for hp in range(4):
                chain(v.tensor_scalar(OT[:, hp, :], OT[:, hp, :], par("rw_gn_w", hp), par("rw_gn_b", hp), ALU.mult, ALU.add))
            chain(v.tensor_tensor(OT, OT, BON, ALU.add))
            done(v.tensor_tensor(OT, OT, GG, ALU.mult), "ob_ready", 1)
            for k in range(KD):
                dve.wait_ge(sem["pab_done"], 2 * k + 1)
                done(v.tensor_tensor(HT[:, k, :], ps[:, 2 * (k % 2), 0:T], SGv[:, k, :], ALU.mult), "pab_evac", 2 * k + 1)
                dve.wait_ge(sem["pab_done"], 2 * k + 2)
                done(v.tensor_tensor(SGv[:, 8 + k, :], ps[:, 2 * (k % 2) + 1, 0:T], SGv[:, 8 + k, :], ALU.mult), "pab_evac", 2 * k + 2)
                v.tensor_tensor(HT[:, k, :], HT[:, k, :], SGv[:, 8 + k, :], ALU.add).then_inc(sem["m_ready"], 1)
            out, bias = add_bias(16, 48)
            dve.wait_ge(sem["mod_evac"], 12)
            chain(v.tensor_tensor(out, out, bias, ALU.add))

            def residual(k, src, gate):
                return (v.scalar_tensor_tensor(out=XT[:, k, 0:NP], in0=src[:, 0:NP], scalar=modT[:, gate + k, 0:1],
                                               in1=XT[:, k, 0:NP], op0=ALU.mult, op1=ALU.add),)

            for k in range(KD):
                dve.wait_ge(sem["wo_done"], k + 1)
                src = ps[:, 4 + k % 4, :]
                chain(v.tensor_tensor(A1[:, k, 0:NS], src[:, NP:T], modT[:, 16 + k, 1:9], ALU.mult))
                v.scalar_tensor_tensor(out=XT[:, k, 0:NP], in0=src[:, 0:NP], scalar=modT[:, 16 + k, 0:1],
                                       in1=XT[:, k, 0:NP], op0=ALU.mult, op1=ALU.add).then_inc(sem["x1_ready"], 1)
                done(v.tensor_tensor(XT[:, k, NP:T], XT[:, k, NP:T], A1[:, k, 0:NS], ALU.add), "x1_ready", 2 * k + 2)
            rms(2)
            done(modulate(24, 32, "norm2"), "h2_ready", 1)

            dve.wait_ge(sem["ld_r"], 48)
            chain(v.memset(POSM, -1.0))
            chain(v.memset(GATE, 0.0))
            v.memset(GT, 0.0).then_inc(sem["gt_zero"], 1)
            IE = cst[:, K_IE:K_IE + NE]
            dve.wait_ge(sem["st_w"], 32)
            dve.wait_ge(sem["lg_done"], 3)
            for n, (_, nt) in enumerate(TILES):
                chain(v.tensor_tensor(LG[0:nt, n, :], ps[0:nt, 4, n * NE:n * NE + NE], brt[0:nt, :], ALU.add))
                chain(v.max(mx8[0:nt, n, :], LG[0:nt, n, :]))
                done(v.tensor_scalar(st[0:nt, 70 + n:71 + n], mx8[0:nt, n, 0:1], -1.0, None, ALU.mult), "top_ready", n + 1)
                chain(v.max_index(ix8[0:nt, n, :], mx8[0:nt, n, :], LG[0:nt, n, :]))
                chain(v.tensor_copy(ixf[0:nt, n, :], ix8[0:nt, n, :]))
                chain(v.tensor_scalar(MSK[0:nt, n, :], IE[0:nt, :], ixf[0:nt, n, 0:1], None, ALU.is_equal))
                for j in range(1, 4):
                    ins = v.scalar_tensor_tensor(out=MSK[0:nt, n, :], in0=IE[0:nt, :], scalar=ixf[0:nt, n, j:j + 1], in1=MSK[0:nt, n, :],
                                                 op0=ALU.is_equal, op1=ALU.add)
                    if j == 3:
                        done(ins, "msk_ready", n + 1)
                    else:
                        chain(ins)
            for n, (_, nt) in enumerate(TILES):
                dve.wait_ge(sem["top_exp"], n + 1)
                g4 = st[0:nt, 56 + 4 * n:60 + 4 * n]
                chain(v.reciprocal(st[0:nt, 73 + n:74 + n], st[0:nt, 76 + n:77 + n]))
                chain(v.tensor_scalar(g4, g4, st[0:nt, 73 + n:74 + n], None, ALU.mult))
                for j in range(4):
                    out = GTE[0:nt, n, :] if j == 0 else TMP32[0:nt, :]
                    chain(v.tensor_scalar(out, IE[0:nt, :], ixf[0:nt, n, j:j + 1], g4[:, j:j + 1], ALU.is_equal, ALU.mult))
                    if j:
                        chain(v.tensor_tensor(GTE[0:nt, n, :], GTE[0:nt, n, :], TMP32[0:nt, :], ALU.add))
            dve.wait_ge(sem["pos_done"], 1)
            for n, (_, nt) in enumerate(TILES):
                chain(v.scalar_tensor_tensor(out=TMP32[0:nt, :], in0=ps[0:nt, 5, n * NE:n * NE + NE], scalar=1.0, in1=MSK[0:nt, n, :],
                                             op0=ALU.add, op1=ALU.mult))
                for q in range(MAXR):
                    chain(v.tensor_scalar(POSM[0:nt, n, q * NE:q * NE + NE], TMP32[0:nt, :], -1.0 - q * C, None, ALU.add))
                    chain(v.tensor_copy(GATE[0:nt, n, q * NE:q * NE + NE], GTE[0:nt, n, :]))
            chain(v.tensor_reduce(st[:, 80:81], ps[:, 5, 96:96 + NE], AX.X, ALU.max))
            chain(v.memset(st[:, 81:82], 1.0))
            for q in range(1, MAXR):
                chain(v.scalar_tensor_tensor(out=st[:, 81:82], in0=st[:, 80:81], scalar=float(q * C), in1=st[:, 81:82],
                                             op0=ALU.is_gt, op1=ALU.add))
            done(v.tensor_copy(rounds_i[:, :], st[:, 81:82]), "rounds_ready", 1)
            dve.sem_inc(sem["pos_evac"], 1)
            IO = cst[:, K_IO:K_IO + C]
            IO2 = cst[:, K_IO:K_IO + 2 * C]

            def slots(col):
                for n in range(3):
                    v.tensor_scalar(OH[:, n, :], IO, POSM[:, n, col], None, ALU.is_equal)
                for n, (_, nt) in enumerate(TILES):
                    last = v.tensor_scalar(OG[0:nt, n, :], IO2[0:nt, :], POSM[0:nt, n, col], GATE[0:nt, n, col], ALU.is_equal, ALU.mult)
                last.then_inc(sem["oh_ready"], 1)

            slots(slice(0, 1))
            dve.wait_ge(sem["gT_done"], 1)
            v.tensor_copy(gT[0:NE, :], ps[0:NE, 4, 0:T]).then_inc(sem["gT_ready"], 1)
            for k in range(KD):
                dve.wait_ge(sem["comb_done"], k + 1)
                v.tensor_copy(YA[:, k, :], ps[:, 6 + k % 2, 0:T]).then_inc(sem["comb_used"], 1)

            rounds = dve.value_load(rounds_i[0:1, 0:1], min_val=1, max_val=MAXR)
            links_before, LINKS = chain.count, 8
            with dve.Fori(0, rounds) as r_:
                with dve.Fori(0, NE) as e:
                    i = r_ * NE + e
                    chain.base, chain.count = i * LINKS + links_before, 0
                    dve.wait_ge(sem["gt_done"], i + 1)
                    slots(bass.ds(i + 1, 1))
                    for hh in range(2):
                        u = ps[:, 2 + hh, :].rearrange("p (f l c) -> p l f c", l=2, f=4)
                        dve.wait_ge(sem["ut_done"], 2 * i + hh + 1)
                        chain(v.tensor_tensor(UG, u[:, 0], b1T[:, bass.ds(e * 16 + 4 * hh, 4)].unsqueeze(2).broadcast_to([P, 4, C]), ALU.add))
                        v.tensor_scalar(UG, UG, 7.0, None, ALU.min).then_inc(sem["ug_ready"], 1)
                        chain(v.tensor_tensor(UL, u[:, 1], b1T[:, bass.ds(e * 16 + 8 + 4 * hh, 4)].unsqueeze(2).broadcast_to([P, 4, C]), ALU.add))
                        chain(v.tensor_scalar(UL, UL, 7.0, -7.0, ALU.min, ALU.max))
                        dve.wait_ge(sem["ug_ready"], 2 * i + hh + 1)
                        chain(v.scalar_tensor_tensor(out=UL, in0=UL, scalar=1.0, in1=UG, op0=ALU.add, op1=ALU.mult))
                        dve.wait_ge(sem["us_ready"], 2 * i + hh + 1)
                        v.tensor_tensor(AC[:, 4 * hh:4 * hh + 4, :], UL, US_, ALU.mult).then_inc(sem["ac_ready"], 1)
                        dve.wait_ge(sem["ac_ready"], 2 * i + hh + 1)
                    for k in range(KD):
                        dve.wait_ge(sem["comb_done"], 8 * i + 9 + k)
                        dve.wait_ge(sem["comb_used"], 8 * i + 1 + k)
                        v.tensor_tensor(YA[:, k, :], ps[:, 6 + k % 2, 0:T], YA[:, k, :], ALU.add).then_inc(sem["comb_used"], 1)
            dve.wait_ge(sem["comb_used"], rounds * (NE * KD) + KD)
            chain.base, chain.count = rounds * (NE * LINKS) + links_before, 0
            chain(v.tensor_tensor(YA[:, :, NP:T], YA[:, :, NP:T], modT[:, 40:48, 1:9], ALU.mult))
            chain(v.tensor_tensor(XT[:, :, NP:T], XT[:, :, NP:T], YA[:, :, NP:T], ALU.add))
            for k in range(KD):
                last = v.scalar_tensor_tensor(out=XT[:, k, 0:NP], in0=YA[:, k, 0:NP], scalar=modT[:, 40 + k, 0:1],
                                              in1=XT[:, k, 0:NP], op0=ALU.mult, op1=ALU.add)
                last.then_inc(sem["x2_ready"], 1)


def _io(nc, inputs):
    def a(name):
        return np.ascontiguousarray(inputs[name])

    lay = {"cst": constants()}
    lay["x_prompt"] = a("x_prompt").reshape(NP, D)
    lay["x_sample"] = a("x_sample").reshape(NS, D)
    lay["c_prompt"] = a("c_prompt").reshape(1, D)
    lay["c_sample"] = a("c_sample").reshape(NS, D)
    lay["cache_k"] = a("cache_k").reshape(NS, WINDOW, P)
    lay["cache_v"] = a("cache_v").reshape(NS, WINDOW, P)
    lay["state_shift"] = a("state_shift").reshape(NS, RW)
    lay["state_wkv"] = a("state_wkv").reshape(NS, 4, 2, 64, 64)
    lay["t5_table"] = a("t5_table")
    lay["sinks"] = a("sinks").reshape(1, HQ)
    for name, rows in PARAMS[:-2]:
        lay[name] = a(name).reshape(rows, P)
    for name in ("q_norm", "k_norm"):
        lay[name] = a(name).reshape(1, HD)
    for name in ("w_mod", "w_in", "w_pa", "w_pb", "w_o", "w_router", "rw_w_w2", "rw_w_a2", "rw_w_g2", "w1", "w2", "b2", "b_router"):
        x = a(name)
        lay[name] = x.reshape(x.shape[1:]) if name != "b_router" else x.reshape(1, NE)
    lay["b1"] = a("b1").reshape(NE * 16, P)
    return lay


OUTS = [("y_prompt", (NP, D), (1, NP, D)), ("y_sample", (NS, D), (NS, 1, D)),
        ("k_prompt", (WINDOW, P), (1, 1, WINDOW, HKV, HD)), ("v_prompt", (WINDOW, P), (1, 1, WINDOW, HKV, HD)),
        ("shift_prompt", (1, RW), (1, 1, RW)), ("wkv_prompt", (8, 64, 64), (1, 1, 8, 64, 64)),
        ("k_sample", (NS, WINDOW, P), (1, NS, WINDOW, HKV, HD)), ("v_sample", (NS, WINDOW, P), (1, NS, WINDOW, HKV, HD)),
        ("shift_sample", (NS, RW), (1, NS, RW)), ("wkv_sample", (NS, 4, 2, 64, 64), (1, NS, 8, 64, 64))]


def kernel(**inputs):
    import concourse.bacc as bacc
    from concourse.bass_utils import run_bass_kernel_spmd as run

    nc = bacc.Bacc("TRN2", target_bir_lowering=False, num_devices=1)
    io, arrays = {}, {}
    for name, x in _io(nc, inputs).items():
        arrays["in_" + name] = x
        io[name] = nc.dram_tensor("in_" + name, x.shape, mybir.dt.from_np(x.dtype), kind="ExternalInput").ap()
    for name, shape, _ in OUTS:
        io[name] = nc.dram_tensor("out_" + name, shape, F32, kind="ExternalOutput").ap()
    build(nc, io)
    r = run(nc, [arrays], core_ids=[0])
    return tuple(r.results[0]["out_" + name].reshape(shape) for name, _, shape in OUTS)
```

```python
from contextlib import ExitStack

import numpy as np
import concourse.bass as bass
from concourse import mybir
from concourse.alu_op_type import AluOpType as ALU

F32 = mybir.dt.float32
I32 = mybir.dt.int32
U32 = mybir.dt.uint32
ACT = mybir.ActivationFunctionType
AX = mybir.AxisListType

P = 128
D = 1024
KD = D // P
NP, NS = 256, 8
T = NP + NS
TILES = [(0, 128), (128, 128), (256, NS)]
HQ, HKV, HD, GQA = 8, 2, 64, 4
WINDOW = 128
KEYS = WINDOW + 1
RW = 1792
NCH = 20
CQ, CK, CV, CR = 0, 4, 5, 6
NE, FE, C = 32, 1024, 64
NF = FE // P
MAXR = -(-T // C)
CH = 64
NCHUNK = NP // CH
RZ_SLOT = 2
SCALE = HD ** -0.5
E_HALF = float(np.exp(-0.5))
NEG = -1e30
LEVELS = [1, 2, 4, 8, 16, 32]

K_ID, K_II, K_BO, K_ONE, K_US, K_REV, K_M2, K_LV, K_IO, K_IE, K_OB = (
    0, 128, 256, 384, 512, 640, 768, 896, 1280, 1408, 1440)
K_COLS = K_OB + KEYS

PARAMS = [("b_mod", 48), ("norm1", 8), ("norm2", 8), ("rw_mu", 14), ("rw_w0", 4), ("rw_a0", 4),
          ("rw_k_k", 4), ("rw_k_a", 4), ("rw_r_k", 4), ("rw_gn_w", 4), ("rw_gn_b", 4),
          ("q_norm", 1), ("k_norm", 1)]
PCOL, _n = {}, 0
for _name, _rows in PARAMS:
    PCOL[_name] = _n
    _n += _rows
NPAR = _n


def constants():
    c = np.zeros((P, K_COLS), np.float32)
    p = np.arange(P)[:, None]
    m = np.arange(P)[None, :]
    c[:, K_ID:K_ID + P] = p == m
    c[:, K_II:K_II + P] = p % 64 == m % 64
    c[:, K_BO:K_BO + P] = p // 64 == m // 64
    c[:, K_ONE:K_ONE + P] = 1.0
    c[:, K_US:K_US + P] = p < m
    c[:, K_REV:K_REV + P] = p + m == P - 1
    s, t = p % 64, np.arange(64)[None, :]
    c[:, K_M2:K_M2 + 64] = t > s
    c[:, K_M2 + 64:K_M2 + 128] = t >= s
    for i, b in enumerate(LEVELS):
        c[:, K_LV + 64 * i:K_LV + 64 * i + 64] = (t // b % 2 == 1) & (s // b == t // b - 1)
    c[:, K_IO:K_IO + 2 * C] = np.arange(2 * C) % C
    c[:, K_IE:K_IE + NE] = np.arange(NE)
    dist = WINDOW - np.arange(KEYS)
    half = NE // 2
    far = half + (np.log(np.maximum(dist, 1).astype(np.float32) / half) / np.log(128 / half) * half).astype(np.int32)
    bucket = np.where(dist < half, dist, np.minimum(far, NE - 1))
    c[:NE, K_OB:K_OB + KEYS] = np.arange(NE)[:, None] == bucket[None, :]
    return c


class Sems(dict):

    def __init__(self, nc, ctx):
        super().__init__()
        self.nc, self.ctx = nc, ctx

    def __missing__(self, name):
        self[name] = self.ctx.enter_context(self.nc.semaphore(name))
        return self[name]


class Chain:

    def __init__(self, engine, sem):
        self.engine, self.sem, self.count, self.base = engine, sem, 0, 0

    def __call__(self, instruction):
        self.count += 1
        instruction.then_inc(self.sem, 1)
        self.engine.wait_ge(self.sem, self.base + self.count)


def build(nc, io):
    with ExitStack() as ctx:
        sem = Sems(nc, ctx)

        def sb(name, shape, dt=F32):
            return ctx.enter_context(nc.sbuf_tensor(name, shape, dt))

        ring = sb("ring", [P, 6, 8, 512])
        RZ = ring[:, RZ_SLOT:6, :, :].rearrange("p a b c -> p (a b c)")
        cst = sb("cst", [P, K_COLS])
        PT = sb("PT", [P, NCH * T])
        XM = sb("XM", [P, 14 * T])
        SG = sb("SG", [P, 16 * T])
        XT = sb("XT", [P, KD, T])
        HT = sb("HT", [P, KD, T])
        SQ = sb("SQ", [P, KD, T])
        XR = sb("XR", [P, 3, D])
        BM = sb("BM", [P, HQ * 2 * P])
        modT = sb("modT", [P, 48, 9])
        PC = sb("PC", [P, NPAR])
        b1T = sb("b1T", [P, NE * 16])
        cT = sb("cT", [P, KD, 32])
        A1 = sb("A1", [P, KD, 9])
        RS = sb("RS", [P, T])
        SS = sb("SS", [P, 14, NS])
        SMP = sb("SMP", [P, 6, 4, NS])
        brow = sb("brow", [HQ, KEYS])
        sinkb = sb("sinkb", [P, HQ])
        sinkc = sb("sinkc", [HQ, 1])
        tab = sb("tab", [NE, HQ])
        brc = sb("brc", [NE, 1])
        st = sb("st", [P, 82])
        pcol = sb("pcol", [P, 4, NCHUNK])

        def view(t, off, *shape):
            n = int(np.prod(shape))
            v = t[:, off:off + n]
            if len(shape) == 2:
                return v.rearrange("p (a b) -> p a b", b=shape[1])
            if len(shape) == 3:
                return v.rearrange("p (a b c) -> p a b c", b=shape[1], c=shape[2])
            if len(shape) == 4:
                return v.rearrange("p (a b c d) -> p a b c d", b=shape[1], c=shape[2], d=shape[3])
            return v

        SQf = SQ[:, :, :].rearrange("p a b -> p (a b)")
        XRf = XR[:, :, :].rearrange("p a b -> p (a b)")
        PTv = PT[:, :].rearrange("p (a b) -> p a b", b=T)
        XMv = XM[:, :].rearrange("p (a b) -> p a b", b=T)
        SGv = SG[:, :].rearrange("p (a b) -> p a b", b=T)
        LD, CS, eP, eN, eM = (view(RZ, 0, 4, T), view(RZ, 1056, 4, NP), view(RZ, 2080, 4, NP),
                              view(RZ, 3104, 4, NP), view(RZ, 4128, 4, NP))
        NK, Aa, TM = view(RZ, 5152, 4, T), view(RZ, 6208, 4, T), view(RZ, 7264, 4, T)
        Bh, Kh = view(RZ, 8320, 4, NP), view(RZ, 9344, 4, NP)
        vcr, SsT, kd, vr = (view(RZ, 10368, NS, P), view(RZ, 11392, NS, KEYS), view(RZ, 12424, 2, T),
                            view(RZ, 12952, 3, P))
        LWw, LWg = view(RZ, 13336, 512), view(RZ, 13848, 512)
        ssr = view(RZ, 14360, RW)
        GG, ZR = view(PT, 6 * T, 4, T), view(PT, 10 * T, 4, NCHUNK, 2, CH)
        BON = SQ[:, 0:4, :]
        NR, KR = view(RZ, 0, 16, P), view(RZ, 2048, 16, P)
        ZU, Br, Kr = view(RZ, 4096, 16, P), view(RZ, 6144, 16, CH), view(RZ, 7168, 16, CH)
        Vr = view(SQf, 1056, 16, CH)
        X, XX = view(XM, 0, 16, CH), view(XM, 1024, 16, CH)
        Y = view(RZ, 8320, 16, CH)
        NM = [view(RZ, 9344, 16, CH), view(RZ, 13336, 16, CH)]
        XZW = view(RZ, 8320, 16, P)
        MC, G4 = view(RZ, 4096, 4, NCHUNK, CH), view(RZ, 5120, NCHUNK, 4, CH)
        N0 = view(XM, 0, 4, NCHUNK, CH)
        OT = view(XM, 1024, 4, T)
        TMn, OSQ = SQ[:, 4:8, :], view(XM, 2112, 4, T)
        Pm, pT = view(RZ, 1056, 4, 2 * P), view(RZ, 0, 4, 2, P)
        kcT, kcr = view(SG, 2048, NS, KEYS), view(SG, 3080, NS, P)
        OA = view(PT, 0, 4, T)
        HK = view(SG, 0, HQ, 2 * P)
        prow, b1r, ext = view(SG, 2048, P), view(SG, 2176, 4, P), view(SG, 2688, 384)
        crow, csig = view(BM, 0, D), view(BM, 1024, D)
        S0, T1, EX = view(XRf, 0, 32, CH), view(RZ, 0, 32, CH), view(RZ, 2048, 32, CH)
        OH, OG = view(PT, 0, 3, C), view(PT, 192, 3, 2 * C)
        POSM, GATE = view(PT, 576, 3, NE * MAXR + 1), view(PT, 1059, 3, NE * MAXR + 1)
        XG, GT = view(PT, 1542, 4, 2, C), view(PT, 2054, 2, T)
        UG, UL, US_, AC = (view(PT, 2582, 4, C), view(PT, 2838, 4, C), view(PT, 3094, 4, C),
                           view(PT, 3350, NF, C))
        YS, XGR, UR = view(PT, 3862, 512), view(PT, 4374, 512), view(SG, 0, 2, 512)
        XGf = view(PT, 1542, 512)
        YA = SQ
        LG, MSK, GTE, RNK = (view(XM, 0, 3, NE), view(XM, 96, 3, NE), view(XM, 192, 3, NE), view(XM, 288, 3, NE))
        gT, b2r = view(XM, 1408, T), view(XM, 2112, D)
        wr, LGT = view(XM, 3168, KD, NE), view(XM, 384, T)
        fin = view(RZ, 0, 3, D)
        mx8, ix8, ixf = sb("mx8", [P, 3, 8]), sb("ix8", [P, 3, 8], U32), sb("ixf", [P, 3, 8])
        rounds_i = sb("rounds_i", [P, 1], I32)
        Qs = sb("Qs", [P, HQ, NS])
        pTs, PSf, OS = view(XRf, 2048, NS, HQ), view(XRf, 2112, NS, HQ)[0:NS], view(XRf, 2176, NS, HQ)
        epsc = sb("epsc", [P, 3])
        qk_eps, gn_eps = epsc[:, 0:1], epsc[:, 1:2]
        kvr = view(XRf, 10 * T, 2, P)
        MR = view(XRf, 10 * T + 256, P)
        wps = view(XM, 0, 4, CH)

        ps = ctx.enter_context(nc.psum_tensor("ps", [P, 8, 512], F32))
        ID = cst[:, K_ID:K_ID + P]
        II = cst[:, K_II:K_II + P]
        BO = cst[:, K_BO:K_BO + P]
        ONE = cst[:, K_ONE:K_ONE + P]
        ext_d = nc.dram_tensor("bias_by_distance", [HQ, 384], F32, kind="Internal")

        def par(name, i=0):
            return PC[:, PCOL[name] + i:PCOL[name] + i + 1]

        win = io["w_in"].rearrange("(k p) n -> p k n", p=P)
        wmod = io["w_mod"].rearrange("(k p) n -> p k n", p=P)
        wo = io["w_o"].rearrange("(k p) n -> p k n", p=P)
        stream = [("mod", wmod, j) for j in range(4)]
        for j, m in zip(range(9), (4, 5, 6, 7, 8, 9, 10, 11, None)):
            stream += [("win", win, j)] + ([("mod", wmod, m)] if m else [])
        stream += [("pa", None, 0), ("wo", wo, 0), ("wo", wo, 1), ("pb", None, 0)]
        slots_of = [0, 1, 2, 3] + [g % 3 for g in range(4, 14)] + [0, 1, 0, 1, 5, 0, 1, 5, 3, 4, 0]
        assert len(slots_of) == len(stream)
        AFTER_RWKV = [g for g in range(14, len(stream)) if slots_of[g] >= RZ_SLOT]
        STREAM_AT = {(kind, j): g for g, (kind, _, j) in enumerate(stream)}

        def uses_before(slot, g=len(stream)):
            return slots_of[:g].count(slot)

        w1v = io["w1"].rearrange("e (k p) n -> e p k n", p=P)
        w2v = io["w2"].rearrange("e (k p) n -> e p k n", p=P)

        def expert_chunk(e, c):
            if c < 4:
                return w1v[e, :, 2 * c:2 * c + 2, :]
            return w2v[e, :, 4 * (c - 4):4 * (c - 4) + 4, :]

        def slot_tile(c):
            return ring[:, c, :, :].rearrange("p a b -> p (a b)").rearrange("p (k n) -> p k n", n=2 * FE if c < 4 else D)

        def slot_used(c, i):
            return (sem["w1_used"], 4 * i + c + 1) if c < 4 else (sem["y2_done"], 2 * i + c - 3)

        a_order = [("x", 8), ("mod0", 1), ("modT0", 1), ("mod1", 1), ("modT1", 1), ("mod2", 1), ("modT2", 1), ("mod3", 1), ("modT3", 1),
                   ("win0", 4), ("mod4", 1), ("win1", 4), ("modT4", 1), ("mod5", 1), ("win2", 4), ("modT5", 1), ("qk", 5),
                   ("mod6", 1), ("win3", 4), ("modT6", 1), ("mod7", 1), ("win4", 4), ("modT7", 1), ("kk", 4), ("mod8", 1),
                   ("decay", 4), ("rate", 4), ("gate", 4), ("modT8", 1),
                   ("win6a", 1), ("mod9", 1), ("win6b", 2), ("modT9", 1), ("win6", 1),
                   ("mod10", 1), ("win7", 4), ("modT10", 1), ("mod11", 1), ("win8", 4), ("modT11", 1)]

        def a_end(what):
            i = [name for name, _ in a_order].index(what)
            return sum(n for _, n in a_order[:i + 1])

        def chunk_used(g):
            kind, _, j = stream[g]
            if (kind, j) == ("win", 5):
                return sem["f_done"], 4
            if kind in ("mod", "win"):
                return sem["a_done"], a_end(f"{kind}{j}")
            if kind == "wo":
                return sem["wo_done"], KD
            return sem["pab_done"], KD if kind == "pa" else 2 * KD

        block = ctx.enter_context(nc.Block())

        @block.sync
        def _(sp):
            sp.dma_start(cst[:, :], io["cst"]).then_inc(sem["ld_cst"], 16)
            sp.dma_start(crow[0:1, :], io["c_prompt"]).then_inc(sem["ld_c"], 16)
            sp.dma_start(crow[1:9, :], io["c_sample"]).then_inc(sem["ld_c"], 16)
            sp.dma_start(prow[0:NPAR, :], io["params"]).then_inc(sem["ld_par"], 16)
            for n, (t0, nt) in enumerate(TILES):
                src = io["x_prompt"][t0:t0 + nt, :] if n < 2 else io["x_sample"]
                sp.dma_start(XR[0:nt, n, :], src).then_inc(sem["ld_x"], 16)
            for g, (kind, src, j) in enumerate(stream):
                slot = slots_of[g]
                if g == AFTER_RWKV[0]:
                    sp.wait_ge(sem["wps_evac"], 1)
                    sp.wait_ge(sem["sh_out"], 32)
                    sp.wait_ge(sem["st_kv"], 64)
                if uses_before(slot, g):
                    last = max(i for i in range(g) if slots_of[i] == slot)
                    sp.wait_ge(*chunk_used(last))
                if kind in ("pa", "pb"):
                    dst = ring[:, slot, :, :].rearrange("p k n -> p (k n)").rearrange("p (k n) -> p k n", n=D)
                    sp.dma_start(dst, io["w_" + kind].rearrange("(k p) n -> p k n", p=P)).then_inc(sem[f"ring{slot}"], 16)
                else:
                    sp.dma_start(ring[:, slot, :, :], src[:, :, j * 512:j * 512 + 512]).then_inc(sem[f"ring{slot}"], 16)
            sp.wait_ge(sem["smp_step"], 5)
            for c in (2, 1, 5, 0, 3, 4):
                if uses_before(c):
                    last = max(i for i in range(len(stream)) if slots_of[i] == c)
                    sp.wait_ge(*chunk_used(last))
                sp.dma_start(slot_tile(c), expert_chunk(0, c)).then_inc(sem[f"ring{c}"], 16)
            with sp.Fori(1, NE) as e:
                for c in range(6):
                    sp.wait_ge(*slot_used(c, e - 1))
                    sp.dma_start(slot_tile(c), expert_chunk(e, c)).then_inc(sem[f"ring{c}"], 16)
            sp.wait_ge(sem["rounds_ready"], 1)
            rounds = sp.value_load(rounds_i[0:1, 0:1], min_val=1, max_val=MAXR)
            with sp.If(rounds > 1):
                with sp.Fori(1, rounds) as r:
                    with sp.Fori(0, NE) as e:
                        for c in range(6):
                            sp.wait_ge(*slot_used(c, r * NE + e - 1))
                            sp.dma_start(slot_tile(c), expert_chunk(e, c)).then_inc(sem[f"ring{c}"], 16)
            for n, (t0, nt) in enumerate(TILES):
                sp.wait_ge(sem["fin_evac"], n + 4)
                dst = io["y_prompt"][t0:t0 + nt, :] if n < 2 else io["y_sample"]
                sp.dma_start(dst, fin[0:nt, n, :]).then_inc(sem["y_out"], 16)
            sp.wait_ge(sem["y_out"], 48)

        k_mod, r, vv = XMv[:, 4:8, :], XMv[:, 0:4, :], XMv[:, 8:12, :]

        def state_rows(h):
            return S0[64 * (h % 2):64 * (h % 2) + 64, (h // 2) * NS:(h // 2) * NS + NS, :]

        @block.gpsimd
        def _(pool):
            chain = Chain(pool, sem["pool_chain"])
            pool.wait_ge(sem["brow_ready"], 1)
            chain(pool.memset(ext[0:HQ, :], NEG))
            chain(pool.tensor_copy(ext[0:HQ, 127:127 + KEYS], brow[:, 0:KEYS]))
            pool.dma_start(ext_d.ap(), ext[0:HQ, :]).then_inc(sem["ext_out"], 16)
            pool.wait_ge(sem["ext_out"], 16)
            band = bass.AP(ext_d, 0, [[1, P], [384, HQ], [1, 2 * P]])
            pool.dma_start(HK, band).then_inc(sem["ld_hk"], 16)
            pool.wait_ge(sem["sh_evac"], 4)
            pool.dma_start(io["shift_prompt"], ssr[0:1, :]).then_inc(sem["sh_out"], 16)
            pool.dma_start(io["shift_sample"], ssr[1:9, :]).then_inc(sem["sh_out"], 16)
            pool.wait_ge(sem["a_done"], a_end("gate"))
            pool.dma_start(wr, io["w_router"].rearrange("(k p) e -> p k e", p=P)).then_inc(sem["ld_r"], 16)
            pool.dma_start(brc[:, :], io["b_router"].rearrange("a b -> b a")).then_inc(sem["ld_r"], 16)
            pool.wait_ge(sem["kmod_ready"], 1)
            for hp in range(4):
                chain(pool.tensor_scalar(TM[:, hp, :], r[:, hp, :], par("rw_r_k", hp), None, ALU.mult))
            chain(pool.tensor_tensor(TM, TM, k_mod, ALU.mult))
            pool.wait_ge(sem["decays"], 4)
            pool.wait_ge(sem["sh_t"], 4)

            def by_chunk(x):
                return x[:, :, 0:NP].rearrange("p h (c t) -> p h c t", t=CH)

            chain(pool.tensor_tensor(ZR[:, :, :, 0, :], by_chunk(NK), by_chunk(eM), ALU.mult))
            chain(pool.tensor_tensor(ZR[:, :, :, 1, :], by_chunk(r), by_chunk(eP), ALU.mult))
            chain(pool.tensor_tensor(Bh, Aa[:, :, 0:NP], eN, ALU.mult))
            chain(pool.tensor_tensor(Kh, k_mod[:, :, 0:NP], eN, ALU.mult))
            chain(pool.tensor_copy(pcol[:, :, :], by_chunk(eP)[:, :, :, CH - 1]))
            for q, src in ((0, NK), (2, Aa), (3, k_mod), (4, r), (5, vv)):
                chain(pool.tensor_copy(SMP[:, q, :, :], src[:, :, NP:T]))
            pool.sem_inc(sem["zr_ready"], 1)

            pool.wait_ge(sem["qk_ready"], 1)
            for h in range(HQ):
                pool.dma_start(state_rows(h), io["state_wkv"][:, h // 2, h % 2].rearrange("b v k -> v b k")).then_inc(sem["ld_s0"], 16)
            pool.wait_ge(sem["kvrow_evac"], 1)
            pool.dma_start(io["k_prompt"], kvr[:, 0, :]).then_inc(sem["st_kv"], 16)
            pool.dma_start(io["v_prompt"], vr[:, 1, :]).then_inc(sem["st_kv"], 16)
            pool.dma_start(io["k_sample"][:, WINDOW - 1, :], kvr[0:NS, 1, :]).then_inc(sem["st_kv"], 16)
            pool.dma_start(io["v_sample"][:, WINDOW - 1, :], vr[0:NS, 2, :]).then_inc(sem["st_kv"], 16)
            for i in range(1, len(LEVELS)):
                pool.wait_ge(sem["nr_ready"], 2)
                pool.wait_ge(sem["kr_ready"], 2)
                if i >= 2:
                    pool.wait_ge(sem["y_done"], 2 * i - 2)
                    pool.wait_ge(sem["x_ready"], 2)
                mask = cst[:, K_LV + 64 * i:K_LV + 64 * i + 64].unsqueeze(1).broadcast_to([P, 16, CH])
                pool.tensor_tensor(NM[i % 2], NR[:, :, 0:CH], mask, ALU.mult).then_inc(sem["nm_ready"], 1)
            for q in range(5):
                pool.wait_ge(sem["o_done"], 4)
                if q:
                    pool.wait_ge(sem["ex_used"], q)
                pool.tensor_tensor(
                    EX, SMP[:, q, :, :].rearrange("p a b -> p (a b)").unsqueeze(2).broadcast_to([P, 32, CH]),
                    II[:, 0:CH].unsqueeze(1).broadcast_to([P, 32, CH]), ALU.mult).then_inc(sem["ex_ready"], 1)
            pool.wait_ge(sem["smp_step"], 5)
            for h in range(HQ):
                pool.dma_start(io["wkv_sample"][:, h // 2, h % 2].rearrange("b v k -> v b k"), state_rows(h)).then_inc(sem["st_s"], 16)
            pool.wait_ge(sem["gn_done"], 8)
            pool.dma_start(b2r[0:NE, :], io["b2"]).then_inc(sem["ld_r"], 16)
            pool.wait_ge(sem["sh_out"], 32)
            pool.wait_ge(sem["st_s"], 16 * HQ)
            pool.wait_ge(sem["st_kv"], 64)
            pool.memset(XR[:, 2, :], 0.0).then_inc(sem["xr_zero"], 1)

        @block.scalar
        def _(act):
            chain = Chain(act, sem["act_chain"])
            dma = act.dma_start
            dma(tab[:, :], io["t5_table"]).then_inc(sem["ld_tab"], 16)
            dma(b1r, io["b1"].rearrange("(a p) f -> p a f", p=P)).then_inc(sem["ld_b1"], 16)
            dma(ssr[0:NS, :], io["state_shift"]).then_inc(sem["ld_ss"], 16)
            dma(LWw[0:64, :], io["rw_w_w2"]).then_inc(sem["ld_lw"], 16)
            dma(LWw[64:128, :], io["rw_w_a2"]).then_inc(sem["ld_lw"], 16)
            dma(LWg, io["rw_w_g2"]).then_inc(sem["ld_lw"], 16)
            dma(sinkb[:, :], io["sinks"].partition_broadcast(P).rearrange("p a b -> p (a b)")).then_inc(sem["ld_sink"], 16)
            dma(sinkc[:, :], io["sinks"].rearrange("a b -> b a")).then_inc(sem["ld_sink"], 16)
            dma(kcr, io["cache_k"].rearrange("b j n -> j b n")).then_inc(sem["ld_kc"], 16)
            dma(vcr, io["cache_v"].rearrange("b j n -> j b n")).then_inc(sem["ld_vc"], 16)
            dma(io["k_sample"][:, 0:WINDOW - 1, :], io["cache_k"][:, 1:WINDOW, :]).then_inc(sem["st_k"], 16)
            dma(io["v_sample"][:, 0:WINDOW - 1, :], io["cache_v"][:, 1:WINDOW, :]).then_inc(sem["st_k"], 16)

            act.wait_ge(sem["ld_c"], 32)
            act.activation(csig[0:9, :], crow[0:9, :], ACT.Sigmoid).then_inc(sem["csig_ready"], 1)

            a = [0]

            def group():
                g = a[0]
                a[0] += 1
                act.wait_ge(sem["a_done"], g + 1)
                return ps[:, g % 4, 0:T]

            for k in range(KD):
                chain(act.copy(XT[:, k, :], group()))
                act.activation(SQ[:, k, :], XT[:, k, :], ACT.Square).then_inc(sem["a_evac"], 1)
            act.wait_ge(sem["ms_ready"], 1)
            act.activation(RS[:, :], RS[:, :], ACT.Sqrt).then_inc(sem["sqrt_done"], 1)

            def project(chunks, parts=range(4)):
                for j in chunks:
                    for s in parts:
                        cc = 4 * j + s
                        if cc < NCH:
                            act.copy(PTv[:, cc, :], group()).then_inc(sem["a_evac"], 1)
                        else:
                            act.activation(SGv[:, cc - NCH, :], group(), ACT.Sigmoid).then_inc(sem["a_evac"], 1)

            def mod_rows(j):
                act.copy(MR, group()[:, 0:P]).then_inc(sem["a_evac"], 1)

            def mod_columns(j):
                act.copy(modT[:, 4 * j:4 * j + 4, :],
                         group()[:, 0:P].rearrange("p (a b) -> p a b", b=32)[:, :, 0:9]).then_inc(sem["a_evac"], 1)

            for j in range(4):
                mod_rows(j)
                mod_columns(j)
            project([0])
            for j, m in ((1, 4), (2, 5)):
                mod_rows(m)
                project([j])
                mod_columns(m)
            for i in range(5):
                act.activation(XRf[:, (5 + i) * T:(6 + i) * T], group(), ACT.Sqrt,
                               bias=qk_eps, scale=1.0 / HD).then_inc(sem["a_evac"], 1)
            for j, m in ((3, 6), (4, 7)):
                mod_rows(m)
                project([j])
                mod_columns(m)
            for hp in range(4):
                act.activation(SQ[:, 4 + hp, :], group(), ACT.Sqrt).then_inc(sem["a_evac"], 1)
            mod_rows(8)
            for i in range(4):
                act.wait_ge(sem["sh_t"], i + 1)
                w = min(512, RW - 512 * i)
                act.copy(ssr[0:9, 512 * i:512 * i + w], ps[0:9, 6 + i % 2, 0:w]).then_inc(sem["sh_evac"], 1)
            act.wait_ge(sem["mixed"], 1)
            act.activation(XMv[0:64, 12, :], XMv[0:64, 12, :], ACT.Tanh).then_inc(sem["lora_in"], 1)
            act.activation(XMv[:, 13, :], XMv[:, 13, :], ACT.Sigmoid).then_inc(sem["lora_in"], 1)
            for hp in range(4):
                act.activation(LD[:, hp, :], group(), ACT.Sigmoid, bias=par("rw_w0", hp)).then_inc(sem["a_evac"], 1)
            for hp in range(4):
                act.activation(Aa[:, hp, :], group(), ACT.Sigmoid, bias=par("rw_a0", hp)).then_inc(sem["a_evac"], 1)
            act.wait_ge(sem["sh_t"], 4)
            for hp in range(4):
                act.copy(GG[:, hp, :], group()).then_inc(sem["a_evac"], 1)
            mod_columns(8)
            act.wait_ge(sem["cs_ready"], 1)
            act.activation(eP, CS, ACT.Exp).then_inc(sem["decays"], 1)
            act.activation(eN, CS, ACT.Exp, scale=-1.0).then_inc(sem["decays"], 1)
            act.wait_ge(sem["cs_ready"], 2)
            act.activation(eM, eM, ACT.Exp).then_inc(sem["decays"], 1)
            act.activation(SMP[:, 1, :, :], LD[:, :, NP:T], ACT.Exp).then_inc(sem["decays"], 1)

            act.wait_ge(sem["kvrow_done"], 2)
            act.copy(kd, ps[:, 0:2, 0:T])
            act.wait_ge(sem["kvrow_done"], 3)
            act.copy(vr[:, 0:2, :], ps[:, 2, 0:2 * P].rearrange("p (a b) -> p a b", b=P))
            act.copy(vr[0:NS, 2, :], ps[0:NS, 2, 2 * P:3 * P])
            act.copy(kvr[:, 0, :], ps[:, 3, 0:P])
            act.copy(kvr[0:NS, 1, :], ps[0:NS, 3, P:2 * P]).then_inc(sem["kvrow_evac"], 1)
            act.wait_ge(sem["qk_ready"], 1)
            act.wait_ge(sem["kc_done"], 1)
            act.wait_ge(sem["ext_out"], 16)
            act.copy(kcT[:, :, 0:P], ps[:, 4:6, :].rearrange("p a (b c) -> p (a b) c", c=P))
            act.copy(kcT[:, :, P], PTv[:, CK, NP:T]).then_inc(sem["kc_evac"], 1)
            for i in range(4):
                act.wait_ge(sem["bm_done"], i + 1)
                act.copy(BM[:, i * 512:i * 512 + 512], ps[:, [6, 7, 4, 5][i], :]).then_inc(sem["bm_evac"], 1)
            for g4 in range(4):
                J = P if g4 < 2 else 2 * P
                act.wait_ge(sem["att_max"], g4 + 1)
                for g in range(4):
                    act.activation(Pm[:, g, 0:J], Pm[:, g, 0:J], ACT.Exp, bias=st[:, 4 + g:5 + g],
                                   accum_out=st[:, 8 + g:9 + g]).then_inc(sem["att_exp"], 1)
                act.activation(st[:, 12:16], st[:, 12:16], ACT.Exp).then_inc(sem["att_exp"], 1)
                act.wait_ge(sem["f_done"], g4 + 1)
                act.activation(SGv[:, g4, :], ps[:, 7, 0:T], ACT.Sigmoid).then_inc(sem["f_evac"], 1)
                for g in range(4 * J // P // 4):
                    act.wait_ge(sem["att_pt"], (g4 if g4 < 2 else 2 * g4 - 2) + g + 1)
                    act.copy(pT[:, :, g, :], ps[:, 4 + g, :].rearrange("p (a b) -> p a b", b=P)).then_inc(sem["att_pte"], 1)
            project([6], range(0, 1))
            mod_rows(9)
            act.wait_ge(sem["smp_max"], 1)
            act.activation(SsT[0:HQ, :, :], SsT[0:HQ, :, :], ACT.Exp).then_inc(sem["smp_exp"], 1)
            act.activation(st[0:HQ, 48:56], st[0:HQ, 48:56], ACT.Exp).then_inc(sem["smp_exp"], 1)
            project([6], range(1, 3))
            mod_columns(9)

            for hp in range(4):
                act.wait_ge(sem["bon_done"], hp + 1)
                act.copy(BON[:, hp, :], ps[:, hp, 0:T]).then_inc(sem["bon_evac"], 1)
            for i in range(8):
                mat, n = i // 2, i % 2
                dst = [ZU[:, 8 * n:8 * n + 8, 0:CH], Br[:, 8 * n:8 * n + 8, :], Kr[:, 8 * n:8 * n + 8, :],
                       Vr[:, 8 * n:8 * n + 8, :]][mat]
                act.wait_ge(sem["row_done"], i + 1)
                act.copy(dst, ps[:, i % 4, :].rearrange("p (a b) -> p a b", b=CH)).then_inc(sem["row_evac"], 1)
            for i in range(1, len(LEVELS)):
                for n in range(2):
                    act.wait_ge(sem["y_done"], 2 * i + n + 1)
                    act.copy(Y[:, 8 * n:8 * n + 8, :], ps[:, 4 * n, :].rearrange("p (a b) -> p a b", b=CH)).then_inc(sem["y_evac"], 1)
            for n in range(2):
                act.wait_ge(sem["u0_done"], n + 1)
                act.copy(ZU[:, 8 * n:8 * n + 8, CH:P], ps[:, 3 + 4 * n, :].rearrange("p (a b) -> p a b", b=CH)).then_inc(sem["u0_evac"], 1)
            for n in range(2):
                act.wait_ge(sem["xzw_done"], n + 1)
                act.copy(XZW[:, 8 * n:8 * n + 8, :],
                         ps[:, 4 * n:4 * n + 2, :].rearrange("p a b -> p (a b)").rearrange("p (a b) -> p a b", b=P)).then_inc(sem["xzw_evac"], 1)
            act.wait_ge(sem["carry_done"], 3)
            for q in range(2):
                act.copy(N0[:, :, q::2, :], ps[:, 2 + q, :].rearrange("p (h c k) -> p h c k", c=2, k=CH)).then_inc(sem["n0_evac"], 1)
            act.wait_ge(sem["wps_done"], 1)
            act.wait_ge(sem["g_ready"], NCHUNK)
            act.copy(wps, ps[:, 2, 0:4 * CH].rearrange("p (a b) -> p a b", b=CH)).then_inc(sem["wps_evac"], 1)
            act.wait_ge(sem["wps_evac"], 1)
            for s in range(2):
                dma(io["wkv_prompt"].rearrange("(hp s) v k -> s v hp k", s=2)[s],
                    wps[64 * s:64 * s + 64, :, :]).then_inc(sem["st_w"], 16)

            project([6], range(3, 4))
            for j, m in ((7, 10), (8, 11)):
                mod_rows(m)
                project([j])
                mod_columns(m)
            for hp in range(4):
                act.wait_ge(sem["gn_done"], hp + 1)
                act.mul(TMn[:, hp, :], ps[:, 4 + hp, 0:T], 1.0 / CH).then_inc(sem["gn_evac"], 1)
            for hp in range(4):
                act.wait_ge(sem["gn_done"], hp + 5)
                act.activation(TMn[:, hp, :], ps[:, 4 + hp, 0:T], ACT.Sqrt, bias=gn_eps, scale=1.0 / CH).then_inc(sem["gn_evac"], 1)
            for k in range(KD):
                act.wait_ge(sem["x1_ready"], 2 * k + 2)
                act.activation(SQ[:, k, :], XT[:, k, :], ACT.Square).then_inc(sem["sq2_ready"], 1)
            act.wait_ge(sem["ms_ready"], 2)
            act.activation(RS[:, :], RS[:, :], ACT.Sqrt).then_inc(sem["sqrt_done"], 1)
            for i in range(6):
                half, n = i // 3, i % 3
                nt = TILES[n][1]
                act.wait_ge(sem["h2r_done"], i + 1)
                if i == 0:
                    act.wait_ge(sem["xr_zero"], 1)
                act.copy(XR[0:nt, n, half * 512:half * 512 + 512], ps[0:nt, i % 4, :]).then_inc(sem["h2r_evac"], 1)
            for n, (_, nt) in enumerate(TILES):
                act.wait_ge(sem["top_ready"], n + 1)
                act.activation(st[0:nt, 56 + 4 * n:60 + 4 * n], mx8[0:nt, n, 0:4], ACT.Exp, bias=st[0:nt, 70 + n:71 + n],
                               accum_out=st[0:nt, 76 + n:77 + n]).then_inc(sem["top_exp"], 1)
                act.activation(RNK[0:nt, n, :], LG[0:nt, n, :], ACT.Exp, bias=st[0:nt, 70 + n:71 + n]).then_inc(sem["top_exp"], 1)

            act.wait_ge(sem["gT_done"], 1)
            act.copy(gT[0:NE, :], ps[0:NE, 4, 0:T]).then_inc(sem["gT_ready"], 1)

            def second_bias(ks):
                for k in ks:
                    act.wait_ge(sem["comb_done"], k + 1)
                    act.copy(YA[:, k, :], ps[:, 6 + k % 2, 0:T]).then_inc(sem["comb_used"], 1)

            second_bias(range(0, 2))

            def scatter_matrix():
                act.copy(GT[0:C, 0, :], ps[0:C, 1, 0:T]).then_inc(sem["gt_evac"], 1)
                act.copy(GT[C:P, 1, :], ps[C:P, 1, 0:T]).then_inc(sem["gt_evac"], 1)

            act.wait_ge(sem["xr_done"], 1)
            act.copy(XGR, ps[:, 0, :]).then_inc(sem["xr_evac"], 1)
            second_bias(range(2, 5))
            act.wait_ge(sem["xg_done"], 1)
            act.copy(XGf, ps[:, 5, :]).then_inc(sem["xg_evac"], 1)
            second_bias(range(5, KD))
            act.wait_ge(sem["gt_zero"], 1)
            act.wait_ge(sem["gt_done"], 1)
            scatter_matrix()
            act.wait_ge(sem["rounds_ready"], 1)
            rounds = act.value_load(rounds_i[0:1, 0:1], min_val=1, max_val=MAXR)
            with act.Fori(0, rounds * NE) as i:
                for h in range(2):
                    act.wait_ge(sem["w1_used"], 4 * i + 4)
                    act.copy(UR[:, h, :], ps[:, 2 + h, :]).then_inc(sem["ur_evac"], 1)
                act.wait_ge(sem["xr_done"], i + 2)
                act.copy(XGR, ps[:, 0, :]).then_inc(sem["xr_evac"], 1)
                for h in range(2):
                    act.wait_ge(sem["ug_ready"], 2 * i + h + 1)
                    act.activation(US_, UG, ACT.Sigmoid, scale=1.702).then_inc(sem["us_ready"], 1)
                act.wait_ge(sem["xg_done"], i + 2)
                act.copy(XGf, ps[:, 5, :]).then_inc(sem["xg_evac"], 1)
                act.wait_ge(sem["y2_done"], 2 * i + 2)
                act.copy(YS, ps[:, 4, :]).then_inc(sem["ys_evac"], 1)
                act.wait_ge(sem["comb_done"], 8 * i + 16)
                scatter_matrix()
            for i in range(6):
                half, n = i // 3, i % 3
                nt = TILES[n][1]
                act.wait_ge(sem["fin_done"], i + 1)
                act.copy(fin[0:nt, n, half * 512:half * 512 + 512], ps[0:nt, i % 4, :]).then_inc(sem["fin_evac"], 1)
            for name, total in (("st_k", 32), ("st_kv", 64), ("st_w", 32)):
                act.wait_ge(sem[name], total)

        @block.tensor
        def _(pe):
            mm, tr = nc.tensor.matmul, nc.tensor.transpose
            a = [0]

            def group():
                g = a[0]
                a[0] += 1
                if g >= 4:
                    pe.wait_ge(sem["a_evac"], g - 3)
                return ps[:, g % 4, :]

            def weights(kind, j):
                g = STREAM_AT[kind, j]
                slot = slots_of[g]
                pe.wait_ge(sem[f"ring{slot}"], 16 * (uses_before(slot, g) + 1))
                return ring[:, slot, :, :]

            pe.wait_ge(sem["ld_cst"], 16)
            pe.wait_ge(sem["ld_x"], 48)
            for k in range(KD):
                bank = group()
                for n, (t0, nt) in enumerate(TILES):
                    last = tr(bank[:, t0:t0 + nt], XR[0:nt, n, k * P:k * P + P], ID[0:nt, 0:nt])
                last.then_inc(sem["a_done"], 1)
            pe.wait_ge(sem["ld_par"], 16)
            tr(ps[:, 6, 0:NPAR], prow[0:NPAR, :], ID[0:NPAR, 0:NPAR]).then_inc(sem["setup_t"], 1)
            pe.wait_ge(sem["ld_b1"], 16)
            for i in range(4):
                last = tr(ps[:, 7, i * P:i * P + P], b1r[:, i, :], ID)
            last.then_inc(sem["setup_t"], 1)
            pe.wait_ge(sem["silu_ready"], 1)
            for k in range(KD):
                last = tr(ps[:, 4, 9 * k:9 * k + 9], crow[0:9, k * P:k * P + P], ID[0:9, 0:9])
            last.then_inc(sem["setup_t"], 1)
            pe.wait_ge(sem["ld_ss"], 16)
            for i in range(14):
                tr(ps[:, 5, NS * i:NS * i + NS], ssr[0:NS, i * P:i * P + P], ID[0:NS, 0:NS])
            pe.wait_ge(sem["ld_tab"], 16)
            mm(ps[0:HQ, 5, 256:256 + KEYS], tab[:, :], cst[0:NE, K_OB:K_OB + KEYS], start=True, stop=True).then_inc(sem["setup_t"], 1)
            pe.wait_ge(sem["setup_ready"], 1)
            for k in range(KD):
                pe.wait_ge(sem["a_evac"], k + 1)
                last = mm(ps[:, 6, 0:T], ONE, SQ[:, k, :], start=(k == 0), stop=(k == KD - 1))
            last.then_inc(sem["ss_done"], 1)

            def modulation(j):
                w, bank = weights("mod", j), group()
                for k in range(KD):
                    for s in range(4):
                        last = mm(bank[32 * s:32 * s + 32, 0:P], cT[:, k, :], w[:, k, s * P:s * P + P], start=(k == 0), stop=(k == KD - 1))
                last.then_inc(sem["a_done"], 1)

            def modulation_transposed(j):
                bank = group()
                pe.wait_ge(sem["a_evac"], a_end(f"mod{j}"))
                tr(bank[:, 0:P], MR, ID).then_inc(sem["a_done"], 1)

            def gate_group(s):
                w = weights("win", 5)
                if s:
                    pe.wait_ge(sem["f_evac"], s)
                for k in range(KD):
                    last = mm(ps[:, 7, 0:T], w[:, k, s * P:s * P + P], HT[:, k, :], start=(k == 0), stop=(k == KD - 1))
                last.then_inc(sem["f_done"], 1)

            def project(js, parts=range(4)):
                for j in js:
                    w = weights("win", j)
                    for s in parts:
                        bank = group()
                        for k in range(KD):
                            last = mm(bank[:, 0:T], w[:, k, s * P:s * P + P], HT[:, k, :], start=(k == 0), stop=(k == KD - 1))
                        last.then_inc(sem["a_done"], 1)

            pe.wait_ge(sem["setup_ready"], 3)
            pe.wait_ge(sem["setup_ready"], 4)
            for j in range(4):
                modulation(j)
                modulation_transposed(j)
            pe.wait_ge(sem["h1_ready"], 2)
            project([0])
            for j, m in ((1, 4), (2, 5)):
                modulation(m)
                project([j])
                modulation_transposed(m)
            pe.wait_ge(sem["qksq_ready"], 1)
            for i in range(5):
                mm(group()[:, 0:T], BO, XRf[:, i * T:i * T + T], start=True, stop=True).then_inc(sem["a_done"], 1)
            for j, m in ((3, 6), (4, 7)):
                modulation(m)
                project([j])
                modulation_transposed(m)
            pe.wait_ge(sem["kksq_ready"], 1)
            for hp in range(4):
                mm(group()[:, 0:T], BO, SQ[:, hp, :], start=True, stop=True).then_inc(sem["a_done"], 1)
            modulation(8)
            pe.wait_ge(sem["ms_ready"], 1)
            pe.wait_ge(sem["setup_ready"], 2)
            for i in range(4):
                if i >= 2:
                    pe.wait_ge(sem["sh_evac"], i - 1)
                for c in range(4 * i, min(4 * i + 4, 14)):
                    last = tr(ps[0:9, 6 + i % 2, (c % 4) * P:(c % 4) * P + P], PTv[:, CR + c, NP - 1:T], ID)
                last.then_inc(sem["sh_t"], 1)
            pe.wait_ge(sem["ld_lw"], 48)
            pe.wait_ge(sem["lora_in"], 1)
            for hp in range(4):
                mm(group()[:, 0:T], LWw[0:64, hp * P:hp * P + P], XMv[0:64, 12, :], start=True, stop=True).then_inc(sem["a_done"], 1)
            for hp in range(4):
                mm(group()[:, 0:T], LWw[64:128, hp * P:hp * P + P], XMv[64:128, 12, :], start=True, stop=True).then_inc(sem["a_done"], 1)
            pe.wait_ge(sem["lora_in"], 2)
            for hp in range(4):
                mm(group()[:, 0:T], LWg[:, hp * P:hp * P + P], XMv[:, 13, :], start=True, stop=True).then_inc(sem["a_done"], 1)
            modulation_transposed(8)
            pe.wait_ge(sem["sh_evac"], 4)

            pe.wait_ge(sem["a_evac"], a_end("modT8"))
            pe.wait_ge(sem["qk_ready"], 1)
            for kv in range(HKV):
                mm(ps[:, kv, 0:T], II[64 * kv:64 * kv + 64, :], PTv[64 * kv:64 * kv + 64, CK, :],
                   start=True, stop=True).then_inc(sem["kvrow_done"], 1)
            for n, (t0, nt) in enumerate(TILES):
                tr(ps[0:nt, 2, n * P:n * P + P], PTv[:, CV, t0:t0 + nt], ID)
            for n, (t0, nt) in enumerate(TILES[1:]):
                last = tr(ps[0:nt, 3, n * P:n * P + P], PTv[:, CK, t0:t0 + nt], ID)
            last.then_inc(sem["kvrow_done"], 1)
            pe.wait_ge(sem["ld_kc"], 16)
            for b in range(NS):
                last = tr(ps[:, 4 + b // 4, (b % 4) * P:(b % 4) * P + P], kcr[:, b, :], ID)
            last.then_inc(sem["kc_done"], 1)
            pe.wait_ge(sem["ld_hk"], 16)
            HKf = HK.rearrange("p a b -> p (a b)")
            for i in range(4):
                if i == 2:
                    pe.wait_ge(sem["kc_evac"], 1)
                mm(ps[:, [6, 7, 4, 5][i], :], cst[:, K_REV:K_REV + P], HKf[:, i * 512:i * 512 + 512],
                   start=True, stop=True).then_inc(sem["bm_done"], 1)
            pe.wait_ge(sem["kvrow_evac"], 1)
            for h in range(HQ):
                s = h % 2
                last = mm(ps[:, 2 + s, NS * (h // 2):NS * (h // 2) + NS], II[64 * s:64 * s + 64, :], PTv[64 * s:64 * s + 64, h // 2, NP:T],
                          start=True, stop=True)
            last.then_inc(sem["qs_done"], 1)
            pe.wait_ge(sem["qs_evac"], 1)
            pe.wait_ge(sem["bm_evac"], 4)

            def scores(g4):
                n, kv = g4 // 2, g4 % 2
                J = P if n == 0 else 2 * P
                for g in range(GQA):
                    h = GQA * kv + g
                    s = h % 2
                    last = mm(ps[:, 2 * (g4 % 2) + s, (g // 2) * J:(g // 2) * J + J],
                              PTv[64 * s:64 * s + 64, h // 2, n * P:n * P + P], kd[64 * s:64 * s + 64, kv, 0:J],
                              start=True, stop=True)
                last.then_inc(sem["att_s"], 1)

            scores(0)
            scores(1)
            gate_group(0)
            for g4 in range(4):
                n, kv = g4 // 2, g4 % 2
                pe.wait_ge(sem["att_p"], g4 + 1)
                for jt in range(n + 1):
                    if g4:
                        pe.wait_ge(sem["att_pte"], g4 if n == 0 else 2 * g4 - 2)
                    for g in range(GQA):
                        last = tr(ps[:, 4 + jt, g * P:g * P + P], Pm[:, g, jt * P:jt * P + P], ID)
                    last.then_inc(sem["att_pt"], 1)
                if g4 < 2:
                    scores(g4 + 2)
                pe.wait_ge(sem["att_pte"], g4 + 1 if n == 0 else 2 * g4)
                if g4:
                    pe.wait_ge(sem["att_oe"], g4)
                for g in range(GQA):
                    s = g % 2
                    for jt in range(n + 1):
                        last = mm(ps[64 * s:64 * s + 64, 6, (g // 2) * P:(g // 2) * P + P], vr[:, jt, 64 * kv:64 * kv + 64],
                                  pT[:, g, jt, :], start=(jt == 0), stop=(jt == n))
                last.then_inc(sem["att_o"], 1)
                if g4 < 3:
                    gate_group(g4 + 1)
            pe.wait_ge(sem["att_oe"], 4)
            for b in range(NS):
                last = mm(ps[0:HQ, 4 + b // 3, (b % 3) * KEYS:(b % 3) * KEYS + KEYS], Qs[:, :, b], kcT[:, b, :], start=True, stop=True)
            last.then_inc(sem["smp_done"], 1)
            project([6], range(0, 1))
            modulation(9)
            pe.wait_ge(sem["f_evac"], 4)
            pe.wait_ge(sem["smp_p"], 1)
            for b in range(NS):
                tr(ps[:, 7, b * NS:b * NS + NS], SsT[0:HQ, b, 0:P], ID[0:HQ, 0:HQ])
            tr(ps[0:NS, 7, 64:72], SsT[0:HQ, :, P], ID[0:HQ, 0:HQ]).then_inc(sem["smp_done"], 1)
            project([6], range(1, 2))
            pe.wait_ge(sem["smp_pte"], 1)
            pe.wait_ge(sem["ld_vc"], 16)
            for b in range(NS):
                mm(ps[:, 4, b * HQ:b * HQ + HQ], vcr[:, b, :], pTs[:, b, :], start=True, stop=False)
                last = mm(ps[:, 4, b * HQ:b * HQ + HQ], vr[0:NS, 2, :], PSf[:, b, :], start=False, stop=True)
            last.then_inc(sem["smp_done"], 1)
            project([6], range(2, 3))
            pe.wait_ge(sem["os_ready"], 1)
            for kv in range(HKV):
                last = mm(ps[:, 5 + kv, 0:32].rearrange("p (a b) -> p a b", b=4), II[64 * kv:64 * kv + 64, :],
                          OS[64 * kv:64 * kv + 64, :, 4 * kv:4 * kv + 4], start=True, stop=True)
            last.then_inc(sem["smp_done"], 1)
            modulation_transposed(9)

            pe.wait_ge(sem["zr_ready"], 1)
            pe.wait_ge(sem["smp_oe"], 1)
            pe.wait_ge(sem["a_evac"], a_end("modT9"))
            for hp in range(4):
                mm(ps[:, hp, 0:T], BO, TM[:, hp, :], start=True, stop=True).then_inc(sem["bon_done"], 1)
            for i in range(8):
                mat, n = i // 2, i % 2
                if i < 4:
                    pe.wait_ge(sem["bon_evac"], i + 1)
                if i >= 4:
                    pe.wait_ge(sem["row_evac"], i - 3)
                for hp in range(4):
                    if mat == 0:
                        for par in range(2):
                            last = mm(ps[64 * par:64 * par + 64, i % 4, hp * P:hp * P + P], ZR[:, hp, 2 * n + par, 0, :], ID,
                                      start=True, stop=True)
                        continue
                    src = [Bh[:, hp, n * P:n * P + P], Kh[:, hp, n * P:n * P + P], XMv[:, 8 + hp, n * P:n * P + P]][mat - 1]
                    last = tr(ps[:, i % 4, hp * P:hp * P + P], src, ID)
                last.then_inc(sem["row_done"], 1)
            units = [(n, h, par) for n in range(2) for h in range(HQ) for par in range(2)]

            def half(x, par):
                return x[64 * par:64 * par + 64]

            for n in range(2):
                if n:
                    pe.wait_ge(sem["nr_ready"], 1)
                    pe.wait_ge(sem["kr_ready"], 1)
                for q, M in enumerate((Bh, Kh)):
                    for _, h, par in units[:16]:
                        s, hp, c = h % 2, h // 2, 2 * n + par
                        last = mm(ps[64 * par:64 * par + 64, 4 + 2 * q + s, hp * P:hp * P + P],
                                  M[64 * s:64 * s + 64, hp, c * CH:c * CH + CH],
                                  ZR[64 * s:64 * s + 64, hp, c, :, :].rearrange("p a b -> p (a b)"), start=True, stop=True)
                    last.then_inc(sem["ab_done"], 1)
            for i in range(len(LEVELS)):
                if i == 0:
                    pe.wait_ge(sem["nm0_ready"], 1)
                else:
                    pe.wait_ge(sem["nm_ready"], i)
                for n in range(2):
                    if i == 0:
                        pe.wait_ge(sem["row_evac"], 8)
                        pe.wait_ge(sem["nr_ready"], 2)
                        pe.wait_ge(sem["kr_ready"], 2)
                    else:
                        pe.wait_ge(sem["x_ready"], 2 * (i - 1) + n + 1)
                    for _, h, par in units[:16]:
                        u = 8 * n + h
                        rhs = II[64 * par:64 * par + 64, 0:CH] if i == 0 else half(X, par)[:, u, :]
                        last = mm(ps[64 * par:64 * par + 64, 4 * n, h * CH:h * CH + CH], half(NM[i % 2], par)[:, u, :], rhs,
                                  start=True, stop=True)
                    last.then_inc(sem["y_done"], 1)
                if i == 0:
                    continue
                for n in range(2):
                    pe.wait_ge(sem["y_evac"], 2 * (i - 1) + n + 1)
                    if i < len(LEVELS) - 1:
                        for _, h, par in units[:16]:
                            u = 8 * n + h
                            last = mm(ps[64 * par:64 * par + 64, 4 * n + 1, h * CH:h * CH + CH], half(XX, par)[:, u, :],
                                      half(Y, par)[:, u, :], start=True, stop=True)
                    for _, h, par in units[:16]:
                        u = 8 * n + h
                        last = mm(ps[64 * par:64 * par + 64, 4 * n + 2, h * CH:h * CH + CH], half(Y, par)[:, u, :],
                                  half(XX, par)[:, u, :], start=True, stop=True)
                    last.then_inc(sem["dx_done"], 1)
            for n in range(2):
                for _, h, par in units[:16]:
                    u = 8 * n + h
                    last = mm(ps[64 * par:64 * par + 64, 3 + 4 * n, h * CH:h * CH + CH], half(KR, par)[:, u, 0:CH],
                              half(Vr, par)[:, u, :], start=True, stop=True)
                last.then_inc(sem["u0_done"], 1)
            for n in range(2):
                pe.wait_ge(sem["x_ready"], 2 * (len(LEVELS) - 1) + n + 1)
                pe.wait_ge(sem["u0_evac"], n + 1)
                for _, h, par in units[:16]:
                    u = 8 * n + h
                    last = mm(ps[64 * par:64 * par + 64, 4 * n + h // 4, (h % 4) * P:(h % 4) * P + P], half(XX, par)[:, u, :],
                              half(ZU, par)[:, u, :], start=True, stop=True)
                last.then_inc(sem["xzw_done"], 1)
            pe.wait_ge(sem["xzw_evac"], 2)
            allu = [(h, c) for h in range(HQ) for c in range(NCHUNK)]

            def head_chunk(bank, h, c):
                col = (h // 2) * 2 * CH + (c // 2) * CH
                s = h % 2
                return ps[64 * s:64 * s + 64, bank + c % 2, col:col + CH]

            def rows_of(M, h, c, lo, hi):
                return M[64 * (c % 2):64 * (c % 2) + 64, 8 * (c // 2) + h, lo:hi]

            for h, c in allu:
                last = mm(head_chunk(0, h, c), rows_of(XZW, h, c, 0, CH), rows_of(NR, h, c, CH, P), start=True, stop=True)
            last.then_inc(sem["carry_done"], 1)
            for h, c in allu:
                last = mm(head_chunk(4, h, c), rows_of(XZW, h, c, 0, CH), rows_of(Br, h, c, 0, CH), start=True, stop=True)
            last.then_inc(sem["carry_done"], 1)
            for h, c in allu:
                mm(head_chunk(2, h, c), rows_of(Br, h, c, 0, CH), rows_of(XZW, h, c, CH, P), start=True, stop=False)
                last = mm(head_chunk(2, h, c), rows_of(Kr, h, c, 0, CH), rows_of(Vr, h, c, 0, CH), start=False, stop=True)
            last.then_inc(sem["carry_done"], 1)
            pe.wait_ge(sem["dr_ready"], 2)
            pe.wait_ge(sem["mc_ready"], 2)
            for c in range(NCHUNK):
                if c:
                    pe.wait_ge(sem["g_ready"], c)
                    for h in range(HQ):
                        s, hp = h % 2, h // 2
                        last = mm(ps[64 * s:64 * s + 64, 7, hp * CH:hp * CH + CH], MC[64 * s:64 * s + 64, hp, c, :],
                                  G4[64 * s:64 * s + 64, c - 1, hp, :], start=True, stop=True)
                    last.then_inc(sem["gm_done"], 1)
                for h in range(HQ):
                    s, hp = h % 2, h // 2
                    out = head_chunk(4, h, c)
                    mm(out, rows_of(XZW, h, c, CH, P), rows_of(NR, h, c, CH, P), start=True, stop=False)
                    last = mm(out, rows_of(Vr, h, c, 0, CH), rows_of(KR, h, c, CH, P), start=False, stop=True)
                for h in range(HQ if c else 0):
                    s, hp = h % 2, h // 2
                    last = mm(ps[64 * s:64 * s + 64, 6 if c < 3 else 3, (c - 1) % 2 * 256 + hp * CH:(c - 1) % 2 * 256 + hp * CH + CH],
                              G4[64 * s:64 * s + 64, c - 1, hp, :], ZR[64 * s:64 * s + 64, hp, c, 1, :], start=True, stop=True)
                last.then_inc(sem["o_done"], 1)
            pe.wait_ge(sem["g_ready"], NCHUNK)
            pe.wait_ge(sem["dr_ready"], 2)
            for h in range(HQ):
                s, hp = h % 2, h // 2
                last = mm(ps[64 * s:64 * s + 64, 2, hp * CH:hp * CH + CH], G4[64 * s:64 * s + 64, NCHUNK - 1, hp, :],
                          II[64 * s:64 * s + 64, 0:CH], start=True, stop=True)
            last.then_inc(sem["wps_done"], 1)
            pe.wait_ge(sem["wps_evac"], 1)
            pe.wait_ge(sem["ot_ready"], 1)

            def spread(q):
                pe.wait_ge(sem["ex_ready"], q + 1)
                if q:
                    pe.wait_ge(sem["smp_step"], q)
                EXf = EX.rearrange("p a b -> p (a b)")
                for i in range(4):
                    last = mm(ps[:, 4 + i, :], BO, EXf[:, i * 512:i * 512 + 512], start=True, stop=True)
                last.then_inc(sem["ex_used"], 1)

            spread(0)
            project([6], range(3, 4))
            modulation(10)
            project([7], range(0, 1))
            spread(1)
            project([7], range(1, 4))
            spread(2)
            modulation_transposed(10)
            modulation(11)
            project([8], range(0, 1))
            spread(3)
            project([8], range(1, 4))
            spread(4)
            modulation_transposed(11)
            pe.wait_ge(sem["a_evac"], a_end("modT11"))

            def mixer(q, ks):
                w = weights(("pa", "pb")[q], 0).rearrange("p k n -> p (k n)").rearrange("p (k n) -> p k n", n=D)
                for k in ks:
                    if KD * q + k >= 4:
                        pe.wait_ge(sem["pab_evac"], KD * q + k - 3)
                    for i in range(4):
                        last = mm(ps[:, k % 4, 0:T], w[:, i, k * P:k * P + P], (OA, OT)[q][:, i, :], start=(i == 0), stop=(i == 3))
                    last.then_inc(sem["pab_done"], 1)

            mixer(0, range(4))
            pe.wait_ge(sem["smp_step"], 5)
            for hp in range(4):
                mm(ps[:, 4 + hp, 0:T], BO, OT[:, hp, :], start=True, stop=True).then_inc(sem["gn_done"], 1)
            pe.wait_ge(sem["gnsq_ready"], 1)
            for hp in range(4):
                mm(ps[:, 4 + hp, 0:T], BO, OSQ[:, hp, :], start=True, stop=True).then_inc(sem["gn_done"], 1)
            mixer(0, range(4, KD))
            pe.wait_ge(sem["ob_ready"], 1)
            mixer(1, range(KD))
            pe.wait_ge(sem["m_ready"], KD)
            pe.wait_ge(sem["pab_evac"], 2 * KD)
            for k in range(KD):
                w = weights("wo", k // 4)
                if k >= 4:
                    pe.wait_ge(sem["x1_ready"], 2 * (k - 3))
                for i in range(KD):
                    last = mm(ps[:, 4 + k % 4, 0:T], w[:, i, (k % 4) * P:(k % 4) * P + P], HT[:, i, :], start=(i == 0), stop=(i == KD - 1))
                last.then_inc(sem["wo_done"], 1)
            for k in range(KD):
                pe.wait_ge(sem["sq2_ready"], k + 1)
                last = mm(ps[:, 0, 0:T], ONE, SQ[:, k, :], start=(k == 0), stop=(k == KD - 1))
            last.then_inc(sem["ss_done"], 1)
            pe.wait_ge(sem["ld_r"], 48)
            for half in range(2):
                pe.wait_ge(sem["h2_ready"], half + 1)
                for k in range(4 * half, 4 * half + 4):
                    last = mm(ps[0:NE, 4, 0:T], wr[:, k, :], HT[:, k, :], start=(k == 0), stop=(k == KD - 1))
                if half:
                    last.then_inc(sem["lg_done"], 1)
                for n, (t0, nt) in enumerate(TILES):
                    i = 3 * half + n
                    if i >= 4:
                        pe.wait_ge(sem["h2r_evac"], i - 3)
                    for k in range(4):
                        last = tr(ps[0:nt, i % 4, k * P:k * P + P], HT[:, 4 * half + k, t0:t0 + nt], ID)
                    last.then_inc(sem["h2r_done"], 1)
                    if i == 3:
                        pe.wait_ge(sem["lgt_ready"], 1)
                        for m, (u0, mt) in enumerate(TILES):
                            last = tr(ps[0:mt, 5, m * NE:m * NE + NE], LGT[0:NE, u0:u0 + mt], ID[0:NE, 0:NE])
                        last.then_inc(sem["lg_done"], 1)
            pe.wait_ge(sem["msk_ready"], 1)
            for n, (t0, nt) in enumerate(TILES):
                for i in range(n + 1):
                    mi = TILES[i][1]
                    mm(ps[0:nt, 5, n * NE:n * NE + NE], (cst[0:mi, K_US:K_US + nt] if i == n else ONE[0:mi, 0:nt]),
                       MSK[0:mi, i, :], start=(i == 0), stop=(i == n))
            for i in range(3):
                mi = TILES[i][1]
                last = mm(ps[:, 5, 96:96 + NE], ONE[0:mi, :], MSK[0:mi, i, :], start=(i == 0), stop=(i == 2))
            last.then_inc(sem["pos_done"], 1)
            pe.wait_ge(sem["gte_ready"], 1)
            for n, (t0, nt) in enumerate(TILES):
                last = tr(ps[0:NE, 4, t0:t0 + nt], GTE[0:nt, n, :], ID[0:nt, 0:nt])
            last.then_inc(sem["gT_done"], 1)
            pe.wait_ge(sem["gT_ready"], 1)

            def second_bias(ks):
                for k in ks:
                    if k >= 2:
                        pe.wait_ge(sem["comb_used"], k - 1)
                    mm(ps[:, 6 + k % 2, 0:T], b2r[0:NE, k * P:k * P + P], gT[0:NE, :], start=True, stop=True).then_inc(sem["comb_done"], 1)

            second_bias(range(0, 2))

            def gather():
                for n in range(3):
                    for s in range(2):
                        last = mm(ps[64 * s:64 * s + 64, 0, :], OH[:, n, :], XR[:, n, s * 512:s * 512 + 512], start=(n == 0), stop=(n == 2))
                last.then_inc(sem["xr_done"], 1)

            def gather_transposed():
                for k in range(4):
                    last = tr(ps[:, 5, k * P:k * P + P], XGR[:, k * P:k * P + P], ID)
                last.then_inc(sem["xg_done"], 1)
                for n, (t0, nt) in enumerate(TILES):
                    last = tr(ps[:, 1, t0:t0 + nt], OG[0:nt, n, :], ID[0:nt, 0:nt])
                last.then_inc(sem["gt_done"], 1)

            pe.wait_ge(sem["h2r_evac"], 6)
            pe.wait_ge(sem["oh_ready"], 1)
            gather()
            second_bias(range(2, 5))
            pe.wait_ge(sem["xr_evac"], 1)
            pe.wait_ge(sem["pos_evac"], 1)
            gather_transposed()
            second_bias(range(5, KD))
            pe.wait_ge(sem["rounds_ready"], 1)
            rounds = pe.value_load(rounds_i[0:1, 0:1], min_val=1, max_val=MAXR)
            before = [uses_before(c) for c in range(6)]
            with pe.Fori(0, rounds * NE) as i:
                pe.wait_ge(sem["xg_evac"], i + 1)
                for c in range(4):
                    pe.wait_ge(sem[f"ring{c}"], i * 16 + 16 * (before[c] + 1))
                    for k in (2 * c, 2 * c + 1):
                        for hh in range(2):
                            for lin in range(2):
                                last = mm(ps[64 * lin:64 * lin + 64, 2 + hh, :], XG[:, k % 4, k // 4, :],
                                          slot_tile(c)[:, k % 2, lin * FE + hh * 512:lin * FE + hh * 512 + 512],
                                          start=(k == 0), stop=(k == KD - 1))
                    last.then_inc(sem["w1_used"], 1)

                def hidden_transposed(hh):
                    pe.wait_ge(sem["ur_evac"], 2 * i + hh + 1)
                    for f in range(4):
                        last = tr(ps[:, 2 + hh, f * P:f * P + P], UR[:, hh, f * P:f * P + P], ID)
                    last.then_inc(sem["ut_done"], 1)

                pe.wait_ge(sem["oh_ready"], i + 2)
                gather()
                hidden_transposed(0)
                hidden_transposed(1)
                pe.wait_ge(sem["xr_evac"], i + 2)
                pe.wait_ge(sem["gt_evac"], 2 * i + 2)
                gather_transposed()
                for c in (4, 5):
                    pe.wait_ge(sem[f"ring{c}"], i * 16 + 16 * (before[c] + 1))
                    pe.wait_ge(sem["ac_ready"], 2 * i + c - 3)
                    for f in range(4 * (c - 4), 4 * (c - 4) + 4):
                        for hh in range(2):
                            last = mm(ps[64 * hh:64 * hh + 64, 4, :], AC[:, f, :], slot_tile(c)[:, f % 4, hh * 512:hh * 512 + 512],
                                      start=(f == 0), stop=(f == NF - 1))
                    last.then_inc(sem["y2_done"], 1)
                pe.wait_ge(sem["ys_evac"], i + 1)
                for k in range(KD):
                    pe.wait_ge(sem["comb_used"], 8 * i + 7 + k)
                    mm(ps[:, 6 + k % 2, 0:T], YS[:, (k % 4) * P:(k % 4) * P + P], GT[:, k // 4, :], start=True, stop=True).then_inc(sem["comb_done"], 1)
            pe.wait_ge(sem["gt_evac"], rounds * (2 * NE) + 2)
            for i in range(6):
                half, n = i // 3, i % 3
                t0, nt = TILES[n]
                pe.wait_ge(sem["x2_ready"], 4 * half + 4)
                if i >= 4:
                    pe.wait_ge(sem["fin_evac"], i - 3)
                for k in range(4):
                    last = tr(ps[0:nt, i % 4, k * P:k * P + P], XT[:, 4 * half + k, t0:t0 + nt], ID)
                last.then_inc(sem["fin_done"], 1)

        @block.vector
        def _(dve):
            v = nc.vector
            chain = Chain(dve, sem["dve_chain"])

            def done(instruction, name, value):
                instruction.then_inc(sem[name], 1)
                dve.wait_ge(sem[name], value)

            v.memset(epsc[:, 0:1], 1e-6)
            v.memset(epsc[:, 1:2], 64e-5)
            v.memset(Qs[:, :, :], 0.0).then_inc(sem["qs_zero"], 1)
            dve.wait_ge(sem["ld_c"], 32)
            dve.wait_ge(sem["csig_ready"], 1)
            v.tensor_tensor(crow[0:9, :], crow[0:9, :], csig[0:9, :], ALU.mult).then_inc(sem["silu_ready"], 1)
            dve.wait_ge(sem["setup_t"], 1)
            done(v.tensor_copy(PC[:, :], ps[:, 6, 0:NPAR]), "setup_ready", 1)
            dve.wait_ge(sem["setup_t"], 2)
            v.tensor_copy(b1T[:, :], ps[:, 7, :]).then_inc(sem["setup_ready"], 1)
            dve.wait_ge(sem["setup_t"], 3)
            chain(v.memset(cT[:, :, :], 0.0))
            v.tensor_copy(cT[:, :, 0:9], ps[:, 4, 0:72].rearrange("p (a b) -> p a b", b=9)).then_inc(sem["setup_ready"], 1)
            dve.wait_ge(sem["setup_t"], 4)
            chain(v.tensor_copy(SS[:, :, :], ps[:, 5, 0:112].rearrange("p (a b) -> p a b", b=NS)))
            v.tensor_copy(brow[:, 0:KEYS], ps[0:HQ, 5, 256:256 + KEYS]).then_inc(sem["brow_ready"], 1)
            dve.wait_ge(sem["brow_ready"], 1)
            dve.sem_inc(sem["setup_ready"], 1)

            def rms(i):
                dve.wait_ge(sem["ss_done"], i)
                v.tensor_scalar(RS[:, :], ps[:, 6 if i == 1 else 0, 0:T], 1.0 / D, 1e-5, ALU.mult, ALU.add).then_inc(sem["ms_ready"], 1)
                dve.wait_ge(sem["sqrt_done"], i)
                chain(v.reciprocal(RS[:, :], RS[:, :]))

            def modulate(shift, scale, norm, name):
                chain(v.scalar_tensor_tensor(out=A1[:, :, :], in0=modT[:, scale:scale + KD, :], scalar=1.0,
                                             in1=PC[:, PCOL[norm]:PCOL[norm] + KD].unsqueeze(2).broadcast_to([P, KD, 9]),
                                             op0=ALU.add, op1=ALU.mult))
                for half in range(2):
                    ks = slice(4 * half, 4 * half + 4)
                    chain(v.tensor_tensor(HT[:, ks, :], XT[:, ks, :], RS[:, :].unsqueeze(1).broadcast_to([P, 4, T]), ALU.mult))
                    for k in range(4 * half, 4 * half + 4):
                        v.tensor_scalar(HT[:, k, 0:NP], HT[:, k, 0:NP], A1[:, k, 0:1], modT[:, shift + k, 0:1], ALU.mult, ALU.add)
                    chain(v.tensor_tensor(HT[:, ks, NP:T], HT[:, ks, NP:T], A1[:, ks, 1:9], ALU.mult))
                    v.tensor_tensor(HT[:, ks, NP:T], HT[:, ks, NP:T], modT[:, shift + 4 * half:shift + 4 * half + 4, 1:9], ALU.add).then_inc(sem[name], 1)
                dve.wait_ge(sem[name], 2)

            def add_bias(lo, hi):
                return modT[:, lo:hi, :], PC[:, PCOL["b_mod"] + lo:PCOL["b_mod"] + hi].unsqueeze(2).broadcast_to([P, hi - lo, 9])

            rms(1)
            dve.wait_ge(sem["a_evac"], a_end("modT3"))
            out, bias = add_bias(0, 16)
            chain(v.tensor_tensor(out, out, bias, ALU.add))
            modulate(0, 8, "norm1", "h1_ready")

            dve.wait_ge(sem["a_evac"], a_end("win1"))
            qk = PT[:, 0:5 * T]
            done(v.tensor_tensor(XRf[:, 0:5 * T], qk, qk, ALU.mult), "qksq_ready", 1)

            def mix(lo, hi, order):
                M, F = XMv[:, lo:hi, :], PTv[:, CR + lo:CR + hi, :]
                v.tensor_tensor(M[:, :, 1:NP], F[:, :, 0:NP - 1], F[:, :, 1:NP], ALU.subtract)
                v.tensor_scalar(M[:, :, 0:1], F[:, :, 0:1], -1.0, None, ALU.mult)
                chain(v.tensor_tensor(M[:, :, NP:T], SS[:, lo:hi, :], F[:, :, NP:T], ALU.subtract))
                for i in order:
                    ins = v.scalar_tensor_tensor(out=XMv[:, i, :], in0=XMv[:, i, :], scalar=par("rw_mu", i), in1=PTv[:, CR + i, :],
                                                 op0=ALU.mult, op1=ALU.add)
                    if i == 13:
                        done(ins, "mixed", 1)
                    elif i == order[-1]:
                        chain(ins)

            dve.wait_ge(sem["a_evac"], a_end("win2"))
            mix(0, 6, range(6))
            dve.wait_ge(sem["a_evac"], a_end("qk"))
            chain(v.reciprocal(XRf[:, 5 * T:10 * T], XRf[:, 5 * T:10 * T]))
            chain(v.tensor_tensor(qk, qk, XRf[:, 5 * T:10 * T], ALU.mult))
            chain(v.tensor_scalar(PT[:, 0:4 * T], PT[:, 0:4 * T], par("q_norm"), SCALE, ALU.mult, ALU.mult))
            done(v.tensor_scalar(PTv[:, CK, :], PTv[:, CK, :], par("k_norm"), None, ALU.mult), "qk_ready", 1)
            dve.wait_ge(sem["a_evac"], a_end("win3"))
            mix(6, 10, range(6, 10))
            for hp in range(4):
                ins = v.tensor_scalar(NK[:, hp, :], XMv[:, 4 + hp, :], par("rw_k_k", hp), None, ALU.mult)
            chain(ins)
            done(v.tensor_tensor(SQ[:, 0:4, :], NK, NK, ALU.mult), "kksq_ready", 1)
            dve.wait_ge(sem["a_evac"], a_end("win4"))
            mix(10, 14, (12, 13, 10, 11))
            dve.wait_ge(sem["a_evac"], a_end("kk"))
            Rn = SQ[:, 4:8, :]
            chain(v.tensor_scalar(Rn, Rn, 1e-12, None, ALU.max))
            chain(v.reciprocal(Rn, Rn))
            chain(v.scalar_tensor_tensor(out=NK, in0=NK, scalar=-1.0, in1=Rn, op0=ALU.mult, op1=ALU.mult))
            dve.wait_ge(sem["a_evac"], a_end("decay"))
            LDf = RZ[:, 0:4 * T]
            chain(v.tensor_scalar(LDf, LDf, -E_HALF, None, ALU.mult))
            for hp in range(4):
                for c in range(NCHUNK):
                    ins = v.tensor_tensor_scan(out=CS[:, hp, c * CH:c * CH + CH], data0=ONE[:, 0:CH], data1=LD[:, hp, c * CH:c * CH + CH],
                                               initial=0.0, op0=ALU.mult, op1=ALU.add)
            done(ins, "cs_ready", 1)
            done(v.tensor_tensor(eM, CS, LD[:, :, 0:NP], ALU.subtract), "cs_ready", 2)
            dve.wait_ge(sem["a_evac"], a_end("rate"))
            for hp in range(4):
                ins = v.tensor_scalar(TM[:, hp, :], Aa[:, hp, :], 1.0, par("rw_k_a", hp), ALU.subtract, ALU.mult)
            chain(ins)
            chain(v.scalar_tensor_tensor(out=k_mod, in0=TM, scalar=1.0, in1=k_mod, op0=ALU.add, op1=ALU.mult))
            done(v.scalar_tensor_tensor(out=Aa, in0=NK, scalar=-1.0, in1=Aa, op0=ALU.mult, op1=ALU.mult), "kmod_ready", 1)
            dve.wait_ge(sem["decays"], 4)
            dve.wait_ge(sem["bm_evac"], 4)
            dve.wait_ge(sem["qs_done"], 1)
            dve.wait_ge(sem["qs_zero"], 1)
            for kv in range(HKV):
                rows = slice(64 * kv, 64 * kv + 64)
                ins = v.tensor_copy(Qs[rows, 4 * kv:4 * kv + 4, :].rearrange("p (j s) b -> p s j b", s=2),
                                    ps[rows, 2:4, 16 * kv:16 * kv + 16].rearrange("p s (j b) -> p s j b", b=NS))
                if kv:
                    done(ins, "qs_evac", 1)
                else:
                    chain(ins)
            BMv = BM[:, :].rearrange("p (a b) -> p a b", b=2 * P)
            dve.wait_ge(sem["ld_sink"], 32)

            def att_out(g4):
                n, kv = g4 // 2, g4 % 2
                dve.wait_ge(sem["att_o"], g4 + 1)
                done(v.tensor_copy(OA[:, 2 * kv:2 * kv + 2, n * P:n * P + P],
                                   ps[:, 6, 0:2 * P].rearrange("p (a b) -> p a b", b=P)), "att_oe", g4 + 1)

            for g4 in range(4):
                n, kv = g4 // 2, g4 % 2
                J = P if n == 0 else 2 * P
                b0 = 2 * (g4 % 2)
                dve.wait_ge(sem["att_s"], g4 + 1)
                S = ps[:, b0:b0 + 2, 0:2 * J].rearrange("p s (j q) -> p s j q", q=J)
                heads = slice(4 * kv, 4 * kv + 4)
                if g4:
                    dve.wait_ge(sem["att_pt"], g4 if n == 0 else 2 * g4 - 2)
                chain(v.tensor_tensor(Pm[:, :, 0:J].rearrange("p (j s) q -> p s j q", s=2), S,
                                      BMv[:, heads, 2 * P - J:2 * P].rearrange("p (j s) q -> p s j q", s=2), ALU.add))
                chain(v.tensor_reduce(st[:, 0:4], Pm[:, :, 0:J], AX.X, ALU.max))
                chain(v.tensor_tensor(st[:, 0:4], st[:, 0:4], sinkb[:, heads], ALU.max))
                chain(v.tensor_scalar(st[:, 4:8], st[:, 0:4], -1.0, None, ALU.mult))
                done(v.tensor_tensor(st[:, 12:16], sinkb[:, heads], st[:, 4:8], ALU.add), "att_max", g4 + 1)
                if g4:
                    att_out(g4 - 1)
                dve.wait_ge(sem["att_exp"], 5 * g4 + 5)
                chain(v.tensor_tensor(st[:, 8:12], st[:, 8:12], st[:, 12:16], ALU.add))
                chain(v.reciprocal(st[:, 8:12], st[:, 8:12]))
                done(v.tensor_tensor(Pm[:, :, 0:J], Pm[:, :, 0:J], st[:, 8:12].unsqueeze(2).broadcast_to([P, 4, J]), ALU.mult),
                     "att_p", g4 + 1)
            att_out(3)
            dve.wait_ge(sem["smp_done"], 1)
            for b0 in range(0, NS, 3):
                nb = min(3, NS - b0)
                chain(v.tensor_tensor(SsT[0:HQ, b0:b0 + nb, :], ps[0:HQ, 4 + b0 // 3, 0:nb * KEYS].rearrange("p (a b) -> p a b", b=KEYS),
                                      brow[:, 0:KEYS].unsqueeze(1).broadcast_to([HQ, nb, KEYS]), ALU.add))
            mx, es, sm = st[0:HQ, 40:48], st[0:HQ, 48:56], st[0:HQ, 32:40]
            chain(v.tensor_reduce(mx, SsT[0:HQ, :, :], AX.X, ALU.max))
            chain(v.tensor_scalar(mx, mx, sinkc[:, 0:1], None, ALU.max))
            chain(v.tensor_scalar(es, mx, -1.0, sinkc[:, 0:1], ALU.mult, ALU.add))
            done(v.tensor_tensor(SsT[0:HQ, :, :], SsT[0:HQ, :, :], mx.unsqueeze(2).broadcast_to([HQ, NS, KEYS]), ALU.subtract), "smp_max", 1)
            dve.wait_ge(sem["smp_exp"], 2)
            chain(v.tensor_reduce(sm, SsT[0:HQ, :, :], AX.X, ALU.add))
            chain(v.tensor_tensor(sm, sm, es, ALU.add))
            chain(v.reciprocal(sm, sm))
            done(v.tensor_tensor(SsT[0:HQ, :, :], SsT[0:HQ, :, :], sm.unsqueeze(2).broadcast_to([HQ, NS, KEYS]), ALU.mult), "smp_p", 1)
            dve.wait_ge(sem["smp_done"], 2)
            chain(v.tensor_copy(pTs[:, :, :], ps[:, 7, 0:64].rearrange("p (a b) -> p a b", b=HQ)))
            done(v.tensor_tensor(PSf[:, :, :], ps[0:NS, 7, 64:72].unsqueeze(1).broadcast_to([NS, NS, HQ]),
                                 ID[0:NS, 0:NS].unsqueeze(2).broadcast_to([NS, NS, HQ]), ALU.mult), "smp_pte", 1)
            dve.wait_ge(sem["smp_done"], 3)
            done(v.tensor_copy(OS[:, :, :], ps[:, 4, 0:64].rearrange("p (a b) -> p a b", b=HQ)), "os_ready", 1)
            dve.wait_ge(sem["smp_done"], 4)
            for kv in range(HKV):
                for s in range(2):
                    src = ps[64 * s:64 * s + 64, 5 + kv, 0:32].rearrange("p (b j s) -> p s j b", j=2, s=2)[:, s]
                    ins = v.tensor_copy(OA[64 * s:64 * s + 64, 2 * kv:2 * kv + 2, NP:T], src)
                    if kv and s:
                        done(ins, "smp_oe", 1)
                    else:
                        chain(ins)

            dve.wait_ge(sem["bon_evac"], 4)
            chain(v.tensor_tensor(BON, BON, vv, ALU.mult))
            M2 = cst[:, K_M2:K_M2 + P].unsqueeze(1).broadcast_to([P, 8, P])
            for n in range(2):
                for q, (M, name) in enumerate(((NR, "nr_ready"), (KR, "kr_ready"))):
                    dve.wait_ge(sem["ab_done"], 2 * n + q + 1)
                    src = ps[:, 4 + 2 * q:6 + 2 * q, :].rearrange("p s (h c) -> p s h c", c=P)
                    done(v.tensor_tensor(M[:, 8 * n:8 * n + 8, :].rearrange("p (h s) c -> p s h c", s=2), src,
                                         M2.rearrange("p (h s) c -> p s h c", s=2), ALU.mult), name, n + 1)
            mask = cst[:, K_LV:K_LV + 64].unsqueeze(1).broadcast_to([P, 16, CH])
            done(v.tensor_tensor(NM[0], NR[:, :, 0:CH], mask, ALU.mult), "nm0_ready", 1)
            Ib = II[:, 0:CH].unsqueeze(1).broadcast_to([P, 8, CH])

            def bank(i):
                return ps[:, i, :].rearrange("p (a b) -> p a b", b=CH)

            dve.wait_ge(sem["row_evac"], 8)
            for n in range(2):
                hs = slice(8 * n, 8 * n + 8)
                chain(v.tensor_tensor(XX[:, hs, :], NM[0][:, hs, :], Ib, ALU.add))
                dve.wait_ge(sem["y_done"], n + 1)
                done(v.tensor_tensor(X[:, hs, :], bank(4 * n), Ib, ALU.add), "x_ready", n + 1)
            for i in range(1, len(LEVELS)):
                for n in range(2):
                    hs = slice(8 * n, 8 * n + 8)
                    dve.wait_ge(sem["dx_done"], 2 * (i - 1) + n + 1)
                    if i < len(LEVELS) - 1:
                        chain(v.tensor_tensor(X[:, hs, :], bank(4 * n + 1), X[:, hs, :], ALU.add))
                    done(v.tensor_tensor(XX[:, hs, :], bank(4 * n + 2), XX[:, hs, :], ALU.add), "x_ready", 2 * i + n + 1)

            def chunks(b):
                return ps[:, b, :].rearrange("p (h c k) -> p h c k", c=2, k=CH)

            dve.wait_ge(sem["carry_done"], 1)
            for q in range(2):
                R_ = ZR[:, :, q::2, 1, :]
                done(v.tensor_tensor(R_, chunks(q), R_, ALU.add), "dr_ready", q + 1)
            dve.wait_ge(sem["carry_done"], 2)
            for q in range(2):
                done(v.tensor_tensor(MC[:, :, q::2, :], chunks(4 + q), II[:, 0:CH].unsqueeze(1).broadcast_to([P, 8, CH]).rearrange(
                    "p (a b) c -> p a b c", b=2), ALU.add), "mc_ready", q + 1)
            dve.wait_ge(sem["n0_evac"], 2)
            for c in range(NCHUNK):
                G = G4[:, c, :, :]
                if c:
                    dve.wait_ge(sem["gm_done"], c)
                    chain(v.tensor_tensor(G, ps[:, 7, 0:4 * CH].rearrange("p (a b) -> p a b", b=CH), N0[:, :, c, :], ALU.add))
                src = G if c else N0[:, :, 0, :]
                done(v.tensor_tensor(G, src, pcol[:, :, c:c + 1].broadcast_to([P, 4, CH]), ALU.mult), "g_ready", c + 1)
            dve.wait_ge(sem["o_done"], NCHUNK)
            OTc = OT[:, :, 0:NP].rearrange("p h (c t) -> p h c t", t=CH)
            for q in range(2):
                chain(v.tensor_copy(OTc[:, :, q::2, :], chunks(4 + q)))
            for c in range(1, NCHUNK):
                src = ps[:, 6 if c < 3 else 3, (c - 1) % 2 * 256:(c - 1) % 2 * 256 + 256].rearrange("p (h k) -> p h k", k=CH)
                ins = v.tensor_tensor(OTc[:, :, c, :], src, OTc[:, :, c, :], ALU.add)
                if c == NCHUNK - 1:
                    done(ins, "ot_ready", 1)
                else:
                    chain(ins)
            dve.wait_ge(sem["ld_s0"], 16 * HQ)
            sa, so = st[:, 0:32], st[:, 32:64]
            for q in range(5):
                dve.wait_ge(sem["ex_used"], q + 1)
                B = ps[:, 4:8, :].rearrange("p a b -> p (a b)").rearrange("p (a b) -> p a b", b=CH)
                if q == 0:
                    chain(v.tensor_tensor(T1, B, S0, ALU.mult))
                    done(v.tensor_reduce(sa, T1, AX.X, ALU.add), "smp_step", 1)
                elif q == 1:
                    done(v.tensor_tensor(S0, B, S0, ALU.mult), "smp_step", 2)
                elif q in (2, 3):
                    w = sa if q == 2 else SMP[:, 5, :, :].rearrange("p a b -> p (a b)")
                    chain(v.tensor_tensor(T1, B, w.unsqueeze(2).broadcast_to([P, 32, CH]), ALU.mult))
                    done(v.tensor_tensor(S0, S0, T1, ALU.add), "smp_step", q + 1)
                else:
                    chain(v.tensor_tensor(T1, B, S0, ALU.mult))
                    chain(v.tensor_reduce(so, T1, AX.X, ALU.add))
                    done(v.tensor_copy(OT[:, :, NP:T], so.rearrange("p (a b) -> p a b", b=NS)), "smp_step", 5)
            dve.wait_ge(sem["gn_evac"], 4)
            chain(v.tensor_tensor(OT, OT, TMn, ALU.subtract))
            done(v.tensor_tensor(OSQ, OT, OT, ALU.mult), "gnsq_ready", 1)
            def attention_mixed(ks):
                for k in ks:
                    dve.wait_ge(sem["pab_done"], k + 1)
                    done(v.tensor_tensor(HT[:, k, :], ps[:, k % 4, 0:T], SGv[:, k, :], ALU.mult), "pab_evac", k + 1)

            attention_mixed(range(4))
            dve.wait_ge(sem["gn_evac"], 8)
            chain(v.reciprocal(TMn, TMn))
            chain(v.tensor_tensor(OT, OT, TMn, ALU.mult))
            for hp in range(4):
                chain(v.tensor_scalar(OT[:, hp, :], OT[:, hp, :], par("rw_gn_w", hp), par("rw_gn_b", hp), ALU.mult, ALU.add))
            chain(v.tensor_tensor(OT, OT, BON, ALU.add))
            done(v.tensor_tensor(OT, OT, GG, ALU.mult), "ob_ready", 1)
            attention_mixed(range(4, KD))
            for k in range(KD):
                dve.wait_ge(sem["pab_done"], KD + k + 1)
                done(v.tensor_tensor(SGv[:, 8 + k, :], ps[:, k % 4, 0:T], SGv[:, 8 + k, :], ALU.mult), "pab_evac", KD + k + 1)
                v.tensor_tensor(HT[:, k, :], HT[:, k, :], SGv[:, 8 + k, :], ALU.add).then_inc(sem["m_ready"], 1)
            out, bias = add_bias(16, 48)
            dve.wait_ge(sem["a_evac"], a_end("modT11"))
            chain(v.tensor_tensor(out, out, bias, ALU.add))

            for k in range(KD):
                dve.wait_ge(sem["wo_done"], k + 1)
                src = ps[:, 4 + k % 4, :]
                chain(v.tensor_tensor(A1[:, k, 0:NS], src[:, NP:T], modT[:, 16 + k, 1:9], ALU.mult))
                v.scalar_tensor_tensor(out=XT[:, k, 0:NP], in0=src[:, 0:NP], scalar=modT[:, 16 + k, 0:1],
                                       in1=XT[:, k, 0:NP], op0=ALU.mult, op1=ALU.add).then_inc(sem["x1_ready"], 1)
                done(v.tensor_tensor(XT[:, k, NP:T], XT[:, k, NP:T], A1[:, k, 0:NS], ALU.add), "x1_ready", 2 * k + 2)
            rms(2)
            modulate(24, 32, "norm2", "h2_ready")

            dve.wait_ge(sem["ld_r"], 48)
            chain(v.memset(POSM, -1.0))
            chain(v.memset(GATE, 0.0))
            v.memset(GT, 0.0).then_inc(sem["gt_zero"], 1)
            IE = cst[:, K_IE:K_IE + NE]
            dve.wait_ge(sem["st_w"], 32)
            dve.wait_ge(sem["lg_done"], 1)
            v.tensor_scalar(LGT[0:NE, :], ps[0:NE, 4, 0:T], brc[:, 0:1], None, ALU.add).then_inc(sem["lgt_ready"], 1)
            dve.wait_ge(sem["lg_done"], 2)

            def tiles(step):
                for n, (_, nt) in enumerate(TILES):
                    ins = step(n, nt)
                chain(ins)

            tiles(lambda n, nt: v.tensor_copy(LG[0:nt, n, :], ps[0:nt, 5, n * NE:n * NE + NE]))
            tiles(lambda n, nt: v.max(mx8[0:nt, n, :], LG[0:nt, n, :]))
            for n, (_, nt) in enumerate(TILES):
                v.tensor_scalar(st[0:nt, 70 + n:71 + n], mx8[0:nt, n, 0:1], -1.0, None, ALU.mult).then_inc(sem["top_ready"], 1)
            tiles(lambda n, nt: v.max_index(ix8[0:nt, n, :], mx8[0:nt, n, :], LG[0:nt, n, :]))
            tiles(lambda n, nt: v.tensor_copy(ixf[0:nt, n, :], ix8[0:nt, n, :]))
            tiles(lambda n, nt: v.tensor_scalar(MSK[0:nt, n, :], IE[0:nt, :], ixf[0:nt, n, 0:1], None, ALU.is_equal))
            for j in range(1, 4):
                tiles(lambda n, nt: v.scalar_tensor_tensor(out=MSK[0:nt, n, :], in0=IE[0:nt, :], scalar=ixf[0:nt, n, j:j + 1],
                                                           in1=MSK[0:nt, n, :], op0=ALU.is_equal, op1=ALU.add))
            dve.sem_inc(sem["msk_ready"], 1)
            dve.wait_ge(sem["top_exp"], 6)
            tiles(lambda n, nt: v.reciprocal(st[0:nt, 73 + n:74 + n], st[0:nt, 76 + n:77 + n]))
            tiles(lambda n, nt: v.scalar_tensor_tensor(out=GTE[0:nt, n, :], in0=RNK[0:nt, n, :], scalar=st[0:nt, 73 + n:74 + n],
                                                       in1=MSK[0:nt, n, :], op0=ALU.mult, op1=ALU.mult))
            dve.sem_inc(sem["gte_ready"], 1)
            for n, (_, nt) in enumerate(TILES):
                chain(v.tensor_copy(GATE[0:nt, n, 0:MAXR * NE].rearrange("p (r e) -> p r e", e=NE),
                                    GTE[0:nt, n, :].unsqueeze(1).broadcast_to([nt, MAXR, NE])))
            dve.wait_ge(sem["pos_done"], 1)
            for n, (_, nt) in enumerate(TILES):
                v.scalar_tensor_tensor(out=RNK[0:nt, n, :], in0=ps[0:nt, 5, n * NE:n * NE + NE], scalar=1.0, in1=MSK[0:nt, n, :],
                                       op0=ALU.add, op1=ALU.mult).then_inc(sem["rnk_ready"], 1)

            def ranks(q):
                for n, (_, nt) in enumerate(TILES):
                    ins = v.tensor_scalar(POSM[0:nt, n, q * NE:q * NE + NE], RNK[0:nt, n, :], -1.0 - q * C, None, ALU.add)
                chain(ins)

            dve.wait_ge(sem["rnk_ready"], 3)
            ranks(0)
            IO = cst[:, K_IO:K_IO + C]
            IO2 = cst[:, K_IO:K_IO + 2 * C]

            def slots(col):
                for n in range(3):
                    v.tensor_scalar(OH[:, n, :], IO, POSM[:, n, col], None, ALU.is_equal)
                for n, (_, nt) in enumerate(TILES):
                    last = v.tensor_scalar(OG[0:nt, n, :], IO2[0:nt, :], POSM[0:nt, n, col], GATE[0:nt, n, col], ALU.is_equal, ALU.mult)
                last.then_inc(sem["oh_ready"], 1)

            slots(slice(0, 1))
            for q in range(1, MAXR):
                ranks(q)
            chain(v.tensor_reduce(st[:, 80:81], ps[:, 5, 96:96 + NE], AX.X, ALU.max))
            chain(v.memset(st[:, 81:82], 1.0))
            for q in range(1, MAXR):
                chain(v.scalar_tensor_tensor(out=st[:, 81:82], in0=st[:, 80:81], scalar=float(q * C), in1=st[:, 81:82],
                                             op0=ALU.is_gt, op1=ALU.add))
            done(v.tensor_copy(rounds_i[:, :], st[:, 81:82]), "rounds_ready", 1)
            dve.sem_inc(sem["pos_evac"], 1)
            rounds = dve.value_load(rounds_i[0:1, 0:1], min_val=1, max_val=MAXR)
            links_before, LINKS = chain.count, 8
            with dve.Fori(0, rounds) as r_:
                with dve.Fori(0, NE) as e:
                    i = r_ * NE + e
                    chain.base, chain.count = i * LINKS + links_before, 0
                    dve.wait_ge(sem["gt_done"], i + 1)
                    slots(bass.ds(i + 1, 1))
                    for hh in range(2):
                        u = ps[:, 2 + hh, :].rearrange("p (f l c) -> p l f c", l=2, f=4)
                        dve.wait_ge(sem["ut_done"], 2 * i + hh + 1)
                        chain(v.tensor_tensor(UG, u[:, 0], b1T[:, bass.ds(e * 16 + 4 * hh, 4)].unsqueeze(2).broadcast_to([P, 4, C]), ALU.add))
                        v.tensor_scalar(UG, UG, 7.0, None, ALU.min).then_inc(sem["ug_ready"], 1)
                        chain(v.tensor_tensor(UL, u[:, 1], b1T[:, bass.ds(e * 16 + 8 + 4 * hh, 4)].unsqueeze(2).broadcast_to([P, 4, C]), ALU.add))
                        chain(v.tensor_scalar(UL, UL, 7.0, -7.0, ALU.min, ALU.max))
                        dve.wait_ge(sem["ug_ready"], 2 * i + hh + 1)
                        chain(v.scalar_tensor_tensor(out=UL, in0=UL, scalar=1.0, in1=UG, op0=ALU.add, op1=ALU.mult))
                        dve.wait_ge(sem["us_ready"], 2 * i + hh + 1)
                        v.tensor_tensor(AC[:, 4 * hh:4 * hh + 4, :], UL, US_, ALU.mult).then_inc(sem["ac_ready"], 1)
                        dve.wait_ge(sem["ac_ready"], 2 * i + hh + 1)
                    for k in range(KD):
                        dve.wait_ge(sem["comb_done"], 8 * i + 9 + k)
                        dve.wait_ge(sem["comb_used"], 8 * i + 1 + k)
                        v.tensor_tensor(YA[:, k, :], ps[:, 6 + k % 2, 0:T], YA[:, k, :], ALU.add).then_inc(sem["comb_used"], 1)
            dve.wait_ge(sem["comb_used"], rounds * (NE * KD) + KD)
            chain.base, chain.count = rounds * (NE * LINKS) + links_before, 0
            chain(v.tensor_tensor(YA[:, :, NP:T], YA[:, :, NP:T], modT[:, 40:48, 1:9], ALU.mult))
            chain(v.tensor_tensor(XT[:, :, NP:T], XT[:, :, NP:T], YA[:, :, NP:T], ALU.add))
            for k in range(KD):
                last = v.scalar_tensor_tensor(out=XT[:, k, 0:NP], in0=YA[:, k, 0:NP], scalar=modT[:, 40 + k, 0:1],
                                              in1=XT[:, k, 0:NP], op0=ALU.mult, op1=ALU.add)
                last.then_inc(sem["x2_ready"], 1)


def _io(nc, inputs):
    def a(name):
        return np.ascontiguousarray(inputs[name])

    lay = {"cst": constants()}
    lay["x_prompt"] = a("x_prompt").reshape(NP, D)
    lay["x_sample"] = a("x_sample").reshape(NS, D)
    lay["c_prompt"] = a("c_prompt").reshape(1, D)
    lay["c_sample"] = a("c_sample").reshape(NS, D)
    lay["cache_k"] = a("cache_k").reshape(NS, WINDOW, P)
    lay["cache_v"] = a("cache_v").reshape(NS, WINDOW, P)
    lay["state_shift"] = a("state_shift").reshape(NS, RW)
    lay["state_wkv"] = a("state_wkv").reshape(NS, 4, 2, 64, 64)
    lay["t5_table"] = a("t5_table")
    lay["sinks"] = a("sinks").reshape(1, HQ)
    lay["params"] = np.concatenate([a(name).reshape(rows, P) for name, rows in PARAMS[:-2]]
                                   + [np.tile(a(name).reshape(1, HD), (1, 2)) for name, _ in PARAMS[-2:]])
    for name in ("w_mod", "w_in", "w_pa", "w_pb", "w_o", "w_router", "rw_w_w2", "rw_w_a2", "rw_w_g2", "w1", "w2", "b2", "b_router"):
        x = a(name)
        lay[name] = x.reshape(x.shape[1:]) if name != "b_router" else x.reshape(1, NE)
    lay["b1"] = a("b1").reshape(NE * 16, P)
    return lay


OUTS = [("y_prompt", (NP, D), (1, NP, D)), ("y_sample", (NS, D), (NS, 1, D)),
        ("k_prompt", (WINDOW, P), (1, 1, WINDOW, HKV, HD)), ("v_prompt", (WINDOW, P), (1, 1, WINDOW, HKV, HD)),
        ("shift_prompt", (1, RW), (1, 1, RW)), ("wkv_prompt", (8, 64, 64), (1, 1, 8, 64, 64)),
        ("k_sample", (NS, WINDOW, P), (1, NS, WINDOW, HKV, HD)), ("v_sample", (NS, WINDOW, P), (1, NS, WINDOW, HKV, HD)),
        ("shift_sample", (NS, RW), (1, NS, RW)), ("wkv_sample", (NS, 4, 2, 64, 64), (1, NS, 8, 64, 64))]


def kernel(**inputs):
    import concourse.bacc as bacc
    from concourse.bass_utils import run_bass_kernel_spmd as run

    nc = bacc.Bacc("TRN2", target_bir_lowering=False, num_devices=1)
    io, arrays = {}, {}
    for name, x in _io(nc, inputs).items():
        arrays["in_" + name] = x
        io[name] = nc.dram_tensor("in_" + name, x.shape, mybir.dt.from_np(x.dtype), kind="ExternalInput").ap()
    for name, shape, _ in OUTS:
        io[name] = nc.dram_tensor("out_" + name, shape, F32, kind="ExternalOutput").ap()
    build(nc, io)
    r = run(nc, [arrays], core_ids=[0])
    return tuple(r.results[0]["out_" + name].reshape(shape) for name, _, shape in OUTS)
```
